# Optimizing a Trainium2 kernel written in Bass

```python
import jax, jax.numpy as jnp
from jax import lax
import numpy as np
import jax
import jax.numpy as jnp

D_MODEL = 1024
BATCH = 1
SEQ = 256
DEPTH = 2

CTX_LEN = 256
GRID_W = 64
EPS = 1e-6
ADA_CHUNKS = 9
D_FF = 2816
FFN_RESIDUAL_WEIGHT = 0.5
D_MIX = D_MODEL
MLA_HEADS = 8
NOPE_DIM = 64
ROPE_DIM = 32
AXIS_DIM = ROPE_DIM // 2
QK_HEAD_DIM = NOPE_DIM + ROPE_DIM
V_HEAD_DIM = 64
Q_LORA = 384
KV_LORA = 256
ATT_WIDTH = MLA_HEADS * V_HEAD_DIM
ROPE_BASE = 10000.0
Q_BLOCK = 128
SG_GROUPS = 4
SG_GROUP_DIM = 64
SG_WIDTH = SG_GROUPS * SG_GROUP_DIM
CHUNK = 128
CONV_WIDTH = 256
CONV_K = 3
OFF_KV = Q_LORA
OFF_KPE = OFF_KV + KV_LORA
OFF_SG = OFF_KPE + ROPE_DIM
OFF_CONV = OFF_SG + 2 * SG_WIDTH
MIX_IN_DIM = OFF_CONV + 3 * CONV_WIDTH


def rms_norm(x, g):
    xf = x.astype(jnp.float32)
    y = xf * lax.rsqrt(jnp.mean(xf * xf, axis=-1, keepdims=True) + EPS)
    return (y * g.astype(jnp.float32)).astype(x.dtype)

def modulate(h, shift, scale):
    return h * (1 + scale) + shift

def ffn_half_step(h, shift, scale, gate, g, w_in, w_out):
    a, b = jnp.split(modulate(rms_norm(h, g), shift, scale) @ w_in, 2, axis=-1)
    return h + FFN_RESIDUAL_WEIGHT * gate * ((jax.nn.silu(a) * b) @ w_out)

def axial_rope_tables(n, dtype):
    rows = n // GRID_W
    row = jnp.repeat(jnp.arange(rows), GRID_W).astype(jnp.float32)
    col = jnp.tile(jnp.arange(GRID_W), rows).astype(jnp.float32)
    inv = 1.0 / (ROPE_BASE ** (jnp.arange(0, AXIS_DIM, 2, dtype=jnp.float32) / AXIS_DIM))
    ang_r = row[:, None] * inv
    ang_c = col[:, None] * inv
    ang = jnp.concatenate([ang_r, ang_r, ang_c, ang_c], axis=-1)
    return jnp.cos(ang).astype(dtype), jnp.sin(ang).astype(dtype)

def rotate_half(t):
    a, b = jnp.split(t, 2, axis=-1)
    return jnp.concatenate([-b, a], axis=-1)

def apply_rope(x, rope):
    cos, sin = rope
    x_nope, x_pe = x[..., :NOPE_DIM], x[..., NOPE_DIM:]
    xr, xc = jnp.split(x_pe, 2, axis=-1)
    rot = jnp.concatenate([rotate_half(xr), rotate_half(xc)], axis=-1)
    x_pe = x_pe * cos[None, :, None, :] + rot * sin[None, :, None, :]
    return jnp.concatenate([x_nope, x_pe], axis=-1)

def mla_queries(q_lat, g_q_lat, w_q_up, g_q_head, rope):
    b, n, _ = q_lat.shape
    q = (rms_norm(q_lat, g_q_lat) @ w_q_up).reshape(b, n, MLA_HEADS, QK_HEAD_DIM)
    q = rms_norm(q, g_q_head)
    return apply_rope(q, rope) if rope is not None else q

def mla_keys_values(kv_lat, k_pe, g_kv_lat, w_kv_up, g_k_head, rope):
    b, n, _ = kv_lat.shape
    kv = (rms_norm(kv_lat, g_kv_lat) @ w_kv_up).reshape(b, n, MLA_HEADS, NOPE_DIM + V_HEAD_DIM)
    k_nope, v = kv[..., :NOPE_DIM], kv[..., NOPE_DIM:]
    k_pe = jnp.broadcast_to(k_pe[:, :, None, :], (b, n, MLA_HEADS, ROPE_DIM))
    k = rms_norm(jnp.concatenate([k_nope, k_pe], axis=-1), g_k_head)
    k = apply_rope(k, rope) if rope is not None else k
    return k, v

def softmax_attend(q, k, v):
    s = jnp.einsum('bqhd,bkhd->bhqk', q, k, preferred_element_type=jnp.float32) * (QK_HEAD_DIM ** -0.5)
    p = jax.nn.softmax(s, axis=-1).astype(v.dtype)
    return jnp.einsum('bhqk,bkhd->bqhd', p, v)

def latent_attention(q, k_lat, v_lat, k_ctx, v_ctx):
    b, n, h, dq = q.shape
    k_all = jnp.concatenate([k_lat, k_ctx], axis=1)
    v_all = jnp.concatenate([v_lat, v_ctx], axis=1)
    qb = q.reshape(b, n // Q_BLOCK, Q_BLOCK, h, dq).transpose(1, 0, 2, 3, 4)
    o = lax.map(lambda qblk: softmax_attend(qblk, k_all, v_all), qb)
    return o.transpose(1, 0, 2, 3, 4).reshape(b, n, h * V_HEAD_DIM)

def spatial_gating(sg_in, g_sgu, w_spatial, b_spatial):
    b, n, _ = sg_in.shape
    u, v = jnp.split(jax.nn.gelu(sg_in), 2, axis=-1)
    v = rms_norm(v.reshape(b, n, SG_GROUPS, SG_GROUP_DIM), g_sgu)
    v = v.reshape(b, n // CHUNK, CHUNK, SG_GROUPS, SG_GROUP_DIM)
    vs = jnp.einsum('gpq,bnqgc->bnpgc', w_spatial, v) + b_spatial.T[:, :, None]
    return u * vs.reshape(b, n, SG_WIDTH)

def short_conv(cv_in, w_conv):
    b_gate, c_gate, xin = jnp.split(cv_in, 3, axis=-1)
    z = c_gate * xin
    y = lax.conv_general_dilated(z, w_conv[:, None, :], window_strides=(1,), padding=[(1, 1)],
                                 dimension_numbers=('NWC', 'WIO', 'NWC'), feature_group_count=CONV_WIDTH)
    return b_gate * y

def merge_groups(attn, sg, cv, g_out, w_mix_out):
    y = jnp.concatenate([rms_norm(attn, g_out[:ATT_WIDTH]),
                         rms_norm(sg, g_out[ATT_WIDTH:ATT_WIDTH + SG_WIDTH]),
                         rms_norm(cv, g_out[ATT_WIDTH + SG_WIDTH:])], axis=-1)
    return y @ w_mix_out

def first_inputs(seed: int = 0) -> dict:
    key = jax.random.key(seed)
    ks = iter(jax.random.split(key, 40))

    def nrm(shape, scale):
        return jax.random.normal(next(ks), shape, jnp.float32) * scale

    def gain(shape):
        return 1.0 + nrm(shape, 0.02)

    L, D = DEPTH, D_MODEL
    return {
        'x': nrm((BATCH, SEQ, D), 1.0),
        'c': nrm((BATCH, D), 1.0),
        'ctx': nrm((BATCH, CTX_LEN, D), 1.0),
        'c_ctx': nrm((D,), 1.0),
        'w_ada': nrm((L, D, ADA_CHUNKS * D), 0.5 * D ** -0.5),
        'b_ada': nrm((L, ADA_CHUNKS * D), 0.02),
        'g_ffn1': gain((L, D)),
        'w_ffn1_in': nrm((L, D, 2 * D_FF), D ** -0.5),
        'w_ffn1_out': nrm((L, D_FF, D), D_FF ** -0.5),
        'g_mix': gain((L, D)),
        'w_mix_in': nrm((L, D, MIX_IN_DIM), D ** -0.5),
        'g_q_lat': gain((L, Q_LORA)),
        'w_q_up': nrm((L, Q_LORA, MLA_HEADS * QK_HEAD_DIM), Q_LORA ** -0.5),
        'g_kv_lat': gain((L, KV_LORA)),
        'w_kv_up': nrm((L, KV_LORA, MLA_HEADS * (NOPE_DIM + V_HEAD_DIM)), KV_LORA ** -0.5),
        'g_q_head': gain((L, QK_HEAD_DIM)),
        'g_k_head': gain((L, QK_HEAD_DIM)),
        'g_sgu': gain((L, SG_GROUPS, SG_GROUP_DIM)),
        'w_spatial': nrm((L, SG_GROUPS, CHUNK, CHUNK), CHUNK ** -0.5),
        'b_spatial': 1.0 + nrm((L, SG_GROUPS, CHUNK), 0.02),
        'w_conv': nrm((L, CONV_K, CONV_WIDTH), CONV_K ** -0.5),
        'g_out': gain((L, D_MIX)),
        'w_mix_out': nrm((L, D_MIX, D), D_MIX ** -0.5),
        'g_ffn2': gain((L, D)),
        'w_ffn2_in': nrm((L, D, 2 * D_FF), D ** -0.5),
        'w_ffn2_out': nrm((L, D_FF, D), D_FF ** -0.5),
    }

def first_block(x, c, ctx, c_ctx, w_ada, b_ada, g_ffn1, w_ffn1_in, w_ffn1_out, g_mix, w_mix_in,
              g_q_lat, w_q_up, g_kv_lat, w_kv_up, g_q_head, g_k_head, g_sgu, w_spatial, b_spatial,
              w_conv, g_out, w_mix_out, g_ffn2, w_ffn2_in, w_ffn2_out):
    rope = axial_rope_tables(x.shape[1], x.dtype)
    h, hc = x, ctx
    sc, scc = jax.nn.silu(c), jax.nn.silu(c_ctx)
    splits = [OFF_KV, OFF_KPE, OFF_SG, OFF_CONV]
    for l in range(DEPTH):
        last = l == DEPTH - 1
        mod_l = jnp.split((sc @ w_ada[l] + b_ada[l])[:, None, :], ADA_CHUNKS, axis=-1)
        mod_c = jnp.split((scc @ w_ada[l] + b_ada[l])[None, None, :], ADA_CHUNKS, axis=-1)

        h = ffn_half_step(h, mod_l[0], mod_l[1], mod_l[2], g_ffn1[l], w_ffn1_in[l], w_ffn1_out[l])
        hc = ffn_half_step(hc, mod_c[0], mod_c[1], mod_c[2], g_ffn1[l], w_ffn1_in[l], w_ffn1_out[l])

        hn = modulate(rms_norm(h, g_mix[l]), mod_l[3], mod_l[4])
        hnc = modulate(rms_norm(hc, g_mix[l]), mod_c[3], mod_c[4])
        q_lat, kv_lat, k_pe, sg_in, cv_in = jnp.split(hn @ w_mix_in[l], splits, axis=-1)
        if last:
            kv_lat_c, k_pe_c = jnp.split(hnc @ w_mix_in[l][:, OFF_KV:OFF_SG], [KV_LORA], axis=-1)
        else:
            q_lat_c, kv_lat_c, k_pe_c, sg_in_c, cv_in_c = jnp.split(hnc @ w_mix_in[l], splits, axis=-1)
        q = mla_queries(q_lat, g_q_lat[l], w_q_up[l], g_q_head[l], rope)
        k, v = mla_keys_values(kv_lat, k_pe, g_kv_lat[l], w_kv_up[l], g_k_head[l], rope)
        kc, vc = mla_keys_values(kv_lat_c, k_pe_c, g_kv_lat[l], w_kv_up[l], g_k_head[l], None)
        attn = latent_attention(q, k, v, kc, vc)
        sg = spatial_gating(sg_in, g_sgu[l], w_spatial[l], b_spatial[l])
        cv = short_conv(cv_in, w_conv[l])
        h = h + mod_l[5] * merge_groups(attn, sg, cv, g_out[l], w_mix_out[l])

        h = ffn_half_step(h, mod_l[6], mod_l[7], mod_l[8], g_ffn2[l], w_ffn2_in[l], w_ffn2_out[l])

        if not last:
            qc = mla_queries(q_lat_c, g_q_lat[l], w_q_up[l], g_q_head[l], None)
            b_sz = hc.shape[0]
            attn_c = softmax_attend(qc, kc, vc).reshape(b_sz, hc.shape[1], ATT_WIDTH)
            sg_c = spatial_gating(sg_in_c, g_sgu[l], w_spatial[l], b_spatial[l])
            cv_c = short_conv(cv_in_c, w_conv[l])
            hc = hc + mod_c[5] * merge_groups(attn_c, sg_c, cv_c, g_out[l], w_mix_out[l])
            hc = ffn_half_step(hc, mod_c[6], mod_c[7], mod_c[8], g_ffn2[l], w_ffn2_in[l], w_ffn2_out[l])
    return h


HEAD_DIM = 64
D_MIX_2 = D_MODEL
D_MLSTM = D_MIX_2 // 2
D_NA = D_MIX_2 - D_MLSTM
H_MLSTM = D_MLSTM // HEAD_DIM
H_NA = D_NA // HEAD_DIM
N_GATE = 4 * H_MLSTM
D_IN = 4 * D_MLSTM + 3 * D_NA + N_GATE
MLSTM_CHUNK = 64
NA_ROWS_MAX = 8
NA_COLS = 16
D_FF_2 = 4 * D_MODEL
N_MOD = 6
F_BIAS_LO = 3.0
F_BIAS_HI = 6.0


def rmsnorm(x, g):
    x32 = x.astype(jnp.float32)
    y = x32 * lax.rsqrt(jnp.mean(x32 * x32, axis=-1, keepdims=True) + EPS)
    return (y * g.astype(jnp.float32)).astype(x.dtype)

def sq_relu_mlp(h, w1, w2):
    return jnp.square(jax.nn.relu(h @ w1)) @ w2

def split_heads(a, n_heads):
    b, t, _ = a.shape
    return a.reshape(b, t, n_heads, HEAD_DIM).transpose(0, 2, 1, 3)

def merge_heads(a):
    b, h, t, d = a.shape
    return a.transpose(0, 2, 1, 3).reshape(b, t, h * d)

def head_layernorm(h, g):
    mu = jnp.mean(h, axis=-1, keepdims=True)
    var = jnp.mean(jnp.square(h - mu), axis=-1, keepdims=True)
    return merge_heads((h - mu) * lax.rsqrt(var + EPS)) * g.astype(jnp.float32)

def axial_rope_tables_2(n_tokens):
    t = jnp.arange(n_tokens)
    row = (t // GRID_W).astype(jnp.float32)
    col = (t % GRID_W).astype(jnp.float32)
    n_freq = HEAD_DIM // 4
    inv_freq = ROPE_BASE ** (-jnp.arange(n_freq, dtype=jnp.float32) / n_freq)
    ang = jnp.concatenate([row[:, None] * inv_freq, col[:, None] * inv_freq], axis=-1)
    return jnp.cos(ang), jnp.sin(ang)

def apply_rope_2(x, cos, sin):
    x1, x2 = jnp.split(x, 2, axis=-1)
    return jnp.concatenate([x1 * cos - x2 * sin, x1 * sin + x2 * cos], axis=-1)

def mlstm_scan(q, k, v, log_i, log_f, state):
    B, H, T, d = q.shape
    L = MLSTM_CHUNK
    nc = T // L

    def chunks(a):
        return jnp.moveaxis(a.reshape(a.shape[:2] + (nc, L) + a.shape[3:]), 2, 0)

    causal = jnp.tril(jnp.ones((L, L), dtype=bool))

    def step(carry, xs):
        C, n, m = carry
        qc, kc, vc, ic, fc = xs
        b = jnp.cumsum(fc, axis=-1)
        d_intra = jnp.where(causal, b[..., :, None] - b[..., None, :] + ic[..., None, :], -jnp.inf)
        d_prev = b + m[..., None]
        m_t = jnp.maximum(d_prev, jnp.max(d_intra, axis=-1))
        w_intra = jnp.exp(d_intra - m_t[..., None])
        w_prev = jnp.exp(d_prev - m_t)
        s = jnp.einsum('bhtd,bhsd->bhts', qc, kc) * w_intra
        num = w_prev[..., None] * jnp.einsum('bhtd,bhde->bhte', qc, C) + jnp.einsum('bhts,bhse->bhte', s, vc)
        qn = w_prev * jnp.einsum('bhtd,bhd->bht', qc, n) + jnp.sum(s, axis=-1)
        h = num / jnp.maximum(jnp.abs(qn), jnp.exp(-m_t))[..., None]
        b_end = b[..., -1]
        d_end = b_end[..., None] - b + ic
        m_new = jnp.maximum(b_end + m, jnp.max(d_end, axis=-1))
        w_c = jnp.exp(b_end + m - m_new)
        w_s = jnp.exp(d_end - m_new[..., None])
        C = w_c[..., None, None] * C + jnp.einsum('bhs,bhsd,bhse->bhde', w_s, kc, vc)
        n = w_c[..., None] * n + jnp.einsum('bhs,bhsd->bhd', w_s, kc)
        return (C, n, m_new), h

    state, h = lax.scan(step, state, (chunks(q), chunks(k), chunks(v), chunks(log_i), chunks(log_f)))
    return jnp.moveaxis(h, 0, 2).reshape(B, H, T, d), state

def mlstm_group(q, k, v, o, gates, qc, kc, vc, oc, gates_c, b_gate, norm_g, cos, sin, need_ctx):
    f32 = jnp.float32
    scale = HEAD_DIM ** -0.5

    def prep(a):
        return split_heads(a, H_MLSTM).astype(f32)

    qx = apply_rope_2(prep(q), cos, sin) * scale
    kx = apply_rope_2(prep(k), cos, sin)
    vx = prep(v)
    qcx = prep(qc) * scale
    kcx = prep(kc)
    vcx = prep(vc)

    def gate_split(g):
        return jnp.split((g.astype(f32) + b_gate.astype(f32)).transpose(0, 2, 1), 4, axis=1)

    i_fw, i_bw, f_fw, f_bw = gate_split(gates)
    ic_fw, ic_bw, fc_fw, fc_bw = gate_split(gates_c)
    B, H, _, d = qx.shape
    state0 = (jnp.zeros((B, H, d, d), f32), jnp.zeros((B, H, d), f32), jnp.zeros((B, H), f32))

    def direction(rev, ig, fg, igc, fgc):
        flip = (lambda a: jnp.flip(a, axis=2)) if rev else (lambda a: a)
        hc, st = mlstm_scan(flip(qcx), flip(kcx), flip(vcx), flip(igc), jax.nn.log_sigmoid(flip(fgc)), state0)
        hx, _ = mlstm_scan(flip(qx), flip(kx), flip(vx), flip(ig), jax.nn.log_sigmoid(flip(fg)), st)
        return flip(hx), flip(hc)

    hx_f, hc_f = direction(False, i_fw, f_fw, ic_fw, fc_fw)
    hx_b, hc_b = direction(True, i_bw, f_bw, ic_bw, fc_bw)
    y = (head_layernorm(hx_f + hx_b, norm_g) * jax.nn.sigmoid(o.astype(f32))).astype(q.dtype)
    yc = None
    if need_ctx:
        yc = (head_layernorm(hc_f + hc_b, norm_g) * jax.nn.sigmoid(oc.astype(f32))).astype(q.dtype)
    return y, yc

def neighborhood_attention(q, k, v, qc, kc, vc, rpb, rows, need_ctx):
    B, S, _ = q.shape
    scale = HEAD_DIM ** -0.5
    kr_n = min(NA_ROWS_MAX, rows)

    def grid(a):
        return split_heads(a, H_NA).reshape(B, H_NA, rows, GRID_W, HEAD_DIM)

    qg = grid(q * scale)
    kg = grid(k)
    vg = grid(v)
    kch = split_heads(kc, H_NA)
    vch = split_heads(vc, H_NA)
    cols = jnp.arange(GRID_W)
    col_start = jnp.clip(cols - NA_COLS // 2, 0, GRID_W - NA_COLS)
    col_mask = (cols[None, :] >= col_start[:, None]) & (cols[None, :] < col_start[:, None] + NA_COLS)
    dc_idx = jnp.clip(cols[None, :] - cols[:, None] + NA_COLS - 1, 0, 2 * NA_COLS - 2)
    rpb_cols = rpb.astype(jnp.float32)[:, :, dc_idx]

    def row_block(r):
        rs = jnp.clip(r - kr_n // 2, 0, rows - kr_n)
        q_r = lax.dynamic_index_in_dim(qg, r, axis=2, keepdims=False)
        k_r = lax.dynamic_slice_in_dim(kg, rs, kr_n, axis=2)
        v_r = lax.dynamic_slice_in_dim(vg, rs, kr_n, axis=2)
        bias = jnp.take(rpb_cols, rs + jnp.arange(kr_n) - r + NA_ROWS_MAX - 1, axis=1)
        s_loc = jnp.einsum('bhqd,bhrkd->bhqrk', q_r, k_r).astype(jnp.float32) + bias.transpose(0, 2, 1, 3)
        s_loc = jnp.where(col_mask[:, None, :], s_loc, -jnp.inf)
        s_ctx = jnp.einsum('bhqd,bhcd->bhqc', q_r, kch).astype(jnp.float32)
        s = jnp.concatenate([s_loc.reshape(B, H_NA, GRID_W, kr_n * GRID_W), s_ctx], axis=-1)
        p = jax.nn.softmax(s, axis=-1).astype(v.dtype)
        p_loc = p[..., :kr_n * GRID_W].reshape(B, H_NA, GRID_W, kr_n, GRID_W)
        p_ctx = p[..., kr_n * GRID_W:]
        return jnp.einsum('bhqrk,bhrkd->bhqd', p_loc, v_r) + jnp.einsum('bhqc,bhcd->bhqd', p_ctx, vch)

    out = lax.map(row_block, jnp.arange(rows))
    y = out.transpose(1, 0, 3, 2, 4).reshape(B, S, H_NA * HEAD_DIM)
    yc = None
    if need_ctx:
        qch = split_heads(qc * scale, H_NA)
        sc = jnp.einsum('bhqd,bhkd->bhqk', qch, kch).astype(jnp.float32)
        pc = jax.nn.softmax(sc, axis=-1).astype(vc.dtype)
        yc = merge_heads(jnp.einsum('bhqk,bhkd->bhqd', pc, vch))
    return y, yc

def token_mixers(p, pc, b_gate, norm_g, rpb, cos, sin, rows, need_ctx):
    cuts = [int(i) for i in np.cumsum([D_MLSTM] * 4 + [D_NA] * 3)]
    qm, km, vm, om, qn, kn, vn, gm = jnp.split(p, cuts, axis=-1)
    qmc, kmc, vmc, omc, qnc, knc, vnc, gmc = jnp.split(pc, cuts, axis=-1)
    y_m, yc_m = mlstm_group(qm, km, vm, om, gm, qmc, kmc, vmc, omc, gmc, b_gate, norm_g, cos, sin, need_ctx)
    y_n, yc_n = neighborhood_attention(qn, kn, vn, qnc, knc, vnc, rpb, rows, need_ctx)
    y = jnp.concatenate([y_m, y_n], axis=-1)
    yc = jnp.concatenate([yc_m, yc_n], axis=-1) if need_ctx else None
    return y, yc

def second_inputs(seed: int = 0) -> dict:
    key = jax.random.key(seed)
    ks = jax.random.split(key, 16)
    nrm = jax.random.normal
    f32 = jnp.float32
    x = nrm(ks[0], (BATCH, SEQ, D_MODEL), f32)
    c = nrm(ks[1], (BATCH, D_MODEL), f32)
    ctx = nrm(ks[2], (BATCH, CTX_LEN, D_MODEL), f32)
    c_ctx = nrm(ks[3], (D_MODEL,), f32)
    w_ada = nrm(ks[4], (DEPTH, D_MODEL, N_MOD * D_MODEL), f32) * (0.5 * D_MODEL ** -0.5)
    b_ada = 0.02 * nrm(ks[5], (DEPTH, N_MOD * D_MODEL), f32)
    norm1_g = 1.0 + 0.02 * nrm(ks[6], (DEPTH, D_MODEL), f32)
    w_in = nrm(ks[7], (DEPTH, D_MODEL, D_IN), f32) * D_MODEL ** -0.5
    i_bias = 0.1 * nrm(ks[8], (DEPTH, 2 * H_MLSTM), f32)
    f_base = jnp.tile(jnp.linspace(F_BIAS_LO, F_BIAS_HI, H_MLSTM, dtype=f32), 2)
    f_bias = f_base[None, :] + 0.1 * nrm(ks[9], (DEPTH, 2 * H_MLSTM), f32)
    b_gate = jnp.concatenate([i_bias, f_bias], axis=-1)
    mlstm_norm_g = 1.0 + 0.02 * nrm(ks[10], (DEPTH, D_MLSTM), f32)
    rpb = 0.1 * nrm(ks[11], (DEPTH, H_NA, 2 * NA_ROWS_MAX - 1, 2 * NA_COLS - 1), f32)
    w_out = nrm(ks[12], (DEPTH, D_MIX_2, D_MODEL), f32) * D_MIX_2 ** -0.5
    norm2_g = 1.0 + 0.02 * nrm(ks[13], (DEPTH, D_MODEL), f32)
    km1, km2 = jax.random.split(ks[14])
    w_mlp1 = nrm(km1, (DEPTH, D_MODEL, D_FF_2), f32) * D_MODEL ** -0.5
    w_mlp2 = nrm(km2, (DEPTH, D_FF_2, D_MODEL), f32) * D_FF_2 ** -0.5
    final_g = 1.0 + 0.02 * nrm(ks[15], (D_MODEL,), f32)
    return {"x": x, "c": c, "ctx": ctx, "c_ctx": c_ctx, "w_ada": w_ada, "b_ada": b_ada,
            "norm1_g": norm1_g, "w_in": w_in, "b_gate": b_gate, "mlstm_norm_g": mlstm_norm_g,
            "rpb": rpb, "w_out": w_out, "norm2_g": norm2_g, "w_mlp1": w_mlp1, "w_mlp2": w_mlp2,
            "final_g": final_g}

def second_block(x, c, ctx, c_ctx, w_ada, b_ada, norm1_g, w_in, b_gate, mlstm_norm_g, rpb, w_out,
              norm2_g, w_mlp1, w_mlp2, final_g):
    B, S, D = x.shape
    rows = S // GRID_W
    cos, sin = axial_rope_tables_2(S)
    silu_c = jax.nn.silu(c)
    silu_cc = jax.nn.silu(c_ctx)
    xc = ctx
    for l in range(DEPTH):
        need_ctx = l < DEPTH - 1
        mod = silu_c @ w_ada[l] + b_ada[l]
        mod_c = silu_cc @ w_ada[l] + b_ada[l]
        sh1, sc1, g1, sh2, sc2, g2 = jnp.split(mod[:, None, :], N_MOD, axis=-1)
        sh1c, sc1c, g1c, sh2c, sc2c, g2c = jnp.split(mod_c, N_MOD, axis=-1)
        h = rmsnorm(x, norm1_g[l]) * (1.0 + sc1) + sh1
        hc = rmsnorm(xc, norm1_g[l]) * (1.0 + sc1c) + sh1c
        y, yc = token_mixers(h @ w_in[l], hc @ w_in[l], b_gate[l], mlstm_norm_g[l], rpb[l],
                             cos, sin, rows, need_ctx)
        x = x + g1 * (y @ w_out[l])
        h = rmsnorm(x, norm2_g[l]) * (1.0 + sc2) + sh2
        x = x + g2 * sq_relu_mlp(h, w_mlp1[l], w_mlp2[l])
        if need_ctx:
            xc = xc + g1c * (yc @ w_out[l])
            hc = rmsnorm(xc, norm2_g[l]) * (1.0 + sc2c) + sh2c
            xc = xc + g2c * sq_relu_mlp(hc, w_mlp1[l], w_mlp2[l])
    return rmsnorm(x, final_g)


def setup_inputs(seed=0):
    out = dict(first_inputs(seed))
    for name, value in second_inputs(seed + 1).items():
        if name != "x":
            out[name + "_2"] = value
    return out


def reference(
    x, c, ctx, c_ctx, w_ada, b_ada, g_ffn1, w_ffn1_in, w_ffn1_out, g_mix, w_mix_in, g_q_lat,
    w_q_up, g_kv_lat, w_kv_up, g_q_head, g_k_head, g_sgu, w_spatial, b_spatial, w_conv, g_out,
    w_mix_out, g_ffn2, w_ffn2_in, w_ffn2_out, c_2, ctx_2, c_ctx_2, w_ada_2, b_ada_2, norm1_g_2,
    w_in_2, b_gate_2, mlstm_norm_g_2, rpb_2, w_out_2, norm2_g_2, w_mlp1_2, w_mlp2_2, final_g_2,
):
    x = first_block(
        x, c, ctx, c_ctx, w_ada, b_ada, g_ffn1, w_ffn1_in, w_ffn1_out, g_mix, w_mix_in, g_q_lat,
        w_q_up, g_kv_lat, w_kv_up, g_q_head, g_k_head, g_sgu, w_spatial, b_spatial, w_conv,
        g_out, w_mix_out, g_ffn2, w_ffn2_in, w_ffn2_out,
    )
    return second_block(
        x, c_2, ctx_2, c_ctx_2, w_ada_2, b_ada_2, norm1_g_2, w_in_2, b_gate_2, mlstm_norm_g_2,
        rpb_2, w_out_2, norm2_g_2, w_mlp1_2, w_mlp2_2, final_g_2,
    )


_drawn_inputs = setup_inputs


def setup_inputs(seed=0):
    import zlib

    import numpy as np

    out = dict(_drawn_inputs(seed))
    spreads = {}
    factors = {'g_ffn1': 8.0,
     'g_mix': 5.236,
     'g_q_lat': 8.0,
     'g_kv_lat': 6.754,
     'g_q_head': 8.0,
     'g_k_head': 8.0,
     'g_sgu': 55.233,
     'b_spatial': 50.897,
     'g_out': 5.562,
     'g_ffn2': 8.0,
     'norm1_g_2': 6.916,
     'mlstm_norm_g_2': 64.0,
     'rpb_2': 50.088,
     'norm2_g_2': 4.84,
     'final_g_2': 8.116}
    for name, (base, spread) in spreads.items():
        noise = np.random.default_rng([zlib.crc32(name.encode()), seed]).standard_normal(out[name].shape)
        drawn = base * np.exp(spread * noise) if base else spread * noise
        out[name] = jnp.asarray(drawn.astype(out[name].dtype))
    for name, factor in factors.items():
        out[name] = (out[name] * factor).astype(out[name].dtype)
    return out
```

```python
from collections import namedtuple
from contextlib import ExitStack

import numpy as np

import concourse.bass as bass
from concourse import mybir

P = 128
D = 1024
DC = D // P
LAT, CTX = 256, 256
TOK = LAT + CTX
HALVES = ((0, LAT, 0), (LAT, TOK, 1))
EPS = 1e-6
GRID_W = 64

D_FF = 2816
PAIRS = D_FF // P
Q_LORA, KV_LORA, ROPE = 384, 256, 32
NOPE, QK, VD = 64, 96, 64
HEADS = 8
SG = 256
CONV = 256
QC, KC = Q_LORA // P, KV_LORA // P
ADA1, ADA2 = 9, 6

D_MLP = 4 * D
MC = D_MLP // P
HD = 64
HP = 4

CREDIT = 1
RING = 8
UNIT = 1024
HW = QC * P + KC * P + KC * VD
NEG = -1.0e30

U_ADA1, U_ADA2 = ADA1 * DC, ADA2 * DC
U_SWIGLU, U_DOWN = 2 * PAIRS, PAIRS
MIX_FM = QC + KC + 1 + 6 + 2
U_MIX = MIX_FM + 2
U_OUT = DC

F32 = mybir.dt.float32
ACT = mybir.ActivationFunctionType
ALU = mybir.AluOpType
AXX = mybir.AxisListType.X

def param_columns():
    at, off = {}, 0
    def put(key, width):
        nonlocal off
        at[key] = (off, width)
        off += width
    for l in range(2):
        for name, width in (("g_ffn1", 16), ("g_mix", 16), ("g_ffn2", 16), ("g_q_lat", QC), ("g_kv_lat", KC),
                            ("g_q_head", 1), ("g_k_head", 1), ("g_sgu", 2), ("g_out", DC), ("w_conv", 6),
                            ("b_ada", ADA1 * 16)):
            put((name, l), width)
    for l in range(2, 4):
        for name, width in (("norm1_g", 16), ("norm2_g", 16), ("norm_g", HP), ("b_gate", 2), ("b_ada", ADA2 * 16)):
            put((name, l), width)
    put("final_g", DC)
    put("cond1", 16)
    put("cond2", 16)
    return at, off


COLS, N_COLS = param_columns()
CONSTS = {}
_off = 0
for _name, _w in (("ident", P), ("ones", P), ("rot1", P), ("cos1", LAT), ("sin1", LAT),
                  ("rot2", P), ("cos2", LAT), ("sin2", LAT)):
    CONSTS[_name] = (_off, _w)
    _off += _w
N_CONSTS = _off


COUNTED = ("unit", "acc", "evac", "silu", "glu", "out", "h", "sq", "sum", "std", "rstd", "scaled", "nout", "ada",
           "derived", "sg", "head", "headtile", "merge", "gates", "pair", "pairtile")
Counts = namedtuple("Counts", COUNTED)
Phase = namedtuple("Phase", ("kind", "at", "layer", "what", "tokens", "tiles", "blocks", "chunks", "pieces",
                             "shifted", "which", "n", "src", "glu_end"), defaults=(None,) * 12)


class NormSpec:
    pass


def make_plan():
    count = dict.fromkeys(COUNTED, 0)
    count["glu"] = 2
    count["evac"] = 4
    count["ada"] = 1
    count["head"] = 0
    plan = []

    def phase(kind, **more):
        adds = more.pop("adds")
        ph = Phase(kind=kind, at=Counts(**count), **more)
        for key, n in adds.items():
            count[key] += n
        plan.append(ph)
        return ph

    def norm(what, chunks, tokens, pieces, shifted, layer, half=0):
        n = chunks * pieces
        return phase("norm", what=what, chunks=chunks, tokens=tokens, pieces=pieces, shifted=shifted, layer=layer,
                     adds=dict(sq=chunks, sum=1, std=1, rstd=1, scaled=n, nout=n if shifted else 0))

    def ada(layer, blocks):
        phase("ada", layer=layer, blocks=blocks, adds=dict(unit=blocks * DC, ada=blocks, derived=1))

    def swiglu(layer, which, tokens):
        halves = tokens // LAT
        norm(which, DC, tokens, halves, True, layer)
        phase("swiglu", layer=layer, tokens=tokens,
              adds=dict(unit=U_SWIGLU, acc=U_SWIGLU, silu=PAIRS, glu=PAIRS))
        phase("down", layer=layer, which=which, tokens=tokens, n=U_DOWN, src="hidden", glu_end=count["glu"],
              adds=dict(unit=U_DOWN, out=4 * U_DOWN, h=DC * halves))

    for l in range(2):
        tokens = TOK if l == 0 else LAT
        halves = tokens // LAT
        tiles = tokens // P
        ada(l, ADA1)
        swiglu(l, "ffn1", TOK)
        norm("mix", DC, TOK, 2, True, l)
        phase("mix_in", layer=l, tokens=tokens, tiles=tiles, adds=dict(unit=U_MIX, acc=MIX_FM + tiles,
                                                                       evac=MIX_FM + tiles))
        norm("q_lat", QC, tokens, 1, False, l)
        norm("kv_lat", KC, TOK, 1, False, l)
        phase("gating", layer=l, tokens=tokens, tiles=tiles, adds=dict(sg=1))
        phase("heads", layer=l, tokens=tokens, tiles=tiles, adds=dict(head=HEADS, headtile=HEADS * tiles))
        phase("turn", layer=l, tokens=tokens, tiles=tiles, adds=dict(merge=4))
        norm("attn", 4, tokens, 1, False, l)
        norm("sg", 2, tokens, 1, False, l)
        norm("cv", 2, tokens, 1, False, l)
        phase("down", layer=l, which="mix", tokens=tokens, n=U_OUT, src="merged", glu_end=0,
              adds=dict(unit=U_OUT, out=4 * U_OUT, h=DC * halves))
        swiglu(l, "ffn2", tokens)
    for l in range(2, 4):
        tokens = TOK if l == 2 else LAT
        halves, tiles = tokens // LAT, tokens // P
        ada(l, ADA2)
        norm("norm1", DC, TOK, 2, True, l)
        phase("gates", layer=l, adds=dict(unit=1, gates=1))
        phase("pairs", layer=l, tokens=tokens, tiles=tiles, adds=dict(pair=HP, pairtile=2 * HP * tiles))
        phase("down", layer=l, which="mix2", tokens=tokens, n=U_OUT, src="merged", glu_end=0,
              adds=dict(unit=U_OUT, out=4 * U_OUT, h=DC * halves))
        norm("norm2", DC, tokens, halves, True, l)
        phase("mlp", layer=l, tokens=tokens, adds=dict(unit=MC, acc=MC, silu=MC, glu=MC))
        phase("down", layer=l, which="mlp", tokens=tokens, n=MC, src="hidden", glu_end=count["glu"],
              adds=dict(unit=MC, out=4 * MC, h=DC * halves))
    norm("final", DC, LAT, 1, False, 4)
    return plan, count


PLAN, TOTAL = make_plan()


def build(nc, stream, head_w, pair_m, pair_n, na_bias, sg_w, masks, consts, params, xT, ctxT, ctx2T, outT):
    units = TOTAL["unit"]
    with ExitStack() as ctx:
        def sb(name, shape):
            return ctx.enter_context(nc.sbuf_tensor(name, shape, F32))

        def sem(name):
            return ctx.enter_context(nc.semaphore(name))

        h = sb("h", [P, DC, TOK])
        xn = sb("xn", [P, DC, TOK])
        ring = sb("ring", [P, RING, UNIT])
        arena = sb("arena", [P, 32, TOK])
        cst = sb("cst", [P, N_CONSTS])
        par = sb("par", [P, N_COLS])
        cond = sb("cond", [P, 2, DC, 2])
        mod = sb("mod", [P, 4, ADA1 * 16])
        gain = sb("gain", [P, 4, 3, 16])
        eps = sb("eps", [P, 1])
        sa = sb("sa", [P, 2, TOK])
        std = sb("std", [P, TOK])
        rstd = sb("rstd", [P, TOK])
        adarow = sb("adarow", [2, UNIT])
        mix = sb("mix", [P, 6720])
        mix_at = [0]

        def carve(*shape):
            n = int(np.prod(shape))
            part = mix[:, mix_at[0]:mix_at[0] + n]
            mix_at[0] += n
            if len(shape) == 1:
                return part
            names = "abcd"[:len(shape)]
            return part.rearrange(f"p ({' '.join(names)}) -> p {' '.join(names)}",
                                  **{k: v for k, v in zip(names[1:], shape[1:])})
        qkraw = sb("qkraw", [P, 2, TOK])
        qkn = sb("qkn", [P, 2, TOK])
        qkt = sb("qkt", [P, 2, TOK])
        vtok = sb("vtok", [P, 4, VD])
        probs = sb("probs", [P, 2, TOK])
        probsT = sb("probsT", [P, 2, TOK])
        nmax = sb("nmax", [P, 4])
        rsum = sb("rsum", [P, 4])
        rinv = sb("rinv", [P, 4])
        gqs = sb("gqs", [P, 1])
        small = sb("small", [P, 64])
        headw = carve(HW)
        attn_tok = carve(4, HEADS * VD)
        vpad = carve(4, 4, P)
        sgw = carve(6 * P)
        zc = carve(2, 2, LAT + 2)
        mix_at[0] = 0
        maskt = carve(2, 4, TOK)
        nabias = carve(2, 2, LAT)
        osig = carve(TOK)
        sel = carve(4, P)[0:64]
        vpair = carve(4, P)
        tok = sb("tok", [P, 4, P])
        wt0 = sb("wt0", [P, 2, TOK])
        PS = ctx.enter_context(nc.psum_tensor("PS", [P, 8, 512], F32))

        qlat, kvlat = arena[:, 0:3, :], arena[:, 3:5, :]
        cv = arena[:, 5:11, :]
        sgu = arena[:, 11:13, :]
        merged = arena[:, 13:21, :]
        sgv = arena[:, 21:23, :].rearrange("p a (b n) -> p (a b) n", n=SG)
        sgt = arena[:, 23:25, :]
        sq = arena[:, 24:32, :]
        hidden = arena
        merged2 = arena[:, 0:8, :]
        g_abs, g_exp, g_ln, g_f, g_b, g_a, g_m, g_guard = (arena[0:64, 8 + j, :] for j in range(8))
        gcol = arena[:, 16, :].rearrange("p (t e d h) -> p t e d h", t=4, e=2, d=2)
        pairw = arena[:, 17:31, :].rearrange("p (j a) n -> p j (a n)", a=2)

        def const(name):
            o, w = CONSTS[name]
            return cst[:, o:o + w]

        def col(name, l, j=0, w=1):
            o, _ = COLS[(name, l) if l is not None else name]
            return par[:, o + j:o + j + w]

        ident, ones = const("ident"), const("ones")

        weights_in = [sem(f"weights_in{s}") for s in range(RING)]
        weights_used = sem("weights_used")
        params_in = sem("params_in")
        x_in = sem("x_in")
        ctx2_in = sem("ctx2_in")
        sgw_in = sem("sgw_in")
        headw_in = sem("headw_in")
        setup_done = sem("setup_done")
        cond_ready = sem("cond_ready")
        ada_mm = sem("ada_mm")
        ada_row = sem("ada_row")
        ada_turned = sem("ada_turned")
        ada_done = sem("ada_done")
        mods_derived = sem("mods_derived")
        acc_ready = sem("acc_ready")
        acc_evacuated = sem("acc_evacuated")
        silu_done = sem("silu_done")
        glu_done = sem("glu_done")
        out_ready = sem("out_ready")
        h_ready = sem("h_ready")
        norm_sq = sem("norm_sq")
        norm_sum = sem("norm_sum")
        norm_std = sem("norm_std")
        norm_rstd = sem("norm_rstd")
        norm_scaled = sem("norm_scaled")
        norm_out = sem("norm_out")
        dve_chain = sem("dve_chain")
        act_chain = sem("act_chain")
        sg_var = sem("sg_var")
        sg_std = sem("sg_std")
        sg_v = sem("sg_v")
        sg_mixed = sem("sg_mixed")
        sg_done = sem("sg_done")
        head_qk = sem("head_qk")
        head_v = sem("head_v")
        head_raw = sem("head_raw")
        head_vtok = sem("head_vtok")
        head_sq = sem("head_sq")
        head_ss = sem("head_ss")
        head_std = sem("head_std")
        head_qn = sem("head_qn")
        head_rot = sem("head_rot")
        head_rope = sem("head_rope")
        score_ready = sem("score_ready")
        max_ready = sem("max_ready")
        exp_done = sem("exp_done")
        probs_turned = sem("probs_turned")
        probsT_ready = sem("probsT_ready")
        pv_ready = sem("pv_ready")
        attn_done = sem("attn_done")
        attn_turned = sem("attn_turned")
        merge_ready = sem("merge_ready")
        out_done = sem("out_done")
        relu_read = silu_done
        masks_in = sem("masks_in")
        pairm_in = sem("pairm_in")
        pairn_in = sem("pairn_in")
        bias_in = sem("bias_in")
        gate_mm = sem("gate_mm")
        gate_softplus = sem("gate_softplus")
        gate_rows = sem("gate_rows")
        gate_guard = sem("gate_guard")
        gate_turned = sem("gate_turned")
        gate_cols = sem("gate_cols")
        pm_acc = sem("pm_acc")
        pm_copied = sem("pm_copied")
        pm_rot = sem("pm_rot")
        pm_rope = sem("pm_rope")
        pm_sel = sem("pm_sel")
        pm_arow = sem("pm_arow")
        pm_score = sem("pm_score")
        pm_logw = sem("pm_logw")
        pm_w = sem("pm_w")
        pm_p = sem("pm_p")
        pm_turned = sem("pm_turned")
        pm_pT = sem("pm_pT")
        pm_pv = sem("pm_pv")
        pm_o = sem("pm_o")
        pm_var = sem("pm_var")
        pm_std = sem("pm_std")
        pm_normed = sem("pm_normed")
        pm_final = sem("pm_final")
        pm_fm = sem("pm_fm")
        na_acc = sem("na_acc")
        na_copied = sem("na_copied")
        na_score = sem("na_score")
        na_max = sem("na_max")
        na_exp = sem("na_exp")
        na_turned = sem("na_turned")
        na_pT = sem("na_pT")
        na_pv = sem("na_pv")
        na_o = sem("na_o")
        na_fm = sem("na_fm")
        pair_done = sem("pair_done")

        def norm_spec(ph):
            l = ph.layer
            s = NormSpec()
            s.dim = ph.chunks * P
            pieces = HALVES[:ph.pieces] if ph.pieces == ph.tokens // LAT and ph.shifted else ((0, ph.tokens, 0),)
            s.pieces = pieces
            if ph.shifted:
                s.src = h
                s.dst = xn
                s.bank = out_bank(0)
                k = {"ffn1": 0, "mix": 1, "ffn2": 2, "norm1": 0, "norm2": 1}[ph.what]
                s.gain = lambda c, cnd: gain[:, l, k, 2 * c + cnd:2 * c + cnd + 1]
                s.shift = lambda c, cnd: mod[:, l, 48 * k + 2 * c + cnd:48 * k + 2 * c + cnd + 1]
            elif ph.what == "final":
                s.src, s.dst, s.bank = h, xn, out_bank(0)
                s.gain = lambda c, cnd: col("final_g", None, c)
            else:
                src, name, j, s.bank = {"q_lat": (qlat, "g_q_lat", 0, 0), "kv_lat": (kvlat, "g_kv_lat", 0, 1),
                                        "attn": (merged[:, 0:4, :], "g_out", 0, 4),
                                        "sg": (merged[:, 4:6, :], "g_out", 4, 5),
                                        "cv": (merged[:, 6:8, :], "g_out", 6, 6)}[ph.what]
                s.src = s.dst = src
                s.gain = lambda c, cnd: col(name, l, j + c)
            return s

        def out_bank(m):
            return (m + 4) % 8

        def h_wait(eng, ph, c):
            if ph.at.h == 0:
                eng.wait_ge(x_in, 32)
            else:
                last = last_down(ph)
                eng.wait_ge(h_ready, last.at.h + (c + 1) * (last.tokens // LAT))
                if ph.layer == 2:
                    eng.wait_ge(ctx2_in, 16)

        def last_down(ph):
            return [q for q in PLAN[:PLAN.index(ph)] if q.kind == "down"][-1]

        block = ctx.enter_context(nc.Block())

        @block.sync
        def _(sp):
            for u in range(RING):
                sp.dma_start(ring[:, u, :], stream[u]).then_inc(weights_in[u], 16)
            whole = units // RING
            with sp.Fori(1, whole) as i:
                for s in range(RING):
                    sp.wait_ge(weights_used, i * RING + (s - RING + 2))
                    sp.dma_start(ring[:, s, :], stream[bass.ds(i * RING + s, 1)].rearrange("o p n -> p (o n)"))\
                        .then_inc(weights_in[s], 16)
            for u in range(whole * RING, units):
                sp.wait_ge(weights_used, u - RING + 2)
                sp.dma_start(ring[:, u % RING, :], stream[u]).then_inc(weights_in[u % RING], 16)
            for c in range(DC):
                sp.wait_ge(norm_scaled, TOTAL["scaled"] - DC + c + 1)
                sp.dma_start(outT[c * P:(c + 1) * P, :], xn[:, c, 0:LAT]).then_inc(out_done, 16)
            sp.wait_ge(out_done, 16 * DC)

        @block.gpsimd
        def _(pool):
            pool.dma_start(sgw[:, :], sg_w[0]).then_inc(sgw_in, 16)
            for ph in PLAN:
                if ph.kind == "gating" and ph.layer == 1:
                    pool.wait_ge(sg_done, ph.at.sg)
                    pool.dma_start(sgw[:, :], sg_w[1]).then_inc(sgw_in, 16)
                if ph.kind == "heads":
                    with pool.Fori(0, HEADS) as i:
                        pool.wait_ge(head_v, i + (ph.at.head + CREDIT))
                        pool.dma_start(headw[:, :], head_w[bass.ds(i + ph.at.head, 1)]
                                       .rearrange("o p n -> p (o n)")).then_inc(headw_in, 16)
                if ph.kind == "norm" and ph.what == "q_lat" and ph.layer == 1:
                    pool.wait_ge(norm_scaled, ph.at.scaled)
                    pool.dma_start(h[:, :, LAT:TOK], ctx2T.rearrange("(c p) t -> p c t", p=P)).then_inc(ctx2_in, 16)
                if ph.kind == "ada" and ph.layer == 2:
                    pool.wait_ge(h_ready, ph.at.h)
                    pool.dma_start(maskt[:, :, :, :], masks).then_inc(masks_in, 16)
                if ph.kind == "pairs":
                    Q0 = ph.at.pair
                    pool.wait_ge(norm_sum, ph.at.sum)
                    with pool.Fori(0, HP) as i:
                        pool.wait_ge(pm_acc, i * 4 + (4 * Q0 + CREDIT))
                        pool.dma_start(pairw[:, 0:4, :].rearrange("p j n -> p (j n)"),
                                       pair_m[bass.ds(i + Q0, 1)].rearrange("o p n -> p (o n)")).then_inc(pairm_in, 16)
                        pool.wait_ge(na_acc, i * 3 + (3 * Q0 + CREDIT))
                        pool.dma_start(pairw[:, 4:7, :].rearrange("p j n -> p (j n)"),
                                       pair_n[bass.ds(i + Q0, 1)].rearrange("o p n -> p (o n)")).then_inc(pairn_in, 16)
                        pool.wait_ge(pair_done, i + (Q0 + CREDIT))
                        pool.dma_start(nabias.rearrange("p a b n -> p (a b n)"),
                                       na_bias[bass.ds(i + Q0, 1)].rearrange("o p n -> p (o n)")).then_inc(bias_in, 16)

        @block.tensor
        def _(pe):
            def unit_in(u0, j, i=0):
                u = u0 + j
                pe.wait_ge(weights_in[u % RING], i * 16 + 16 * (u // RING + 1))
                return u % RING

            def ada(ph):
                if ph.at.h:
                    pe.wait_ge(h_ready, ph.at.h)
                with pe.Fori(0, ph.blocks) as i:
                    for k in range(DC):
                        s = unit_in(ph.at.unit, k, i)
                        if k == 0:
                            pe.wait_ge(ada_row, i + (ph.at.ada))
                        for half in range(2):
                            m = pe.matmul(PS[0:2, 6 + half, :], cond[:, ph.layer // 2, k, :],
                                          ring[:, s, half * 512:half * 512 + 512], start=k == 0, stop=k == DC - 1)
                            if half == 0:
                                m.then_inc(weights_used, 1)
                        if k == DC - 1:
                            m.then_inc(ada_mm, 1)
                    pe.wait_ge(ada_row, i + (ph.at.ada + 1))
                    pe.wait_ge(ada_done, i + ph.at.ada)
                    for c in range(DC):
                        m = pe.matmul(PS[:, 5, 2 * c:2 * c + 2], adarow[:, c * P:(c + 1) * P], ident[0:2, 0:2],
                                      start=True, stop=True)
                    m.then_inc(ada_turned, 1)

            def norm(ph):
                s = norm_spec(ph)
                if ph.at.std:
                    pe.wait_ge(norm_std, ph.at.std)
                for c in range(ph.chunks):
                    pe.wait_ge(norm_sq, ph.at.sq + c + 1)
                    m = pe.matmul(PS[:, s.bank, 0:ph.tokens], ones, sq[:, c, 0:ph.tokens],
                                  start=c == 0, stop=c == ph.chunks - 1)
                m.then_inc(norm_sum, 1)

            def fm_unit(s, bank, tokens):
                for k in range(DC):
                    m = pe.matmul(PS[:, bank, 0:tokens], ring[:, s, k * P:(k + 1) * P], xn[:, k, 0:tokens],
                                  start=k == 0, stop=k == DC - 1)
                    if k == 0:
                        m.then_inc(weights_used, 1)
                m.then_inc(acc_ready, 1)

            def swiglu(ph):
                pe.wait_ge(norm_out, ph.at.nout)
                head = U_SWIGLU % RING

                def pair(i, j):
                    pe.wait_ge(glu_done, i * (RING // 2) + (ph.at.glu + j - 1))
                    for e in range(2):
                        s = unit_in(ph.at.unit, 2 * j + e, i)
                        fm_unit(s, 2 * (j % 2) + e, ph.tokens)
                for j in range(head // 2):
                    pair(0, j)
                with pe.Fori(0, U_SWIGLU // RING) as i:
                    for j in range(RING // 2):
                        pair(i, head // 2 + j)

            def down(ph):
                src = hidden if ph.src == "hidden" else merged if ph.layer < 2 else merged2
                head = ph.n % RING or RING

                def rows(i, k):
                    s = unit_in(ph.at.unit, k, i)
                    if ph.src == "hidden":
                        pe.wait_ge(glu_done, i * RING + (ph.glu_end - ph.n + k + 1))
                    for m_ in range(DC):
                        if ph.src == "hidden" and isinstance(i, int) and k == 0 and m_ == 4:
                            pe.wait_ge(glu_done, ph.glu_end)
                        rhs = src[:, k, 0:ph.tokens] if isinstance(i, int) else \
                            src[:, bass.ds(i * RING + k, 1), 0:ph.tokens].rearrange("p o n -> p (o n)")
                        m = pe.matmul(PS[:, out_bank(m_), 0:ph.tokens], ring[:, s, m_ * P:(m_ + 1) * P], rhs,
                                      start=isinstance(i, int) and k == 0, stop=True, skip_group_check=True)
                        if m_ == 0:
                            m.then_inc(weights_used, 1)
                        if m_ % 2:
                            m.then_inc(out_ready, 1)
                if ph.src == "merged":
                    pe.wait_ge(norm_scaled, ph.at.scaled)
                    if ph.layer >= 2:
                        pe.wait_ge(pair_done, ph.at.pair + CREDIT)
                for k in range(head):
                    rows(0, k)
                if ph.n > head:
                    with pe.Fori(0, (ph.n - head) // RING) as i:
                        for k in range(RING):
                            rows(i, head + k)

            def mix_in(ph):
                pe.wait_ge(norm_out, ph.at.nout)
                for j in range(MIX_FM):
                    pe.wait_ge(acc_evacuated, ph.at.evac + j - 3)
                    s = unit_in(ph.at.unit, j)
                    fm_unit(s, j % 4, TOK if QC <= j <= QC + KC else ph.tokens)
                s = [unit_in(ph.at.unit, MIX_FM + e) for e in range(2)]
                for t in range(ph.tiles):
                    j = MIX_FM + t
                    pe.wait_ge(acc_evacuated, ph.at.evac + j - 3)
                    for k in range(DC):
                        m = pe.matmul(PS[:, j % 4, 0:SG], xn[:, k, t * P:(t + 1) * P],
                                      ring[:, s[k // 4], (k % 4) * SG:(k % 4 + 1) * SG],
                                      start=k == 0, stop=k == DC - 1)
                        if (t, k) in ((0, 0), (ph.tiles - 1, 4)):
                            m.then_inc(weights_used, 1)
                    m.then_inc(acc_ready, 1)

            def gating(ph):
                pe.wait_ge(sgw_in, 16 * (ph.at.sg + 1))
                pe.wait_ge(sg_v, ph.at.sg + 1)
                for t in range(ph.tiles):
                    for cb in range(2):
                        for e in range(2):
                            g = 2 * cb + e
                            m = pe.matmul(PS[:, 5 + cb, t * P:(t + 1) * P], vpad[:, t, g, :],
                                          sgw[:, g * P:(g + 1) * P], start=e == 0, stop=e == 1)
                m.then_inc(sg_mixed, 1)

            def heads(ph):
                tiles, H0, T0 = ph.tiles, ph.at.head, ph.at.headtile
                pe.wait_ge(norm_scaled, ph.at.scaled)
                with pe.Fori(0, HEADS) as i:
                    pe.wait_ge(headw_in, i * 16 + 16 * (H0 + 1))
                    pe.wait_ge(sg_done, ph.at.sg)
                    pe.wait_ge(attn_done, i * tiles + (T0 + CREDIT))
                    for k in range(QC):
                        m = pe.matmul(PS[:, 0, 0:ph.tokens], headw[:, k * P:(k + 1) * P], qlat[:, k, 0:ph.tokens],
                                      start=k == 0, stop=k == QC - 1)
                    m.then_inc(head_qk, 1)
                    for k in range(KC):
                        m = pe.matmul(PS[:, 1, :], headw[:, (QC + k) * P:(QC + k + 1) * P], kvlat[:, k, :],
                                      start=k == 0, stop=k == KC - 1)
                    m.then_inc(head_qk, 1)
                    for t in range(4):
                        for k in range(KC):
                            o = (QC + KC) * P + k * VD
                            m = pe.matmul(PS[:, 2, t * VD:(t + 1) * VD], kvlat[:, k, t * P:(t + 1) * P],
                                          headw[:, o:o + VD], start=k == 0, stop=k == KC - 1)
                    m.then_inc(head_v, 1)
                    pe.wait_ge(head_sq, i * 2 + (2 * H0 + 1))
                    pe.matmul(PS[:, 3, 0:ph.tokens], ones, qkt[:, 0, 0:ph.tokens], start=True, stop=True)
                    pe.wait_ge(head_sq, i * 2 + (2 * H0 + 2))
                    pe.matmul(PS[:, 4, :], ones, qkt[:, 1, :], start=True, stop=True).then_inc(head_ss, 1)
                    pe.wait_ge(head_qn, i * 2 + (2 * H0 + 2))
                    for e in range(2):
                        m = pe.matmul(PS[:, e, 0:LAT], const("rot1"), qkn[:, e, 0:LAT], start=True, stop=True)
                    m.then_inc(head_rot, 1)
                    pe.wait_ge(head_rope, i + (H0 + 1))

                    def scores(t):
                        keys = 0 if t < 2 else LAT
                        if t >= 2:
                            pe.wait_ge(exp_done, i * tiles + (T0 + t - 1))
                        pe.matmul(PS[:, 5 + t % 2, keys:TOK], qkn[:, 0, t * P:(t + 1) * P], qkn[:, 1, keys:TOK],
                                  start=True, stop=True).then_inc(score_ready, 1)

                    def values(t):
                        k0 = 0 if t < 2 else 2
                        bank = 7 if t % 2 == 0 else 3
                        pe.wait_ge(exp_done, i * tiles + (T0 + t + 1))
                        if t >= 2:
                            pe.wait_ge(probsT_ready, i * tiles + (T0 + t - 1))
                        for k in range(k0, 4):
                            m = pe.transpose(PS[:, bank, k * P:(k + 1) * P], probs[:, t % 2, k * P:(k + 1) * P], ident)
                        m.then_inc(probs_turned, 1)
                        pe.wait_ge(probsT_ready, i * tiles + (T0 + t + 1))
                        if t == 0:
                            pe.wait_ge(head_vtok, i + (H0 + 1))
                        if t >= 2:
                            pe.wait_ge(attn_done, i * tiles + (T0 + t - 1 + CREDIT))
                        for k in range(k0, 4):
                            m = pe.matmul(PS[:, 4 - 2 * (t % 2), 0:VD], probsT[:, t % 2, k * P:(k + 1) * P],
                                          vtok[:, k, :], start=k == k0, stop=k == 3)
                        m.then_inc(pv_ready, 1)
                    scores(0)
                    for t in range(1, tiles + 1):
                        if t < tiles:
                            scores(t)
                        values(t - 1)

            def turn(ph):
                pe.wait_ge(attn_done, ph.at.headtile + CREDIT)
                for c in range(4):
                    for t in range(ph.tiles):
                        m = pe.transpose(PS[:, c, t * P:(t + 1) * P], attn_tok[:, t, c * P:(c + 1) * P], ident)
                    m.then_inc(attn_turned, 1)

            def gates(ph):
                pe.wait_ge(norm_out, ph.at.nout)
                s = unit_in(ph.at.unit, 0)
                for e in range(2):
                    for k in range(DC):
                        m = pe.matmul(PS[0:64, e, :], ring[:, s, k * P + 64 * e:k * P + 64 * e + 64], xn[:, k, :],
                                      start=k == 0, stop=k == DC - 1)
                        if e == 0 and k == 0:
                            m.then_inc(weights_used, 1)
                    if k:
                        m.then_inc(gate_mm, 1)
                pe.wait_ge(gate_guard, ph.at.gates + 1)
                for t in range(4):
                    for e, g in enumerate((g_m, g_guard)):
                        m = pe.transpose(PS[:, 2, (2 * t + e) * 64:(2 * t + e + 1) * 64], g[:, t * P:(t + 1) * P],
                                         ident[0:64, 0:64])
                m.then_inc(gate_turned, 1)

            def pairs(ph):
                tiles, Q0, N0, per = ph.tiles, ph.at.pair, ph.at.pairtile, 2 * ph.tiles
                pe.wait_ge(gate_cols, 2 * ph.at.gates)

                def fm(j, bank, tokens):
                    for k in range(DC):
                        m = pe.matmul(PS[:, bank, 0:tokens], pairw[:, j, k * P:(k + 1) * P], xn[:, k, 0:tokens],
                                      start=k == 0, stop=k == DC - 1)
                    return m

                def tm(j, bank):
                    for t in range(4):
                        for k in range(DC):
                            m = pe.matmul(PS[:, bank, t * P:(t + 1) * P], xn[:, k, t * P:(t + 1) * P],
                                          pairw[:, j, k * P:(k + 1) * P], start=k == 0, stop=k == DC - 1)
                    return m

                def score(n, free, ready):
                    e, t = n // tiles, n % tiles
                    keys = 0 if t < 2 else LAT
                    if n >= 2:
                        pe.wait_ge(free, i * per + (N0 + n - 1))
                    r = slice(64 * e, 64 * e + 64)
                    pe.matmul(PS[:, 6 + n % 2, keys:TOK], qkraw[r, 0, t * P:(t + 1) * P], qkraw[r, 1, keys:TOK],
                              start=True, stop=True).then_inc(ready, 1)

                def value(n, made, turned, copied, pv, left):
                    e, t = n // tiles, n % tiles
                    k0 = 0 if t < 2 else 2
                    if n >= 2:
                        pe.wait_ge(copied, i * per + (N0 + n - 1))
                    pe.wait_ge(made, i * per + (N0 + n + 1))
                    for k in range(k0, 4):
                        m = pe.transpose(PS[:, n % 2, k * P:(k + 1) * P], probs[:, n % 2, k * P:(k + 1) * P], ident)
                    m.then_inc(turned, 1)
                    if n >= 2:
                        pe.wait_ge(left, i * per + (N0 + n - 1))
                    pe.wait_ge(copied, i * per + (N0 + n + 1))
                    for k in range(k0, 4):
                        m = pe.matmul(PS[:, 2 + n % 2, 0:HD], probsT[:, n % 2, k * P:(k + 1) * P],
                                      vpair[:, k, e * HD:(e + 1) * HD], start=k == k0, stop=k == 3)
                    m.then_inc(pv, 1)

                def turn_tok(sem_):
                    for t in range(tiles):
                        m = pe.transpose(PS[:, 4, t * P:(t + 1) * P], tok[:, t, :], ident)
                    m.then_inc(sem_, 1)

                with pe.Fori(0, HP) as i:
                    pe.wait_ge(pairm_in, i * 16 + 16 * (Q0 + 1))
                    pe.wait_ge(pair_done, i + (Q0 + CREDIT))
                    fm(0, 0, ph.tokens).then_inc(pm_acc, 1)
                    fm(1, 1, TOK).then_inc(pm_acc, 1)
                    fm(3, 2, ph.tokens).then_inc(pm_acc, 1)
                    tm(2, 3).then_inc(pm_acc, 1)
                    pe.wait_ge(pm_copied, i * 4 + (4 * Q0 + 2))
                    for e in range(2):
                        m = pe.matmul(PS[:, e, 0:LAT], const("rot2"), qkraw[:, e, 0:LAT], start=True, stop=True)
                    m.then_inc(pm_rot, 1)
                    pe.wait_ge(pm_sel, i + (Q0 + 1))

                    def arow(e):
                        if e:
                            pe.wait_ge(pm_logw, i * per + (N0 + tiles))
                        for d in range(2):
                            m = pe.matmul(PS[:, 4 + d, :], sel[:, 2 * d + e, :], g_a, start=True, stop=True)
                        m.then_inc(pm_arow, 1)
                    arow(0)
                    pe.wait_ge(pm_copied, i * 4 + (4 * Q0 + 4))
                    pe.wait_ge(pm_rope, i + (Q0 + 1))
                    score(0, pm_p, pm_score)
                    for n in range(1, per + 1):
                        if n < per:
                            score(n, pm_p, pm_score)
                        if n == tiles:
                            arow(1)
                        value(n - 1, pm_p, pm_turned, pm_pT, pm_pv, pm_o)
                    pe.wait_ge(pm_normed, i + (Q0 + 1))
                    turn_tok(pm_fm)
                    pe.wait_ge(pairn_in, i * 16 + 16 * (Q0 + 1))
                    fm(4, 0, ph.tokens).then_inc(na_acc, 1)
                    fm(5, 1, TOK).then_inc(na_acc, 1)
                    tm(6, 3).then_inc(na_acc, 1)
                    pe.wait_ge(na_copied, i * 3 + (3 * Q0 + 3))
                    score(0, na_exp, na_score)
                    for n in range(1, per + 1):
                        if n < per:
                            score(n, na_exp, na_score)
                        value(n - 1, na_exp, na_turned, na_pT, na_pv, na_o)
                    pe.wait_ge(na_o, i * per + (N0 + per))
                    pe.wait_ge(pm_final, i + (Q0 + 1))
                    turn_tok(na_fm)

            def mlp(ph):
                pe.wait_ge(norm_out, ph.at.nout)
                with pe.Fori(0, MC // RING) as i:
                    for j in range(RING):
                        pe.wait_ge(relu_read, i * RING + (ph.at.silu + j - 3))
                        s = unit_in(ph.at.unit, j, i)
                        fm_unit(s, j % 4, ph.tokens)

            pe.wait_ge(setup_done, 1)
            pe.wait_ge(params_in, 32)
            pe.wait_ge(cond_ready, 2)
            run = dict(ada=ada, norm=norm, swiglu=swiglu, down=down, mix_in=mix_in, gating=gating, heads=heads,
                       turn=turn, gates=gates, pairs=pairs, mlp=mlp)
            for ph in PLAN:
                run[ph.kind](ph)

        @block.scalar
        def _(act):
            chain = [0]

            def link(ins):
                chain[0] += 1
                ins.then_inc(act_chain, 1)
                act.wait_ge(act_chain, chain[0])

            act.dma_start(cst[:, :], consts).then_inc(params_in, 16)
            act.dma_start(par[:, :], params).then_inc(params_in, 16)
            act.dma_start(h[:, :, 0:LAT], xT.rearrange("(c p) t -> p c t", p=P)).then_inc(x_in, 16)
            act.dma_start(h[:, :, LAT:TOK], ctxT.rearrange("(c p) t -> p c t", p=P)).then_inc(x_in, 16)
            act.wait_ge(params_in, 32)
            act.wait_ge(setup_done, 1)
            for b in range(2):
                o, w = COLS[f"cond{b + 1}"]
                act.activation(cond[:, b, :, :].rearrange("p c j -> p (c j)"), par[:, o:o + w], ACT.Silu)\
                    .then_inc(cond_ready, 1)

            def ada(ph):
                with act.Fori(0, ph.blocks) as i:
                    act.wait_ge(ada_mm, i + ph.at.ada)
                    act.activation(adarow[:, :], PS[0:2, 6:8, :].rearrange("p a n -> p (a n)"), ACT.Copy)\
                        .then_inc(ada_row, 1)

            def norm(ph):
                s = norm_spec(ph)
                if ph.at.sum:
                    act.wait_ge(norm_sum, ph.at.sum)
                halves = ph.tokens // LAT
                for c in range(ph.chunks):
                    if s.src is h:
                        h_wait(act, ph, c)
                    elif ph.what == "sg" or ph.what == "cv":
                        act.wait_ge(sg_done, ph.at.sg)
                    act.activation(sq[:, c, 0:ph.tokens], s.src[:, c, 0:ph.tokens], ACT.Square).then_inc(norm_sq, 1)
                act.wait_ge(norm_sum, ph.at.sum + 1)
                if ph.at.rstd:
                    act.wait_ge(norm_rstd, ph.at.rstd)
                act.activation(std[:, 0:ph.tokens], PS[:, s.bank, 0:ph.tokens], ACT.Sqrt, bias=eps[:, :],
                               scale=1.0 / s.dim).then_inc(norm_std, 1)
                if ph.shifted:
                    n = 0
                    for c in range(ph.chunks):
                        for a, b, cnd in s.pieces:
                            n += 1
                            act.wait_ge(norm_scaled, ph.at.scaled + n)
                            act.activation(s.dst[:, c, a:b], s.dst[:, c, a:b], ACT.Identity, bias=s.shift(c, cnd))\
                                .then_inc(norm_out, 1)

            def swiglu(ph):
                head = U_SWIGLU % RING // 2

                def pair(i, j):
                    act.wait_ge(acc_ready, i * RING + (ph.at.acc + 2 * j + 1))
                    act.wait_ge(glu_done, i * (RING // 2) + (ph.at.glu + j - 1))
                    act.activation(sa[:, j % 2, 0:ph.tokens], PS[:, 2 * (j % 2), 0:ph.tokens], ACT.Silu)\
                        .then_inc(silu_done, 1)
                for j in range(head):
                    pair(0, j)
                with act.Fori(0, U_SWIGLU // RING) as i:
                    for j in range(RING // 2):
                        pair(i, head + j)

            def mlp(ph):
                with act.Fori(0, MC // RING) as i:
                    for j in range(RING):
                        act.wait_ge(acc_ready, i * RING + (ph.at.acc + j + 1))
                        act.wait_ge(glu_done, i * RING + (ph.at.glu + j - 1))
                        act.activation(sa[:, j % 2, 0:ph.tokens], PS[:, j % 4, 0:ph.tokens], ACT.Relu)\
                            .then_inc(relu_read, 1)

            def mix_in(ph):
                for j in range(MIX_FM + ph.tiles):
                    act.wait_ge(acc_ready, ph.at.acc + j + 1)
                    bank = PS[:, j % 4, :]
                    if j < QC + KC:
                        n = ph.tokens if j < QC else TOK
                        ins = act.activation(arena[:, j, 0:n], bank[:, 0:n], ACT.Copy)
                    elif j == QC + KC:
                        ins = act.activation(qkraw[64:128, 1, :], bank[64:128, :], ACT.Copy)
                    elif j < MIX_FM - 2:
                        ins = act.activation(arena[:, j - 1, 0:ph.tokens], bank[:, 0:ph.tokens], ACT.Copy)
                    elif j < MIX_FM:
                        ins = act.activation(arena[:, j - 1, 0:ph.tokens], bank[:, 0:ph.tokens],
                                             ACT.Gelu_apprx_tanh)
                    else:
                        ins = act.activation(sgv[:, j - MIX_FM, :], bank[:, 0:SG], ACT.Gelu_apprx_tanh)
                    ins.then_inc(acc_evacuated, 1)

            def gating(ph):
                act.wait_ge(sg_var, ph.at.sg + 1)
                act.activation(sgt[:, 1, 0:4 * ph.tiles], sgt[:, 1, 32:32 + 4 * ph.tiles], ACT.Sqrt, bias=eps[:, :],
                               scale=1.0 / 64).then_inc(sg_std, 1)

            def heads(ph):
                tiles, H0, T0 = ph.tiles, ph.at.head, ph.at.headtile
                with act.Fori(0, HEADS) as i:
                    act.wait_ge(head_qk, i * 2 + (2 * H0 + 1))
                    act.activation(qkraw[:, 0, 0:ph.tokens], PS[:, 0, 0:ph.tokens], ACT.Copy).then_inc(head_raw, 1)
                    act.wait_ge(head_qk, i * 2 + (2 * H0 + 2))
                    act.activation(qkraw[0:64, 1, :], PS[0:64, 1, :], ACT.Copy).then_inc(head_raw, 1)
                    act.wait_ge(head_raw, i * 2 + (2 * H0 + 1))
                    act.activation(qkt[:, 0, 0:ph.tokens], qkraw[:, 0, 0:ph.tokens], ACT.Square).then_inc(head_sq, 1)
                    act.wait_ge(head_raw, i * 2 + (2 * H0 + 2))
                    act.activation(qkt[:, 1, :], qkraw[:, 1, :], ACT.Square).then_inc(head_sq, 1)
                    act.wait_ge(head_v, i + (H0 + 1 + CREDIT))
                    act.activation(vtok[:, :, :].rearrange("p t d -> p (t d)"), PS[:, 2, 0:4 * VD], ACT.Copy)\
                        .then_inc(head_vtok, 1)
                    act.wait_ge(head_ss, i + (H0 + 1))
                    act.activation(probsT[:, 0, 0:ph.tokens], PS[:, 3, 0:ph.tokens], ACT.Sqrt, bias=eps[:, :],
                                   scale=1.0 / QK).then_inc(head_std, 1)
                    act.activation(probsT[:, 1, :], PS[:, 4, :], ACT.Sqrt, bias=eps[:, :],
                                   scale=1.0 / QK).then_inc(head_std, 1)

                    def exps(t):
                        k = 0 if t < 2 else LAT
                        act.wait_ge(max_ready, i * tiles + (T0 + t + 1))
                        if t >= 2:
                            act.wait_ge(probs_turned, i * tiles + (T0 + t - 1))
                        act.activation(probs[:, t % 2, k:TOK], PS[:, 5 + t % 2, k:TOK], ACT.Exp,
                                       bias=nmax[:, t:t + 1], accum_out=rsum[:, t:t + 1]).then_inc(exp_done, 1)

                    def turned(t):
                        k = 0 if t < 2 else LAT
                        act.wait_ge(probs_turned, i * tiles + (T0 + t + 1))
                        if t >= 2:
                            act.wait_ge(pv_ready, i * tiles + (T0 + t - 1))
                        act.activation(probsT[:, t % 2, k:TOK], PS[:, 7 if t % 2 == 0 else 3, k:TOK], ACT.Copy)\
                            .then_inc(probsT_ready, 1)
                    exps(0)
                    for t in range(1, tiles + 1):
                        if t < tiles:
                            exps(t)
                        turned(t - 1)

            def turn(ph):
                for c in range(4):
                    act.wait_ge(attn_turned, ph.at.merge + c + 1)
                    act.activation(merged[:, c, 0:ph.tokens], PS[:, c, 0:ph.tokens], ACT.Copy)\
                        .then_inc(merge_ready, 1)
                act.wait_ge(merge_ready, ph.at.merge + 4)

            def gates(ph):
                G = ph.at.gates
                act.wait_ge(gate_mm, 2 * G + 2)
                o, _ = COLS[("b_gate", ph.layer)]
                link(act.activation(g_abs, PS[0:64, 1, :], ACT.Abs, bias=par[0:64, o + 1:o + 2]))
                link(act.activation(g_exp, g_abs, ACT.Exp, scale=-1.0))
                act.activation(g_ln, g_exp, ACT.Ln, bias=1.0).then_inc(gate_softplus, 1)
                act.wait_ge(gate_rows, G + 1)
                act.activation(g_guard, g_guard, ACT.Exp, scale=-1.0).then_inc(gate_guard, 1)
                act.wait_ge(gate_turned, G + 1)
                turned = PS[:, 2, :].rearrange("p (t e n) -> p t e n", t=4, e=2)
                cols = arena[:, 16, :].rearrange("p (t e n) -> p t e n", t=4, e=2)
                act.activation(cols[:, :, 0, :], turned[:, :, 0, :], ACT.Copy, scale=-1.0).then_inc(gate_cols, 1)
                act.activation(cols[:, :, 1, :], turned[:, :, 1, :], ACT.Copy).then_inc(gate_cols, 1)

            def pairs(ph):
                tiles, Q0, N0, per, T = ph.tiles, ph.at.pair, ph.at.pairtile, 2 * ph.tiles, ph.tokens
                with act.Fori(0, HP) as i:
                    def copied(acc, n, per_acc, sem_, out, in_, func=ACT.Copy, **kw):
                        act.wait_ge(acc, i * per_acc + (per_acc * Q0 + n + CREDIT))
                        act.activation(out, in_, func, **kw).then_inc(sem_, 1)

                    def transposed(n, turned, pv, sem_):
                        k = 0 if n % tiles < 2 else LAT
                        act.wait_ge(turned, i * per + (N0 + n + 1))
                        if n >= 2:
                            act.wait_ge(pv, i * per + (N0 + n - 1))
                        act.activation(probsT[:, n % 2, k:TOK], PS[:, n % 2, k:TOK], ACT.Copy).then_inc(sem_, 1)

                    v = vpair.rearrange("p t d -> p (t d)")
                    copied(pm_acc, 1, 4, pm_copied, qkraw[:, 0, 0:T], PS[:, 0, 0:T], scale=float(HD) ** -0.5)
                    copied(pm_acc, 2, 4, pm_copied, qkraw[:, 1, :], PS[:, 1, :])
                    copied(pm_acc, 3, 4, pm_copied, osig[:, 0:T], PS[:, 2, 0:T], ACT.Sigmoid)
                    copied(pm_acc, 4, 4, pm_copied, v, PS[:, 3, :])

                    def weigh(n):
                        k = 0 if n % tiles < 2 else LAT
                        w = (wt0, qkn)[n % 2]
                        act.wait_ge(pm_logw, i * per + (N0 + n + 1))
                        act.activation(w[:, :, k:TOK], w[:, :, k:TOK], ACT.Exp).then_inc(pm_w, 1)

                    weigh(0)
                    for n in range(per):
                        if n + 1 < per:
                            weigh(n + 1)
                        transposed(n, pm_turned, pm_pv, pm_pT)
                        act.wait_ge(pm_pv, i * per + (N0 + n + 1))
                        e, t = n // tiles, n % tiles
                        act.activation(tok[:, t, e * HD:(e + 1) * HD], PS[:, 2 + n % 2, 0:HD], ACT.Copy)\
                            .then_inc(pm_o, 1)
                    act.wait_ge(pm_var, i + (Q0 + 1))
                    act.activation(small[:, 16:16 + per], small[:, 8:8 + per], ACT.Sqrt, bias=eps[:, :],
                                   scale=1.0 / HD).then_inc(pm_std, 1)

                    copied(na_acc, 1, 3, na_copied, qkraw[:, 0, 0:T], PS[:, 0, 0:T], scale=float(HD) ** -0.5)
                    copied(na_acc, 2, 3, na_copied, qkraw[:, 1, :], PS[:, 1, :])
                    copied(na_acc, 3, 3, na_copied, v, PS[:, 3, :])

                    def exps(n):
                        k = 0 if n % tiles < 2 else LAT
                        act.wait_ge(na_max, i * per + (N0 + n + 1))
                        if n >= 2:
                            act.wait_ge(na_turned, i * per + (N0 + n - 1))
                        act.activation(probs[:, n % 2, k:TOK], PS[:, 6 + n % 2, k:TOK], ACT.Exp,
                                       bias=small[:, 32 + n:33 + n], accum_out=small[:, 40 + n:41 + n])\
                            .then_inc(na_exp, 1)
                    exps(0)
                    for n in range(per):
                        if n + 1 < per:
                            exps(n + 1)
                        transposed(n, na_turned, na_pv, na_pT)

            run = dict(ada=ada, norm=norm, swiglu=swiglu, down=lambda ph: None, mix_in=mix_in, gating=gating,
                       heads=heads, turn=turn, gates=gates, pairs=pairs, mlp=mlp)
            for ph in PLAN:
                if ph.kind == "norm" and ph.what in ("q_lat", "kv_lat"):
                    act.wait_ge(acc_evacuated, ph.at.evac)
                run[ph.kind](ph)

        @block.vector
        def _(dve):
            chain = [0, None, 0]

            def link(ins):
                chain[0] += 1
                ins.then_inc(dve_chain, 1)
                if chain[1] is None:
                    dve.wait_ge(dve_chain, chain[0])
                else:
                    dve.wait_ge(dve_chain, chain[1] * chain[2] + chain[0])

            def loop(i, per):
                chain[1], chain[2] = i, per
                return chain[0]

            def loop_end(start, times):
                assert chain[0] - start == chain[2], (chain[0] - start, chain[2])
                chain[0] = start + chain[2] * times
                chain[1] = None

            tt = dve.tensor_tensor
            stt = dve.scalar_tensor_tensor
            link(dve.memset(vpad[:, :, :, :], 0.0))
            link(dve.memset(zc[:, :, :, :], 0.0))
            dve.memset(eps[:, :], EPS).then_inc(setup_done, 1)
            dve.sem_inc(glu_done, 2)
            dve.sem_inc(acc_evacuated, 4)
            dve.sem_inc(ada_row, 1)
            dve.sem_inc(ada_done, 1)
            for s in (head_v, attn_done, pm_acc, na_acc, pair_done):
                dve.sem_inc(s, CREDIT)
            dve.wait_ge(params_in, 32)

            def ada(ph):
                l = ph.layer
                ob, _ = COLS[("b_ada", l)]
                with dve.Fori(0, ph.blocks) as i:
                    dve.wait_ge(ada_turned, i + ph.at.ada)
                    tt(mod[:, l, bass.ds(i * 16, 16)], PS[:, 5, 0:16], par[:, bass.ds(i * 16 + ob, 16)],
                       ALU.add).then_inc(ada_done, 1)
                dve.wait_ge(ada_done, ph.at.ada + ph.blocks)
                if l < 2:
                    for k, name in enumerate(("g_ffn1", "g_mix", "g_ffn2")):
                        link(stt(gain[:, l, k, :], mod[:, l, 48 * k + 16:48 * k + 32], 1.0, col(name, l, 0, 16),
                                 ALU.add, ALU.mult))
                    for k in (0, 2):
                        g = mod[:, l, 48 * k + 32:48 * k + 48]
                        link(dve.tensor_scalar(g, g, 0.5, None, ALU.mult))
                else:
                    for k, name in enumerate(("norm1_g", "norm2_g")):
                        link(stt(gain[:, l, k, :], mod[:, l, 48 * k + 16:48 * k + 32], 1.0, col(name, l, 0, 16),
                                 ALU.add, ALU.mult))

            def norm(ph):
                s = norm_spec(ph)
                dve.wait_ge(norm_std, ph.at.std + 1)
                if ph.at.scaled:
                    dve.wait_ge(norm_scaled, ph.at.scaled)
                dve.reciprocal(rstd[:, 0:ph.tokens], std[:, 0:ph.tokens]).then_inc(norm_rstd, 1)
                dve.wait_ge(norm_rstd, ph.at.rstd + 1)
                for c in range(ph.chunks):
                    for a, b, cnd in s.pieces:
                        stt(s.dst[:, c, a:b], s.src[:, c, a:b], s.gain(c, cnd), rstd[:, a:b], ALU.mult, ALU.mult)\
                            .then_inc(norm_scaled, 1)

            def swiglu(ph):
                head = U_SWIGLU % RING // 2

                def pair(i, j):
                    dst = hidden[:, j, 0:ph.tokens] if isinstance(i, int) else \
                        hidden[:, bass.ds(i * (RING // 2) + j, 1), 0:ph.tokens].rearrange("p o n -> p (o n)")
                    dve.wait_ge(silu_done, i * (RING // 2) + (ph.at.silu + j + 1))
                    dve.wait_ge(acc_ready, i * RING + (ph.at.acc + 2 * j + 2))
                    tt(dst, PS[:, 2 * (j % 2) + 1, 0:ph.tokens], sa[:, j % 2, 0:ph.tokens], ALU.mult)\
                        .then_inc(glu_done, 1)
                for j in range(head):
                    pair(0, j)
                with dve.Fori(0, U_SWIGLU // RING) as i:
                    for j in range(RING // 2):
                        pair(i, head + j)

            def down(ph):
                g0 = {"ffn1": 32, "mix": 80, "ffn2": 128, "mix2": 32, "mlp": 80}[ph.which]
                for m in range(DC):
                    dve.wait_ge(out_ready, ph.at.out + 4 * (ph.n - 1) + m // 2 + 1)
                    for a, b, cnd in HALVES[:ph.tokens // LAT]:
                        g = g0 + 2 * m + cnd
                        stt(h[:, m, a:b], PS[:, out_bank(m), a:b], mod[:, ph.layer, g:g + 1], h[:, m, a:b],
                            ALU.mult, ALU.add).then_inc(h_ready, 1)

            def gating(ph):
                l, n = ph.layer, ph.tiles
                dve.wait_ge(acc_evacuated, ph.at.evac)
                v = sgv[:, 0:n, :].rearrange("p t c -> p (t c)")
                t0 = sgt[:, 0:1, :].rearrange("p o n -> p (o n)")
                for q in range(n // 2):
                    part = v[:, q * 512:(q + 1) * 512]
                    link(tt(t0, part, part, ALU.mult))
                    red = dve.tensor_reduce(sgt[:, 1, 32 + 8 * q:40 + 8 * q], t0.rearrange("p (g c) -> p g c", c=64),
                                            AXX, ALU.add)
                    if q == n // 2 - 1:
                        red.then_inc(sg_var, 1)
                    else:
                        link(red)
                dve.wait_ge(sg_std, ph.at.sg + 1)
                link(dve.reciprocal(sgt[:, 1, 64:64 + 4 * n], sgt[:, 1, 0:4 * n]))
                if ph.at.sg:
                    dve.wait_ge(sg_mixed, ph.at.sg)
                for e in range(2):
                    src = sgv[:, 0:n, :].rearrange("p t (g e c) -> p t g e c", e=2, c=64)[:, :, :, e, :]
                    r = sgt[:, 1, 64:64 + 4 * n].rearrange("p (t g e) -> p t g e", e=2, g=2)[:, :, :, e:e + 1]\
                        .broadcast_to([P, n, 2, 64])
                    dst = vpad[:, 0:n, :, :].rearrange("p t (g e) c -> p t g e c", e=2)[:, :, :, e,
                                                                                       64 * e:64 * e + 64]
                    ins = tt(dst, src, r, ALU.mult)
                    if e == 0:
                        link(ins)
                ins.then_inc(sg_v, 1)
                hs = ph.tokens // LAT
                for cb in range(2):
                    part = lambda j: cv[:, 2 * j + cb, 0:ph.tokens].rearrange("p (s t) -> p s t", s=hs)
                    z = zc[:, cb, 0:hs, :]
                    y = merged[:, 6 + cb, 0:ph.tokens].rearrange("p (s t) -> p s t", s=hs)
                    link(tt(z[:, :, 1:LAT + 1], part(1), part(2), ALU.mult))
                    w = lambda k: col("w_conv", l, 3 * cb + k)
                    link(dve.tensor_scalar(y, z[:, :, 0:LAT], w(0), None, ALU.mult))
                    link(stt(y, z[:, :, 1:LAT + 1], w(1), y, ALU.mult, ALU.add))
                    link(stt(y, z[:, :, 2:LAT + 2], w(2), y, ALU.mult, ALU.add))
                    link(tt(y, y, part(0), ALU.mult))
                dve.wait_ge(sg_mixed, ph.at.sg + 1)
                for cb in range(2):
                    b = sgw[:, (4 + cb) * P:(5 + cb) * P].rearrange("p (o n) -> p o n", o=1).broadcast_to([P, n, P])
                    y = merged[:, 4 + cb, 0:ph.tokens]
                    link(stt(y.rearrange("p (t n) -> p t n", n=P),
                             PS[:, 5 + cb, 0:ph.tokens].rearrange("p (t n) -> p t n", n=P),
                             col("g_sgu", l, cb), b, ALU.mult, ALU.add))
                    link(tt(y, y, sgu[:, cb, 0:ph.tokens], ALU.mult))
                dve.tensor_scalar(gqs[:, :], col("g_q_head", l), float(QK) ** -0.5, None, ALU.mult)\
                    .then_inc(sg_done, 1)

            def heads(ph):
                l, tiles, H0, T0 = ph.layer, ph.tiles, ph.at.head, ph.at.headtile
                dve.wait_ge(sg_done, ph.at.sg)
                with dve.Fori(0, HEADS) as i:
                    start = loop(i, 4 + tiles)
                    dve.wait_ge(head_std, i * 2 + (2 * H0 + 1))
                    link(dve.reciprocal(probs[:, 0, 0:ph.tokens], probsT[:, 0, 0:ph.tokens]))
                    stt(qkn[:, 0, 0:ph.tokens], qkraw[:, 0, 0:ph.tokens], gqs[:, :], probs[:, 0, 0:ph.tokens],
                        ALU.mult, ALU.mult).then_inc(head_qn, 1)
                    dve.wait_ge(head_std, i * 2 + (2 * H0 + 2))
                    link(dve.reciprocal(probs[:, 1, :], probsT[:, 1, :]))
                    stt(qkn[:, 1, :], qkraw[:, 1, :], col("g_k_head", l), probs[:, 1, :], ALU.mult, ALU.mult)\
                        .then_inc(head_qn, 1)
                    trig = lambda name: const(name).rearrange("p (o n) -> p o n", o=1).broadcast_to([P, 2, LAT])
                    dve.wait_ge(head_rot, i + (H0 + 1))
                    link(tt(qkt[:, :, 0:LAT], PS[:, 0:2, 0:LAT], trig("sin1"), ALU.mult))
                    link(tt(qkn[:, :, 0:LAT], qkn[:, :, 0:LAT], trig("cos1"), ALU.mult))
                    tt(qkn[:, :, 0:LAT], qkn[:, :, 0:LAT], qkt[:, :, 0:LAT], ALU.add).then_inc(head_rope, 1)

                    def maxes(t):
                        k = 0 if t < 2 else LAT
                        dve.wait_ge(score_ready, i * tiles + (T0 + t + 1))
                        dve.tensor_reduce(nmax[:, t:t + 1], PS[:, 5 + t % 2, k:TOK], AXX, ALU.max, negate=True)\
                            .then_inc(max_ready, 1)

                    def outs(t):
                        dve.wait_ge(exp_done, i * tiles + (T0 + t + 1))
                        link(dve.reciprocal(rinv[:, t:t + 1], rsum[:, t:t + 1]))
                        dve.wait_ge(pv_ready, i * tiles + (T0 + t + 1))
                        dve.tensor_scalar(attn_tok[:, t, bass.ds(i * VD, VD)], PS[:, 4 - 2 * (t % 2), 0:VD],
                                          rinv[:, t:t + 1], None, ALU.mult).then_inc(attn_done, 1)
                    maxes(0)
                    for t in range(1, tiles + 1):
                        if t < tiles:
                            maxes(t)
                        outs(t - 1)
                    loop_end(start, HEADS)

            def gates(ph):
                G = ph.at.gates
                o, _ = COLS[("b_gate", ph.layer)]
                dve.wait_ge(gate_mm, 2 * G + 2)
                dve.wait_ge(gate_softplus, G + 1)
                link(dve.tensor_scalar(g_f, PS[0:64, 1, :], par[0:64, o + 1:o + 2], 0.0, ALU.add, ALU.min))
                link(tt(g_f, g_f, g_ln, ALU.subtract))

                def scan(out, src, initial, op0, op1):
                    for rows, back, edge in ((slice(0, 32), False, TOK - 1), (slice(32, 64), True, LAT)):
                        for part, first in ((slice(LAT, TOK), True), (slice(0, LAT), False)):
                            o_, s_ = out[rows, part], src[rows, part]
                            if back:
                                o_, s_ = o_[:, ::-1], s_[:, ::-1]
                            link(dve.tensor_tensor_scan(o_, s_, s_, initial if first else out[rows, edge:edge + 1],
                                                        op0, op1))
                scan(g_b, g_f, 0.0, ALU.add, ALU.bypass)
                link(stt(g_a, PS[0:64, 0, :], par[0:64, o:o + 1], g_b, ALU.add, ALU.subtract))
                scan(g_m, g_a, 0.0, ALU.max, ALU.max)
                tt(g_guard, g_b, g_m, ALU.add).then_inc(gate_rows, 1)
                dve.wait_ge(gate_cols, 2 * G + 2)
                dve.wait_ge(masks_in, 16)

            def pairs(ph):
                tiles, Q0, N0, per, T = ph.tiles, ph.at.pair, ph.at.pairtile, 2 * ph.tiles, ph.tokens
                og, _ = COLS[("norm_g", ph.layer)]
                mtok = tok[:, 0:tiles, :].rearrange("p t (e d) -> p (t e) d", e=2)
                tmp = qkt[:, 0, 0:T].rearrange("p (g d) -> p g d", d=HD)
                with dve.Fori(0, HP) as i:
                    start = loop(i, 11 + 6 * per)
                    for d in range(2):
                        for e in range(2):
                            ins = dve.tensor_scalar(sel[:, 2 * d + e, :], ones[0:64, :],
                                                    ident[0:64, bass.ds(i * 2 + (32 * d + e), 1)], None, ALU.mult)
                    ins.then_inc(pm_sel, 1)
                    trig = lambda name: const(name).rearrange("p (o n) -> p o n", o=1).broadcast_to([P, 2, LAT])
                    dve.wait_ge(pm_rot, i + (Q0 + 1))
                    link(tt(qkt[:, :, 0:LAT], PS[:, 0:2, 0:LAT], trig("sin2"), ALU.mult))
                    link(tt(qkraw[:, :, 0:LAT], qkraw[:, :, 0:LAT], trig("cos2"), ALU.mult))
                    tt(qkraw[:, :, 0:LAT], qkraw[:, :, 0:LAT], qkt[:, :, 0:LAT], ALU.add).then_inc(pm_rope, 1)

                    def log_weights(n):
                        e, t = n // tiles, n % tiles
                        k = 0 if t < 2 else LAT
                        w = (wt0, qkn)[n % 2]
                        dve.wait_ge(pm_arow, i * 2 + (2 * Q0 + e + 1))
                        for d in range(2):
                            ins = stt(w[:, d, k:TOK], PS[:, 4 + d, k:TOK],
                                      gcol[:, t, 0, d, bass.ds(i * 2 + e, 1)], maskt[:, d, t, k:TOK],
                                      ALU.add, ALU.add)
                        ins.then_inc(pm_logw, 1)

                    def weighted(n):
                        e, t = n // tiles, n % tiles
                        k = 0 if t < 2 else LAT
                        w = (wt0, qkn)[n % 2]
                        dve.wait_ge(pm_w, i * per + (N0 + n + 1))
                        dve.wait_ge(pm_score, i * per + (N0 + n + 1))
                        for d in range(2):
                            ins = dve.tensor_tensor_reduce(w[:, d, k:TOK], PS[:, 6 + n % 2, k:TOK], w[:, d, k:TOK],
                                                           1.0, 0.0, ALU.mult, ALU.add, small[:, d:d + 1])
                        link(ins)
                        link(stt(small[:, 2:4], small[:, 0:2], -1.0, small[:, 0:2], ALU.mult, ALU.max))
                        link(tt(small[:, 2:4], small[:, 2:4],
                                gcol[:, t, 1, :, bass.ds(i * 2 + e, 1)].rearrange("p d o -> p (d o)"), ALU.max))
                        link(dve.reciprocal(small[:, 4:6], small[:, 2:4]))
                        link(dve.tensor_scalar(w[:, 1, k:TOK], w[:, 1, k:TOK], small[:, 5:6], None, ALU.mult))
                        if n >= 2:
                            dve.wait_ge(pm_turned, i * per + (N0 + n - 1))
                        stt(probs[:, n % 2, k:TOK], w[:, 0, k:TOK], small[:, 4:5], w[:, 1, k:TOK], ALU.mult, ALU.add)\
                            .then_inc(pm_p, 1)
                        dve.wait_ge(pm_p, i * per + (N0 + n + 1))

                    log_weights(0)
                    for n in range(per):
                        if n + 1 < per:
                            log_weights(n + 1)
                        weighted(n)
                    dve.wait_ge(pm_o, i * per + (N0 + per))
                    mu = small[:, 0:per]
                    link(dve.tensor_reduce(mu, mtok, AXX, ALU.add))
                    link(dve.tensor_scalar(mu, mu, 1.0 / HD, None, ALU.mult))
                    wide = lambda a: a.rearrange("p (g o) -> p g o", o=1).broadcast_to([P, per, HD])
                    link(tt(mtok, mtok, wide(mu), ALU.subtract))
                    link(tt(tmp, mtok, mtok, ALU.mult))
                    dve.tensor_reduce(small[:, 8:8 + per], tmp, AXX, ALU.add).then_inc(pm_var, 1)
                    dve.wait_ge(pm_std, i + (Q0 + 1))
                    link(dve.reciprocal(small[:, 24:24 + per], small[:, 16:16 + per]))
                    tt(mtok, mtok, wide(small[:, 24:24 + per]), ALU.mult).then_inc(pm_normed, 1)
                    dve.wait_ge(pm_fm, i + (Q0 + 1))
                    stt(merged2[:, bass.ds(i, 1), 0:T].rearrange("p o n -> p (o n)"), PS[:, 4, 0:T],
                        par[:, bass.ds(i + og, 1)], osig[:, 0:T], ALU.mult, ALU.mult).then_inc(pm_final, 1)

                    dve.wait_ge(bias_in, i * 16 + 16 * (Q0 + 1))

                    def maxes(n):
                        e, t = n // tiles, n % tiles
                        k = 0 if t < 2 else LAT
                        dve.wait_ge(na_score, i * per + (N0 + n + 1))
                        if t < 2:
                            s = PS[:, 6 + n % 2, 0:LAT]
                            link(tt(s, s, nabias[:, e, t, :], ALU.add))
                        dve.tensor_reduce(small[:, 32 + n:33 + n], PS[:, 6 + n % 2, k:TOK], AXX, ALU.max, negate=True)\
                            .then_inc(na_max, 1)

                    def outs(n):
                        e, t = n // tiles, n % tiles
                        dve.wait_ge(na_exp, i * per + (N0 + n + 1))
                        link(dve.reciprocal(small[:, 48 + n:49 + n], small[:, 40 + n:41 + n]))
                        dve.wait_ge(na_pv, i * per + (N0 + n + 1))
                        dve.tensor_scalar(tok[:, t, e * HD:(e + 1) * HD], PS[:, 2 + n % 2, 0:HD],
                                          small[:, 48 + n:49 + n], None, ALU.mult).then_inc(na_o, 1)
                    maxes(0)
                    for n in range(per):
                        if n + 1 < per:
                            maxes(n + 1)
                        outs(n)
                    dve.wait_ge(na_fm, i + (Q0 + 1))
                    dve.tensor_scalar(merged2[:, bass.ds(i + HP, 1), 0:T].rearrange("p o n -> p (o n)"),
                                      PS[:, 4, 0:T], 1.0, None, ALU.mult).then_inc(pair_done, 1)
                    loop_end(start, HP)

            def mlp(ph):
                with dve.Fori(0, MC // RING) as i:
                    for j in range(RING):
                        dve.wait_ge(relu_read, i * RING + (ph.at.silu + j + 1))
                        r = sa[:, j % 2, 0:ph.tokens]
                        tt(hidden[:, bass.ds(i * RING + j, 1), 0:ph.tokens].rearrange("p o n -> p (o n)"), r, r,
                           ALU.mult).then_inc(glu_done, 1)

            run = dict(ada=ada, norm=norm, swiglu=swiglu, down=down, mix_in=lambda ph: None, gating=gating,
                       heads=heads, turn=lambda ph: None, gates=gates, pairs=pairs, mlp=mlp)
            for ph in PLAN:
                if ph.kind == "norm" and ph.what in ("q_lat", "kv_lat"):
                    dve.wait_ge(acc_evacuated, ph.at.evac)
                if ph.kind == "norm" and ph.what == "attn":
                    dve.wait_ge(merge_ready, ph.at.merge)
                run[ph.kind](ph)


def unit_fm(w):
    m = w.shape[1] // P
    return w.reshape(DC, P, m, P).transpose(2, 1, 0, 3).reshape(m, P, UNIT)


def unit_tm(w):
    n = w.shape[1]
    return w.reshape(DC * n // UNIT, UNIT // n, P, n).transpose(0, 2, 1, 3).reshape(-1, P, UNIT)


def unit_rows(w):
    return w.reshape(-1, P, UNIT)


def unit_ada(w):
    return w.reshape(DC, P, -1, UNIT).transpose(2, 0, 1, 3).reshape(-1, P, UNIT)


def padded(w, left, width):
    out = np.zeros((w.shape[0], width), np.float32)
    out[:, left:left + w.shape[1]] = w
    return out


def interleaved(w):
    return w.reshape(D, 2, PAIRS, P).transpose(0, 2, 1, 3).reshape(D, 2 * D_FF)


def columns(v, times=1):
    return np.repeat(v.reshape(-1, P).T, times, axis=1)


def rope_tables():
    t = np.arange(LAT)
    row, colm = (t // GRID_W).astype(np.float32), (t % GRID_W).astype(np.float32)
    axis = ROPE // 2
    inv = (1.0 / (10000.0 ** (np.arange(0, axis, 2, dtype=np.float32) / axis))).astype(np.float32)
    ar, ac = row[:, None] * inv, colm[:, None] * inv
    ang = np.concatenate([ar, ar, ac, ac], axis=-1)
    cos1, sin1 = np.ones((P, LAT), np.float32), np.zeros((P, LAT), np.float32)
    cos1[NOPE:QK], sin1[NOPE:QK] = np.cos(ang).T, np.sin(ang).T
    rot1 = np.zeros((P, P), np.float32)
    for a in range(NOPE, QK, axis):
        for j in range(axis // 2):
            rot1[a + axis // 2 + j, a + j] = -1.0
            rot1[a + j, a + axis // 2 + j] = 1.0
    n = HD // 4
    inv2 = (10000.0 ** (-np.arange(n, dtype=np.float32) / n)).astype(np.float32)
    ang2 = np.concatenate([row[:, None] * inv2, colm[:, None] * inv2], axis=-1)
    cos2, sin2 = np.tile(np.cos(ang2).T, (4, 1)), np.tile(np.sin(ang2).T, (4, 1))
    rot2 = np.zeros((P, P), np.float32)
    for a in range(0, P, HD):
        for j in range(HD // 2):
            rot2[a + HD // 2 + j, a + j] = -1.0
            rot2[a + j, a + HD // 2 + j] = 1.0
    return rot1, cos1, sin1, rot2, cos2.astype(np.float32), sin2.astype(np.float32)


def neighbour_bias(rpb):
    t = np.arange(LAT)
    row, colm = t // GRID_W, t % GRID_W
    start = np.clip(colm - 8, 0, GRID_W - 16)
    inside = (colm[None, :] >= start[:, None]) & (colm[None, :] < start[:, None] + 16)
    dr = row[None, :] - row[:, None] + 7
    dc = np.clip(colm[None, :] - colm[:, None] + 15, 0, 30)
    bias = np.where(inside, rpb[:, dr, dc], np.float32(NEG))
    return bias.reshape(HP, 2, 2, P, LAT).transpose(0, 3, 1, 2, 4).reshape(HP, P, 4 * LAT)


def scan_masks():
    m = np.full((P, 2, 4, TOK), np.float32(NEG))
    key = np.arange(LAT)[None, :]
    for t in range(4):
        query = (t % 2) * P + np.arange(P)[:, None]
        own = slice(0, LAT) if t < 2 else slice(LAT, TOK)
        if t < 2:
            m[:, :, t, LAT:TOK] = 0.0
        m[:, 0, t, own] = np.where(key <= query, np.float32(0), np.float32(NEG))
        m[:, 1, t, own] = np.where(key >= query, np.float32(0), np.float32(NEG))
    return m


def layout(x, c, ctx, c_ctx, w_ada, b_ada, g_ffn1, w_ffn1_in, w_ffn1_out, g_mix, w_mix_in, g_q_lat, w_q_up, g_kv_lat,
           w_kv_up, g_q_head, g_k_head, g_sgu, w_spatial, b_spatial, w_conv, g_out, w_mix_out, g_ffn2, w_ffn2_in,
           w_ffn2_out, c_2, ctx_2, c_ctx_2, w_ada_2, b_ada_2, norm1_g_2, w_in_2, b_gate_2, mlstm_norm_g_2, rpb_2,
           w_out_2, norm2_g_2, w_mlp1_2, w_mlp2_2, final_g_2):
    parts = []
    cut = np.cumsum([Q_LORA, KV_LORA, ROPE, 2 * SG])
    for l in range(2):
        q, kv, kpe, sgm, cvm = np.split(w_mix_in[l], cut, axis=1)
        parts += [unit_ada(w_ada[l]), unit_fm(interleaved(w_ffn1_in[l])), unit_rows(w_ffn1_out[l]),
                  unit_fm(q), unit_fm(kv), unit_fm(padded(kpe, NOPE, P)), unit_fm(cvm), unit_fm(sgm[:, :SG]),
                  unit_tm(np.ascontiguousarray(sgm[:, SG:])), unit_rows(w_mix_out[l]),
                  unit_fm(interleaved(w_ffn2_in[l])), unit_rows(w_ffn2_out[l])]
    pair_m, pair_n, na_bias = [], [], []
    q_, k_, v_, o_, nq, nk, nv, gm = range(8)
    for l in range(2):
        w = np.split(w_in_2[l], np.cumsum([512] * 7), axis=1)
        gate = np.zeros((D, P), np.float32)
        for e in range(2):
            for d in range(2):
                gate[:, 64 * e + 32 * d:64 * e + 32 * d + 8] = w[gm][:, 16 * e + 8 * d:16 * e + 8 * d + 8]
        parts += [unit_ada(w_ada_2[l]), unit_fm(gate), unit_rows(w_out_2[l]), unit_fm(w_mlp1_2[l]),
                  unit_rows(w_mlp2_2[l])]
        fm = [unit_fm(a) for a in w[:7]]
        pair_m.append(np.concatenate([fm[j] for j in (q_, k_, v_, o_)], axis=2))
        pair_n.append(np.concatenate([fm[j] for j in (nq, nk, nv)], axis=2))
        na_bias.append(neighbour_bias(rpb_2[l]))
    stream = np.concatenate(parts)

    head_w = np.zeros((2, HEADS, P, HW), np.float32)
    for l in range(2):
        for hd in range(HEADS):
            q = padded(w_q_up[l][:, hd * QK:(hd + 1) * QK], 0, P).reshape(QC, P, P).transpose(1, 0, 2)
            kv = w_kv_up[l][:, hd * P:(hd + 1) * P]
            k = padded(kv[:, :NOPE], 0, P).reshape(KC, P, P).transpose(1, 0, 2)
            v = kv[:, NOPE:].reshape(KC, P, VD).transpose(1, 0, 2)
            head_w[l, hd] = np.concatenate([q.reshape(P, -1), k.reshape(P, -1), v.reshape(P, -1)], axis=1)

    sg_w = np.stack([np.concatenate([
        w_spatial[l].transpose(2, 0, 1).reshape(P, 4 * P),
        np.repeat(b_spatial[l], 64, axis=0).reshape(2, P, P).transpose(1, 0, 2).reshape(P, 2 * P)], axis=1)
        for l in range(2)])

    rot1, cos1, sin1, rot2, cos2, sin2 = rope_tables()
    consts = np.concatenate([np.eye(P, dtype=np.float32), np.ones((P, P), np.float32), rot1, cos1, sin1,
                             rot2, cos2, sin2], axis=1)
    cols = []
    for l in range(2):
        cols += [columns(g_ffn1[l], 2), columns(g_mix[l], 2), columns(g_ffn2[l], 2), columns(g_q_lat[l]),
                 columns(g_kv_lat[l]), padded(g_q_head[l][None], 0, P).T, padded(g_k_head[l][None], 0, P).T,
                 columns(g_sgu[l]), columns(g_out[l]),
                 w_conv[l].reshape(3, 2, P).transpose(2, 1, 0).reshape(P, 6), columns(b_ada[l], 2)]
    for l in range(2):
        bg = np.zeros((P, 2), np.float32)
        for e in range(2):
            for d in range(2):
                bg[32 * d:32 * d + 8, e] = b_gate_2[l, 16 * e + 8 * d:16 * e + 8 * d + 8]
        cols += [columns(norm1_g_2[l], 2), columns(norm2_g_2[l], 2), columns(mlstm_norm_g_2[l]), bg,
                 columns(b_ada_2[l], 2)]
    cols += [columns(final_g_2),
             np.stack([columns(c[0]), columns(c_ctx)], axis=2).reshape(P, 16),
             np.stack([columns(c_2[0]), columns(c_ctx_2)], axis=2).reshape(P, 16)]
    params = np.concatenate(cols, axis=1)
    return dict(pair_m=np.concatenate(pair_m), pair_n=np.concatenate(pair_n), na_bias=np.concatenate(na_bias),
                masks=scan_masks(), stream=stream, head_w=head_w.reshape(2 * HEADS, P, HW), sg_w=sg_w, consts=consts, params=params,
                xT=np.ascontiguousarray(x[0].T), ctxT=np.ascontiguousarray(ctx[0].T),
                ctx2T=np.ascontiguousarray(ctx_2[0].T))


def kernel(**inputs):
    import concourse.bacc as bacc
    from concourse.bass_utils import run_bass_kernel_spmd

    arrays = layout(**{k: np.asarray(v) for k, v in inputs.items()})
    nc = bacc.Bacc("TRN2", target_bir_lowering=False, num_devices=1)
    args = {k: nc.dram_tensor(k, a.shape, F32, kind="ExternalInput").ap() for k, a in arrays.items()}
    out = nc.dram_tensor("outT", (D, LAT), F32, kind="ExternalOutput").ap()
    build(nc, outT=out, **args)
    r = run_bass_kernel_spmd(nc, [arrays], core_ids=[0])
    return np.ascontiguousarray(r.results[0]["outT"].T)[None]
```

```python
from collections import namedtuple
from contextlib import ExitStack

import numpy as np

import concourse.bass as bass
from concourse import mybir

P = 128
D = 1024
DC = D // P
LAT, CTX = 256, 256
TOK = LAT + CTX
HALVES = ((0, LAT, 0), (LAT, TOK, 1))
EPS = 1e-6
GRID_W = 64

D_FF = 2816
PAIRS = D_FF // P
Q_LORA, KV_LORA, ROPE = 384, 256, 32
NOPE, QK, VD = 64, 96, 64
HEADS = 8
SG = 256
CONV = 256
QC, KC = Q_LORA // P, KV_LORA // P
ADA = (9, 9, 6, 6)
ADA_AT = tuple(sum(ADA[:l]) for l in range(4))

D_MLP = 4 * D
MC = D_MLP // P
HD = 64
HP = 4

CREDIT = 1
RING = 8
UNIT = 1024
HW = QC * P + KC * P + KC * VD
NEG = -1.0e30

U_SWIGLU, U_DOWN = 2 * PAIRS, PAIRS
MIX_FM = QC + KC + 1 + 6 + 2
U_MIX = MIX_FM + 2
U_OUT = DC

F32 = mybir.dt.float32
ACT = mybir.ActivationFunctionType
ALU = mybir.AluOpType
AXX = mybir.AxisListType.X

def param_columns():
    at, off = {}, 0
    def put(key, width):
        nonlocal off
        at[key] = (off, width)
        off += width
    for l in range(2):
        for name, width in (("g_ffn1", DC), ("g_mix", DC), ("g_ffn2", DC), ("g_q_lat", QC), ("g_kv_lat", KC),
                            ("g_q_head", 1), ("g_k_head", 1), ("g_sgu", 2), ("g_out", DC), ("w_conv", 6)):
            put((name, l), width)
    for l in range(2, 4):
        for name, width in (("norm1_g", DC), ("norm2_g", DC), ("norm_g", HP), ("b_gate", 2)):
            put((name, l), width)
    put("final_g", DC)
    put("b_ada", sum(ADA) * DC)
    put("cond", DC * 4)
    return at, off


COLS, N_COLS = param_columns()
CONSTS = {}
_off = 0
for _name, _w in (("ident", P), ("ones", P), ("rot1", P), ("cos1", LAT), ("sin1", LAT),
                  ("rot2", P), ("cos2", LAT), ("sin2", LAT), ("ada_sel", 8)):
    CONSTS[_name] = (_off, _w)
    _off += _w
N_CONSTS = _off


COUNTED = ("unit", "acc", "evac", "silu", "glu", "out", "h", "sq", "sum", "std", "rstd", "scaled", "nout", "ada",
           "sg", "head", "headtile", "merge", "gates", "pair", "pairtile")
Counts = namedtuple("Counts", COUNTED)
Phase = namedtuple("Phase", ("kind", "at", "layer", "what", "tokens", "tiles", "blocks", "chunks", "pieces",
                             "shifted", "which", "n", "src", "glu_end", "ada"), defaults=(None,) * 12 + (0,))


class NormSpec:
    pass


def make_plan():
    count = dict.fromkeys(COUNTED, 0)
    count["glu"] = 2
    count["evac"] = 4
    count["ada"] = 1
    count["head"] = 0
    plan = []

    def phase(kind, **more):
        adds = more.pop("adds")
        ph = Phase(kind=kind, at=Counts(**count), **more)
        for key, n in adds.items():
            count[key] += n
        plan.append(ph)
        return ph

    def norm(what, chunks, tokens, pieces, shifted, layer, half=0):
        n = chunks * pieces
        return phase("norm", what=what, chunks=chunks, tokens=tokens, pieces=pieces, shifted=shifted, layer=layer,
                     adds=dict(sq=chunks, sum=1, std=1, rstd=1, scaled=n, nout=n if shifted else 0))

    def swiglu(layer, which, tokens, ada):
        halves = tokens // LAT
        norm(which, DC, tokens, halves, True, layer)
        phase("swiglu", layer=layer, which=which, tokens=tokens, ada=ada,
              adds=dict(unit=U_SWIGLU + ada * DC, acc=U_SWIGLU, silu=PAIRS, glu=PAIRS, ada=ada))
        phase("down", layer=layer, which=which, tokens=tokens, n=U_DOWN, src="hidden", glu_end=count["glu"],
              adds=dict(unit=U_DOWN, out=4 * U_DOWN, h=DC * halves))

    phase("ada", blocks=2, adds=dict(unit=2 * DC, ada=2))
    for l in range(2):
        tokens = TOK if l == 0 else LAT
        halves = tokens // LAT
        tiles = tokens // P
        swiglu(l, "ffn1", TOK, 5)
        norm("mix", DC, TOK, 2, True, l)
        phase("mix_in", layer=l, tokens=tokens, tiles=tiles, ada=2,
              adds=dict(unit=U_MIX + 2 * DC, acc=MIX_FM + tiles, evac=MIX_FM + tiles, ada=2))
        norm("q_lat", QC, tokens, 1, False, l)
        norm("kv_lat", KC, TOK, 1, False, l)
        phase("gating", layer=l, tokens=tokens, tiles=tiles, adds=dict(sg=1))
        phase("heads", layer=l, tokens=tokens, tiles=tiles, adds=dict(head=HEADS, headtile=HEADS * tiles))
        phase("turn", layer=l, tokens=tokens, tiles=tiles, adds=dict(merge=4))
        norm("attn", 4, tokens, 1, False, l)
        norm("sg", 2, tokens, 1, False, l)
        norm("cv", 2, tokens, 1, False, l)
        phase("down", layer=l, which="mix", tokens=tokens, n=U_OUT, src="merged", glu_end=0,
              adds=dict(unit=U_OUT, out=4 * U_OUT, h=DC * halves))
        swiglu(l, "ffn2", tokens, 5)
    for l in range(2, 4):
        tokens = TOK if l == 2 else LAT
        halves, tiles = tokens // LAT, tokens // P
        norm("norm1", DC, TOK, 2, True, l)
        phase("gates", layer=l, adds=dict(unit=1 + 2 * 4, gates=1))
        phase("pairs", layer=l, tokens=tokens, tiles=tiles, adds=dict(pair=HP, pairtile=2 * HP * tiles))
        phase("down", layer=l, which="mix2", tokens=tokens, n=U_OUT, src="merged", glu_end=0,
              adds=dict(unit=U_OUT, out=4 * U_OUT, h=DC * halves))
        norm("norm2", DC, tokens, halves, True, l)
        ada = MC // RING if l == 2 else 0
        phase("mlp", layer=l, tokens=tokens, ada=ada,
              adds=dict(unit=MC + ada * DC, acc=MC, silu=MC, glu=MC, ada=ada))
        phase("down", layer=l, which="mlp", tokens=tokens, n=MC, src="hidden", glu_end=count["glu"],
              adds=dict(unit=MC, out=4 * MC, h=DC * halves))
    norm("final", DC, LAT, 1, False, 4)
    return plan, count


PLAN, TOTAL = make_plan()


def build(nc, stream, head_w, pair_m, pair_n, na_bias, sg_w, masks, consts, params, xT, ctxT, ctx2T, outT):
    units = TOTAL["unit"]
    with ExitStack() as ctx:
        def sb(name, shape):
            return ctx.enter_context(nc.sbuf_tensor(name, shape, F32))

        def sem(name):
            return ctx.enter_context(nc.semaphore(name))

        h = sb("h", [P, DC, TOK])
        xn = sb("xn", [P, DC, TOK])
        ring = sb("ring", [P, RING, UNIT])
        arena = sb("arena", [P, 32, TOK])
        cst = sb("cst", [P, N_CONSTS])
        par = sb("par", [P, N_COLS])
        cond = sb("cond", [P, DC, 32])
        mod = sb("mod", [P, sum(ADA) * DC * 4])
        gain = sb("gain", [P, 16])
        gate = sb("gate", [P, 16])
        eps = sb("eps", [P, 1])
        sa = sb("sa", [P, 2, TOK])
        std = sb("std", [P, TOK])
        rstd = sb("rstd", [P, TOK])
        adarow = sb("adarow", [P, 512])
        mix = sb("mix", [P, 6720])
        mix_at = [0]

        def carve(*shape):
            n = int(np.prod(shape))
            part = mix[:, mix_at[0]:mix_at[0] + n]
            mix_at[0] += n
            if len(shape) == 1:
                return part
            names = "abcd"[:len(shape)]
            return part.rearrange(f"p ({' '.join(names)}) -> p {' '.join(names)}",
                                  **{k: v for k, v in zip(names[1:], shape[1:])})
        qkraw = sb("qkraw", [P, 2, TOK])
        qkn = sb("qkn", [P, 2, TOK])
        qkt = sb("qkt", [P, 2, TOK])
        vtok = sb("vtok", [P, 4, VD])
        probs = sb("probs", [P, 2, TOK])
        probsT = sb("probsT", [P, 2, TOK])
        nmax = sb("nmax", [P, 4])
        rsum = sb("rsum", [P, 4])
        rinv = sb("rinv", [P, 4])
        gqs = sb("gqs", [P, 1])
        small = sb("small", [P, 64])
        headw = carve(HW)
        attn_tok = carve(4, HEADS * VD)
        vpad = carve(4, 4, P)
        sgw = carve(6 * P)
        zc = carve(2, 2, LAT + 2)
        mix_at[0] = 0
        maskt = carve(2, 4, TOK)
        nabias = carve(2, 2, LAT)
        osig = carve(TOK)
        sel = carve(4, P)[0:64]
        tokn = carve(4, P)
        tok = sb("tok", [P, 4, P])
        qkna = sa
        wt0 = sb("wt0", [P, 2, TOK])
        PS = ctx.enter_context(nc.psum_tensor("PS", [P, 8, 512], F32))

        qlat, kvlat = arena[:, 0:3, :], arena[:, 3:5, :]
        cv = arena[:, 5:11, :]
        sgu = arena[:, 11:13, :]
        merged = arena[:, 13:21, :]
        sgv = arena[:, 21:23, :].rearrange("p a (b n) -> p (a b) n", n=SG)
        sgt = arena[:, 23:25, :]
        sq = arena[:, 24:32, :]
        hidden = arena
        merged2 = arena[:, 0:8, :]
        g_a = arena[0:64, 8, :]
        gcol = arena[:, 9, :].rearrange("p (t e d h) -> p t e d h", t=4, e=2, d=2)
        pairw = arena[:, 10:20, :].rearrange("p (j a) n -> p j (a n)", a=2)
        vall = arena[:, 20:28, :].rearrange("p (m t) n -> p m t n", m=2)
        g_soft, g_f, g_b, g_m = (arena[0:64, 28 + j, :] for j in range(4))
        g_guard = g_f

        def const(name):
            o, w = CONSTS[name]
            return cst[:, o:o + w]

        def col(name, l, j=0, w=1):
            o, _ = COLS[(name, l) if l is not None else name]
            return par[:, o + j:o + j + w]

        ident, ones = const("ident"), const("ones")

        weights_in = [sem(f"weights_in{s}") for s in range(RING)]
        weights_used = sem("weights_used")
        params_in = sem("params_in")
        x_in = sem("x_in")
        ctx2_in = sem("ctx2_in")
        sgw_in = sem("sgw_in")
        headw_in = sem("headw_in")
        setup_done = sem("setup_done")
        cond_ready = sem("cond_ready")
        ada_mm = sem("ada_mm")
        ada_row = sem("ada_row")
        ada_turned = sem("ada_turned")
        ada_done = sem("ada_done")
        acc_ready = sem("acc_ready")
        acc_evacuated = sem("acc_evacuated")
        silu_done = sem("silu_done")
        glu_done = sem("glu_done")
        out_ready = sem("out_ready")
        h_ready = sem("h_ready")
        norm_sq = sem("norm_sq")
        norm_sum = sem("norm_sum")
        norm_std = sem("norm_std")
        norm_rstd = sem("norm_rstd")
        norm_scaled = sem("norm_scaled")
        norm_out = sem("norm_out")
        dve_chain = sem("dve_chain")
        act_chain = sem("act_chain")
        sg_var = sem("sg_var")
        sg_std = sem("sg_std")
        sg_v = sem("sg_v")
        sg_mixed = sem("sg_mixed")
        sg_done = sem("sg_done")
        head_qk = sem("head_qk")
        head_v = sem("head_v")
        head_raw = sem("head_raw")
        head_vtok = sem("head_vtok")
        head_sq = sem("head_sq")
        head_ss = sem("head_ss")
        head_std = sem("head_std")
        head_qn = sem("head_qn")
        head_rot = sem("head_rot")
        head_rope = sem("head_rope")
        score_ready = sem("score_ready")
        max_ready = sem("max_ready")
        exp_done = sem("exp_done")
        probs_turned = sem("probs_turned")
        probsT_ready = sem("probsT_ready")
        pv_ready = sem("pv_ready")
        attn_done = sem("attn_done")
        attn_turned = sem("attn_turned")
        merge_ready = sem("merge_ready")
        out_done = sem("out_done")
        relu_read = silu_done
        masks_in = sem("masks_in")
        pairm_in = sem("pairm_in")
        pairn_in = sem("pairn_in")
        bias_in = sem("bias_in")
        gate_mm = sem("gate_mm")
        gate_softplus = sem("gate_softplus")
        gate_rows = sem("gate_rows")
        gate_guard = sem("gate_guard")
        gate_turned = sem("gate_turned")
        gate_cols = sem("gate_cols")
        v_acc = sem("v_acc")
        v_copied = sem("v_copied")
        pm_acc = sem("pm_acc")
        pm_copied = sem("pm_copied")
        pm_rot = sem("pm_rot")
        pm_rope = sem("pm_rope")
        pm_sel = sem("pm_sel")
        pm_arow = sem("pm_arow")
        pm_score = sem("pm_score")
        pm_logw = sem("pm_logw")
        pm_w = sem("pm_w")
        pm_p = sem("pm_p")
        pm_turned = sem("pm_turned")
        pm_pT = sem("pm_pT")
        pm_pv = sem("pm_pv")
        pm_o = sem("pm_o")
        pm_var = sem("pm_var")
        pm_std = sem("pm_std")
        pm_normed = sem("pm_normed")
        pm_final = sem("pm_final")
        pm_fm = sem("pm_fm")
        na_acc = sem("na_acc")
        na_copied = sem("na_copied")
        na_score = sem("na_score")
        na_max = sem("na_max")
        na_exp = sem("na_exp")
        na_turned = sem("na_turned")
        na_pT = sem("na_pT")
        na_pv = sem("na_pv")
        na_o = sem("na_o")
        na_fm = sem("na_fm")
        pair_done = sem("pair_done")

        def mod_of(l, v):
            at = (ADA_AT[l] + v) * DC * 4
            pair = slice(0, 2) if l < 2 else slice(2, 4)
            return mod[:, at:at + DC * 4].rearrange("p (c j) -> p c j", j=4)[:, :, pair]

        def norm_spec(ph):
            l = ph.layer
            s = NormSpec()
            s.dim = ph.chunks * P
            pieces = HALVES[:ph.pieces] if ph.pieces == ph.tokens // LAT and ph.shifted else ((0, ph.tokens, 0),)
            s.pieces = pieces
            if ph.shifted:
                s.src = h
                s.dst = xn
                s.bank = out_bank(0)
                k = {"ffn1": 0, "mix": 1, "ffn2": 2, "norm1": 0, "norm2": 1}[ph.what]
                s.scale = mod_of(l, 3 * k + 1)
                s.blocks = ADA_AT[l] + 3 * k + 2
                s.g = col({"ffn1": "g_ffn1", "mix": "g_mix", "ffn2": "g_ffn2", "norm1": "norm1_g",
                           "norm2": "norm2_g"}[ph.what], l, 0, DC)
                s.gain = lambda c, cnd: gain[:, 2 * c + cnd:2 * c + cnd + 1]
                s.shift = lambda c, cnd: mod_of(l, 3 * k)[:, c, cnd:cnd + 1]
            elif ph.what == "final":
                s.src, s.dst, s.bank = h, xn, out_bank(0)
                s.gain = lambda c, cnd: col("final_g", None, c)
            else:
                src, name, j, s.bank = {"q_lat": (qlat, "g_q_lat", 0, 0), "kv_lat": (kvlat, "g_kv_lat", 0, 1),
                                        "attn": (merged[:, 0:4, :], "g_out", 0, 4),
                                        "sg": (merged[:, 4:6, :], "g_out", 4, 5),
                                        "cv": (merged[:, 6:8, :], "g_out", 6, 6)}[ph.what]
                s.src = s.dst = src
                s.gain = lambda c, cnd: col(name, l, j + c)
            return s

        def out_bank(m):
            return (m + 4) % 8

        def h_wait(eng, ph, c):
            if ph.at.h == 0:
                eng.wait_ge(x_in, 32)
            else:
                last = last_down(ph)
                eng.wait_ge(h_ready, last.at.h + (c + 1) * (last.tokens // LAT))
                if ph.layer == 2:
                    eng.wait_ge(ctx2_in, 16)

        def last_down(ph):
            return [q for q in PLAN[:PLAN.index(ph)] if q.kind == "down"][-1]

        block = ctx.enter_context(nc.Block())

        @block.sync
        def _(sp):
            for u in range(RING):
                sp.dma_start(ring[:, u, :], stream[u]).then_inc(weights_in[u], 16)
            whole = units // RING
            with sp.Fori(1, whole) as i:
                for s in range(RING):
                    sp.wait_ge(weights_used, i * RING + (s - RING + 2))
                    sp.dma_start(ring[:, s, :], stream[bass.ds(i * RING + s, 1)].rearrange("o p n -> p (o n)"))\
                        .then_inc(weights_in[s], 16)
            for u in range(whole * RING, units):
                sp.wait_ge(weights_used, u - RING + 2)
                sp.dma_start(ring[:, u % RING, :], stream[u]).then_inc(weights_in[u % RING], 16)
            for c in range(DC):
                sp.wait_ge(norm_scaled, TOTAL["scaled"] - DC + c + 1)
                sp.dma_start(outT[c * P:(c + 1) * P, :], xn[:, c, 0:LAT]).then_inc(out_done, 16)
            sp.wait_ge(out_done, 16 * DC)

        @block.gpsimd
        def _(pool):
            pool.dma_start(sgw[:, :], sg_w[0]).then_inc(sgw_in, 16)
            for ph in PLAN:
                if ph.kind == "gating" and ph.layer == 1:
                    pool.wait_ge(sg_done, ph.at.sg)
                    pool.dma_start(sgw[:, :], sg_w[1]).then_inc(sgw_in, 16)
                if ph.kind == "heads":
                    with pool.Fori(0, HEADS) as i:
                        pool.wait_ge(head_v, i + (ph.at.head + CREDIT))
                        pool.dma_start(headw[:, :], head_w[bass.ds(i + ph.at.head, 1)]
                                       .rearrange("o p n -> p (o n)")).then_inc(headw_in, 16)
                if ph.kind == "norm" and ph.what == "q_lat" and ph.layer == 1:
                    pool.wait_ge(norm_scaled, ph.at.scaled)
                    pool.dma_start(h[:, :, LAT:TOK], ctx2T.rearrange("(c p) t -> p c t", p=P)).then_inc(ctx2_in, 16)
                if ph.kind == "norm" and ph.what == "norm1" and ph.layer == 2:
                    pool.wait_ge(h_ready, ph.at.h)
                    pool.dma_start(maskt[:, :, :, :], masks).then_inc(masks_in, 16)
                if ph.kind == "pairs":
                    Q0 = ph.at.pair
                    pool.wait_ge(norm_sum, ph.at.sum)
                    with pool.Fori(0, HP) as i:
                        pool.wait_ge(pm_acc, i * 3 + (3 * Q0 + CREDIT))
                        pool.dma_start(pairw[:, 0:3, :].rearrange("p j n -> p (j n)"),
                                       pair_m[bass.ds(i + Q0, 1)].rearrange("o p n -> p (o n)")).then_inc(pairm_in, 16)
                        pool.wait_ge(na_acc, i * 2 + (2 * Q0 + CREDIT))
                        pool.dma_start(pairw[:, 3:5, :].rearrange("p j n -> p (j n)"),
                                       pair_n[bass.ds(i + Q0, 1)].rearrange("o p n -> p (o n)")).then_inc(pairn_in, 16)
                        pool.wait_ge(pair_done, i + (Q0 + CREDIT))
                        pool.dma_start(nabias.rearrange("p a b n -> p (a b n)"),
                                       na_bias[bass.ds(i + Q0, 1)].rearrange("o p n -> p (o n)")).then_inc(bias_in, 16)

        @block.tensor
        def _(pe):
            def unit_in(u0, j, i=0, rounds=1):
                u = u0 + j
                pe.wait_ge(weights_in[u % RING], i * (16 * rounds) + 16 * (u // RING + 1))
                return u % RING

            def ada_units(ph, block, j, k, i=0, rounds=1):
                if k == 0:
                    pe.wait_ge(ada_row, i + (ph.at.ada + block))
                for kk in range(2):
                    s = unit_in(ph.at.unit, j + kk, i, rounds)
                    for half in range(2):
                        q = 32 * (2 * kk + half)
                        m = pe.matmul(PS[q:q + 32, 5, :], cond[:, k + kk, :], ring[:, s, half * 512:half * 512 + 512],
                                      start=k == 0, stop=k == DC - 2)
                        if half == 0:
                            m.then_inc(weights_used, 1)
                if k == DC - 2:
                    m.then_inc(ada_mm, 1)

            def ada_turn(ph, block, i=0):
                pe.wait_ge(ada_done, i + (ph.at.ada + block))
                pe.wait_ge(ada_row, i + (ph.at.ada + block + 1))
                for c in range(4):
                    m = pe.matmul(PS[:, 6, 8 * c:8 * c + 8], adarow[:, c * P:(c + 1) * P], const("ada_sel"),
                                  start=True, stop=True)
                m.then_inc(ada_turned, 1)

            def ada(ph):
                with pe.Fori(0, ph.blocks) as i:
                    for k in range(0, DC, 2):
                        ada_units(ph, 0, k, k, i)
                    ada_turn(ph, 0, i)

            def norm(ph):
                s = norm_spec(ph)
                if ph.at.std:
                    pe.wait_ge(norm_std, ph.at.std)
                for c in range(ph.chunks):
                    pe.wait_ge(norm_sq, ph.at.sq + c + 1)
                    m = pe.matmul(PS[:, s.bank, 0:ph.tokens], ones, sq[:, c, 0:ph.tokens],
                                  start=c == 0, stop=c == ph.chunks - 1)
                m.then_inc(norm_sum, 1)

            def fm_unit(s, bank, tokens):
                for k in range(DC):
                    m = pe.matmul(PS[:, bank, 0:tokens], ring[:, s, k * P:(k + 1) * P], xn[:, k, 0:tokens],
                                  start=k == 0, stop=k == DC - 1)
                    if k == 0:
                        m.then_inc(weights_used, 1)
                m.then_inc(acc_ready, 1)

            def swiglu(ph):
                pe.wait_ge(norm_out, ph.at.nout)
                head = U_SWIGLU % RING

                def pair(i, j, at, rounds=1, between=None):
                    pe.wait_ge(glu_done, i * (RING // 2) + (ph.at.glu + j - 1))
                    for e in range(2):
                        s = unit_in(ph.at.unit, at + e, i, rounds)
                        fm_unit(s, 2 * (j % 2) + e, ph.tokens)
                        if e == 0 and between:
                            between()
                for j in range(head // 2):
                    pair(0, j, 2 * j)
                with pe.Fori(0, ph.ada) as i:
                    pair(i, head // 2, head, 2)
                    ada_units(ph, 0, head + 2, 0, i, 2)
                    pair(i, head // 2 + 1, head + 4, 2)
                    ada_units(ph, 0, head + 6, 2, i, 2)
                    pair(i, head // 2 + 2, head + 8, 2)
                    ada_units(ph, 0, head + 10, 4, i, 2)
                    ada_units(ph, 0, head + 12, 6, i, 2)
                    pair(i, head // 2 + 3, head + 14, 2, between=lambda: ada_turn(ph, 0, i))

            def down(ph):
                src = hidden if ph.src == "hidden" else merged if ph.layer < 2 else merged2
                head = ph.n % RING or RING

                def rows(i, k):
                    s = unit_in(ph.at.unit, k, i)
                    if ph.src == "hidden":
                        pe.wait_ge(glu_done, i * RING + (ph.glu_end - ph.n + k + 1))
                    for m_ in range(DC):
                        if ph.src == "hidden" and isinstance(i, int) and k == 0 and m_ == 1:
                            pe.wait_ge(ada_done, ph.at.ada)
                        if ph.src == "hidden" and isinstance(i, int) and k == 0 and m_ == 4:
                            pe.wait_ge(glu_done, ph.glu_end)
                        rhs = src[:, k, 0:ph.tokens] if isinstance(i, int) else \
                            src[:, bass.ds(i * RING + k, 1), 0:ph.tokens].rearrange("p o n -> p (o n)")
                        m = pe.matmul(PS[:, out_bank(m_), 0:ph.tokens], ring[:, s, m_ * P:(m_ + 1) * P], rhs,
                                      start=isinstance(i, int) and k == 0, stop=True, skip_group_check=True)
                        if m_ == 0:
                            m.then_inc(weights_used, 1)
                        if m_ % 2:
                            m.then_inc(out_ready, 1)
                if ph.src == "merged":
                    pe.wait_ge(norm_scaled, ph.at.scaled)
                    if ph.layer >= 2:
                        pe.wait_ge(pair_done, ph.at.pair + CREDIT)
                for k in range(head):
                    rows(0, k)
                if ph.n > head:
                    with pe.Fori(0, (ph.n - head) // RING) as i:
                        for k in range(RING):
                            rows(i, head + k)

            def mix_in(ph):
                pe.wait_ge(norm_out, ph.at.nout)
                at = 0
                for j in range(MIX_FM):
                    pe.wait_ge(acc_evacuated, ph.at.evac + j - 3)
                    s = unit_in(ph.at.unit, at)
                    at += 1
                    fm_unit(s, j % 4, TOK if QC <= j <= QC + KC else ph.tokens)
                    if j < DC:
                        ada_units(ph, j // 4, at, 2 * (j % 4))
                        at += 2
                    if j in (4, 9):
                        ada_turn(ph, j // 5)
                s = [unit_in(ph.at.unit, at + e) for e in range(2)]
                for t in range(ph.tiles):
                    j = MIX_FM + t
                    pe.wait_ge(acc_evacuated, ph.at.evac + j - 3)
                    for k in range(DC):
                        m = pe.matmul(PS[:, j % 4, 0:SG], xn[:, k, t * P:(t + 1) * P],
                                      ring[:, s[k // 4], (k % 4) * SG:(k % 4 + 1) * SG],
                                      start=k == 0, stop=k == DC - 1)
                        if (t, k) in ((0, 0), (ph.tiles - 1, 4)):
                            m.then_inc(weights_used, 1)
                    m.then_inc(acc_ready, 1)

            def gating(ph):
                pe.wait_ge(sgw_in, 16 * (ph.at.sg + 1))
                pe.wait_ge(sg_v, ph.at.sg + 1)
                for t in range(ph.tiles):
                    for cb in range(2):
                        for e in range(2):
                            g = 2 * cb + e
                            m = pe.matmul(PS[:, 5 + cb, t * P:(t + 1) * P], vpad[:, t, g, :],
                                          sgw[:, g * P:(g + 1) * P], start=e == 0, stop=e == 1)
                m.then_inc(sg_mixed, 1)

            def heads(ph):
                tiles, H0, T0 = ph.tiles, ph.at.head, ph.at.headtile
                pe.wait_ge(norm_scaled, ph.at.scaled)
                with pe.Fori(0, HEADS) as i:
                    pe.wait_ge(headw_in, i * 16 + 16 * (H0 + 1))
                    pe.wait_ge(sg_done, ph.at.sg)
                    pe.wait_ge(attn_done, i * tiles + (T0 + CREDIT))
                    for k in range(QC):
                        m = pe.matmul(PS[:, 0, 0:ph.tokens], headw[:, k * P:(k + 1) * P], qlat[:, k, 0:ph.tokens],
                                      start=k == 0, stop=k == QC - 1)
                    m.then_inc(head_qk, 1)
                    for k in range(KC):
                        m = pe.matmul(PS[:, 1, :], headw[:, (QC + k) * P:(QC + k + 1) * P], kvlat[:, k, :],
                                      start=k == 0, stop=k == KC - 1)
                    m.then_inc(head_qk, 1)
                    for t in range(4):
                        for k in range(KC):
                            o = (QC + KC) * P + k * VD
                            m = pe.matmul(PS[:, 2, t * VD:(t + 1) * VD], kvlat[:, k, t * P:(t + 1) * P],
                                          headw[:, o:o + VD], start=k == 0, stop=k == KC - 1)
                    m.then_inc(head_v, 1)
                    pe.wait_ge(head_sq, i * 2 + (2 * H0 + 1))
                    pe.matmul(PS[:, 3, 0:ph.tokens], ones, qkt[:, 0, 0:ph.tokens], start=True, stop=True)
                    pe.wait_ge(head_sq, i * 2 + (2 * H0 + 2))
                    pe.matmul(PS[:, 4, :], ones, qkt[:, 1, :], start=True, stop=True).then_inc(head_ss, 1)
                    pe.wait_ge(head_qn, i * 2 + (2 * H0 + 2))
                    for e in range(2):
                        m = pe.matmul(PS[:, e, 0:LAT], const("rot1"), qkn[:, e, 0:LAT], start=True, stop=True)
                    m.then_inc(head_rot, 1)
                    pe.wait_ge(head_rope, i + (H0 + 1))

                    def scores(t):
                        keys = 0 if t < 2 else LAT
                        if t >= 2:
                            pe.wait_ge(exp_done, i * tiles + (T0 + t - 1))
                        pe.matmul(PS[:, 5 + t % 2, keys:TOK], qkn[:, 0, t * P:(t + 1) * P], qkn[:, 1, keys:TOK],
                                  start=True, stop=True).then_inc(score_ready, 1)

                    def values(t):
                        k0 = 0 if t < 2 else 2
                        bank = 7 if t % 2 == 0 else 3
                        pe.wait_ge(exp_done, i * tiles + (T0 + t + 1))
                        if t >= 2:
                            pe.wait_ge(probsT_ready, i * tiles + (T0 + t - 1))
                        for k in range(k0, 4):
                            m = pe.transpose(PS[:, bank, k * P:(k + 1) * P], probs[:, t % 2, k * P:(k + 1) * P], ident)
                        m.then_inc(probs_turned, 1)
                        pe.wait_ge(probsT_ready, i * tiles + (T0 + t + 1))
                        if t == 0:
                            pe.wait_ge(head_vtok, i + (H0 + 1))
                        if t >= 2:
                            pe.wait_ge(attn_done, i * tiles + (T0 + t - 1 + CREDIT))
                        for k in range(k0, 4):
                            m = pe.matmul(PS[:, 4 - 2 * (t % 2), 0:VD], probsT[:, t % 2, k * P:(k + 1) * P],
                                          vtok[:, k, :], start=k == k0, stop=k == 3)
                        m.then_inc(pv_ready, 1)
                    scores(0)
                    for t in range(1, tiles + 1):
                        if t < tiles:
                            scores(t)
                        values(t - 1)

            def turn(ph):
                pe.wait_ge(attn_done, ph.at.headtile + CREDIT)
                for c in range(4):
                    for t in range(ph.tiles):
                        m = pe.transpose(PS[:, c, t * P:(t + 1) * P], attn_tok[:, t, c * P:(c + 1) * P], ident)
                    m.then_inc(attn_turned, 1)

            def gates(ph):
                pe.wait_ge(norm_out, ph.at.nout)
                s = unit_in(ph.at.unit, 0)
                for e in range(2):
                    for k in range(DC):
                        m = pe.matmul(PS[0:64, e, :], ring[:, s, k * P + 64 * e:k * P + 64 * e + 64], xn[:, k, :],
                                      start=k == 0, stop=k == DC - 1)
                        if e == 0 and k == 0:
                            m.then_inc(weights_used, 1)
                    if k:
                        m.then_inc(gate_mm, 1)
                for mixer in range(2):
                    for u in range(4):
                        s = unit_in(ph.at.unit, 1 + 4 * mixer + u)
                        for t in range(4):
                            if mixer and u == 0:
                                pe.wait_ge(v_copied, 8 * ph.at.gates + t + 1)
                            for k in range(2):
                                m = pe.matmul(PS[:, 4 + t, :], xn[:, 2 * u + k, t * P:(t + 1) * P],
                                              ring[:, s, k * 512:(k + 1) * 512], start=u == 0 and k == 0,
                                              stop=u == 3 and k == 1)
                                if t == 0 and k == 0:
                                    m.then_inc(weights_used, 1)
                            if u == 3:
                                m.then_inc(v_acc, 1)

            def pair_product(ph, j, k, bank, tokens, weights):
                return pe.matmul(PS[:, bank, 0:tokens], pairw[:, weights, k * P:(k + 1) * P], xn[:, k, 0:tokens],
                                 start=k == 0, stop=k == DC - 1)

            def mlstm_products(ph, p, a, b):
                Q = ph.at.pair
                for x in range(a, b):
                    j, k = x // DC, x % DC
                    if x == 0:
                        pe.wait_ge(pairm_in, p * 16 + 16 * (Q + 1))
                    if x == 2 * DC:
                        pe.wait_ge(pm_copied, p * 3 + (3 * Q + 1))
                    if x == 21:
                        pe.wait_ge(pm_copied, p * 3 + (3 * Q + 2))
                        for e in range(2):
                            m = pe.matmul(PS[:, 3, e * LAT:(e + 1) * LAT], const("rot2"), qkraw[:, e, 0:LAT],
                                          start=True, stop=True)
                        m.then_inc(pm_rot, 1)
                    m = pair_product(ph, j, k, 2 + j % 2, TOK if j == 1 else ph.tokens, j)
                    if k == DC - 1:
                        m.then_inc(pm_acc, 1)

            def neighbour_products(ph, p, a, b):
                Q = ph.at.pair
                for x in range(a, b):
                    j, k = x // DC, x % DC
                    if x == 0:
                        pe.wait_ge(pairn_in, p * 16 + 16 * (Q + 1))
                        pe.wait_ge(pm_copied, p * 3 + (3 * Q + 3))
                    m = pair_product(ph, j, k, 2 + j, TOK if j else ph.tokens, 3 + j)
                    if k == DC - 1:
                        m.then_inc(na_acc, 1)

            def pairs(ph):
                tiles, Q0, N0, per = ph.tiles, ph.at.pair, ph.at.pairtile, 2 * ph.tiles
                pe.wait_ge(v_copied, 8 * ph.at.gates)
                mlstm_products(ph, 0, 0, 3 * DC)
                pe.wait_ge(gate_guard, ph.at.gates)
                for t in range(4):
                    for e, g in enumerate((g_m, g_guard)):
                        m = pe.transpose(PS[:, 0, (2 * t + e) * 64:(2 * t + e + 1) * 64], g[:, t * P:(t + 1) * P],
                                         ident[0:64, 0:64])
                m.then_inc(gate_turned, 1)

                def arow(p, e):
                    for d in range(2):
                        m = pe.matmul(PS[:, 4 + d, :], sel[:, 2 * d + e, :], g_a, start=True, stop=True)
                    m.then_inc(pm_arow, 1)

                def score(i, n, qk, free, ready):
                    e, t = n // tiles, n % tiles
                    keys = 0 if t < 2 else LAT
                    if n >= 2:
                        pe.wait_ge(free, i * per + (N0 + n - 1))
                    r = slice(64 * e, 64 * e + 64)
                    pe.matmul(PS[:, 6 + n % 2, keys:TOK], qk[r, 0, t * P:(t + 1) * P], qk[r, 1, keys:TOK],
                              start=True, stop=True).then_inc(ready, 1)

                def turned(i, n, made, copied, turned_):
                    k0 = 0 if n % tiles < 2 else 2
                    pe.wait_ge(made, i * per + (N0 + n + 1))
                    if n >= 1:
                        pe.wait_ge(copied, i * per + (N0 + n))
                    for k in range(k0, 4):
                        m = pe.transpose(PS[:, 0, k * P:(k + 1) * P], probs[:, n % 2, k * P:(k + 1) * P], ident)
                    m.then_inc(turned_, 1)

                def value(i, n, mixer, copied, left, pv):
                    e, k0 = n // tiles, 0 if n % tiles < 2 else 2
                    if n >= 1:
                        pe.wait_ge(left, i * per + (N0 + n))
                    pe.wait_ge(copied, i * per + (N0 + n + 1))
                    for k in range(k0, 4):
                        m = pe.matmul(PS[:, 1, 0:HD], probsT[:, n % 2, k * P:(k + 1) * P],
                                      vall[:, mixer, k, bass.ds(i * P + e * HD, HD)], start=k == k0, stop=k == 3)
                    m.then_inc(pv, 1)

                def turn_tok(src, bank, sem_):
                    for t in range(tiles):
                        m = pe.transpose(PS[:, bank, t * P:(t + 1) * P], src[:, t, :], ident)
                    m.then_inc(sem_, 1)

                def iteration(i, last):
                    pe.wait_ge(pair_done, i + (Q0 + CREDIT))
                    pe.wait_ge(pm_rope, i + (Q0 + 1))
                    step = 2 * DC // per
                    score(i, 0, qkraw, pm_p, pm_score)
                    for n in range(per):
                        if n + 1 < per:
                            score(i, n + 1, qkraw, pm_p, pm_score)
                        if n + 1 == tiles:
                            pe.wait_ge(pm_logw, i * per + (N0 + tiles))
                            arow(i, 1)
                        neighbour_products(ph, i, n * step, n * step + step // 2)
                        turned(i, n, pm_p, pm_pT, pm_turned)
                        neighbour_products(ph, i, n * step + step // 2, (n + 1) * step)
                        value(i, n, 0, pm_pT, pm_o, pm_pv)
                    step = 3 * DC // per
                    pe.wait_ge(na_copied, i * 2 + (2 * Q0 + 2))
                    score(i, 0, qkna, na_exp, na_score)
                    for n in range(per):
                        if n + 1 < per:
                            score(i, n + 1, qkna, na_exp, na_score)
                        if not last:
                            mlstm_products(ph, i + 1, n * step, n * step + step // 2)
                        turned(i, n, na_exp, na_pT, na_turned)
                        if not last:
                            mlstm_products(ph, i + 1, n * step + step // 2, (n + 1) * step)
                        if n == 0:
                            pe.wait_ge(pm_o, i * per + (N0 + per))
                        value(i, n, 1, na_pT, na_o, na_pv)
                        if n == 1:
                            pe.wait_ge(pm_normed, i + (Q0 + 1))
                            turn_tok(tok, 4, pm_fm)
                    if not last:
                        pe.wait_ge(pm_sel, i + (Q0 + 2))
                        pe.wait_ge(pm_final, i + (Q0 + 1))
                        arow(i + 1, 0)
                    pe.wait_ge(na_o, i * per + (N0 + per))
                    turn_tok(tokn, 0, na_fm)

                pe.wait_ge(pm_sel, Q0 + 1)
                arow(0, 0)
                pe.wait_ge(gate_cols, 2 * ph.at.gates)
                with pe.Fori(0, HP - 1) as i:
                    iteration(i, False)
                iteration(HP - 1, True)

            def mlp(ph):
                pe.wait_ge(norm_out, ph.at.nout)
                rounds = 2 if ph.ada else 1
                with pe.Fori(0, MC // RING) as i:
                    at = 0
                    for j in range(RING):
                        pe.wait_ge(relu_read, i * RING + (ph.at.silu + j - 3))
                        s = unit_in(ph.at.unit, at, i, rounds)
                        at += 1
                        fm_unit(s, j % 4, ph.tokens)
                        if ph.ada and j < 4:
                            ada_units(ph, 0, at, 2 * j, i, 2)
                            at += 2
                        if ph.ada and j == 5:
                            ada_turn(ph, 0, i)

            pe.wait_ge(setup_done, 1)
            pe.wait_ge(params_in, 32)
            pe.wait_ge(cond_ready, 1)
            run = dict(ada=ada, norm=norm, swiglu=swiglu, down=down, mix_in=mix_in, gating=gating, heads=heads,
                       turn=turn, gates=gates, pairs=pairs, mlp=mlp)
            for ph in PLAN:
                run[ph.kind](ph)

        @block.scalar
        def _(act):
            chain = [0]

            def link(ins):
                chain[0] += 1
                ins.then_inc(act_chain, 1)
                act.wait_ge(act_chain, chain[0])

            act.dma_start(cst[:, :], consts).then_inc(params_in, 16)
            act.dma_start(par[:, :], params).then_inc(params_in, 16)
            act.dma_start(h[:, :, 0:LAT], xT.rearrange("(c p) t -> p c t", p=P)).then_inc(x_in, 16)
            act.dma_start(h[:, :, LAT:TOK], ctxT.rearrange("(c p) t -> p c t", p=P)).then_inc(x_in, 16)
            act.wait_ge(params_in, 32)
            act.wait_ge(setup_done, 1)
            act.activation(cond[:, :, 0:4], col("cond", None, 0, 4 * DC).rearrange("p (c j) -> p c j", j=4),
                           ACT.Silu).then_inc(cond_ready, 1)

            def ada_copy(ph, block, i=0):
                act.wait_ge(ada_mm, i + (ph.at.ada + block))
                act.activation(adarow[:, :], PS[:, 5, :], ACT.Copy).then_inc(ada_row, 1)

            def ada(ph):
                with act.Fori(0, ph.blocks) as i:
                    ada_copy(ph, 0, i)

            def norm(ph):
                s = norm_spec(ph)
                if ph.at.sum:
                    act.wait_ge(norm_sum, ph.at.sum)
                halves = ph.tokens // LAT
                for c in range(ph.chunks):
                    if s.src is h:
                        h_wait(act, ph, c)
                    elif ph.what == "sg" or ph.what == "cv":
                        act.wait_ge(sg_done, ph.at.sg)
                    act.activation(sq[:, c, 0:ph.tokens], s.src[:, c, 0:ph.tokens], ACT.Square).then_inc(norm_sq, 1)
                act.wait_ge(norm_sum, ph.at.sum + 1)
                if ph.at.rstd:
                    act.wait_ge(norm_rstd, ph.at.rstd)
                act.activation(std[:, 0:ph.tokens], PS[:, s.bank, 0:ph.tokens], ACT.Sqrt, bias=eps[:, :],
                               scale=1.0 / s.dim).then_inc(norm_std, 1)
                if ph.shifted:
                    n = 0
                    for c in range(ph.chunks):
                        for a, b, cnd in s.pieces:
                            n += 1
                            act.wait_ge(norm_scaled, ph.at.scaled + n)
                            act.activation(s.dst[:, c, a:b], s.dst[:, c, a:b], ACT.Identity, bias=s.shift(c, cnd))\
                                .then_inc(norm_out, 1)

            def swiglu(ph):
                head = U_SWIGLU % RING // 2

                def pair(i, j):
                    act.wait_ge(acc_ready, i * RING + (ph.at.acc + 2 * j + 1))
                    act.wait_ge(glu_done, i * (RING // 2) + (ph.at.glu + j - 1))
                    act.activation(sa[:, j % 2, 0:ph.tokens], PS[:, 2 * (j % 2), 0:ph.tokens], ACT.Silu)\
                        .then_inc(silu_done, 1)
                for j in range(head):
                    pair(0, j)
                with act.Fori(0, U_SWIGLU // RING) as i:
                    for j in range(RING // 2):
                        if j == 3:
                            ada_copy(ph, 0, i)
                        pair(i, head + j)

            def mlp(ph):
                with act.Fori(0, MC // RING) as i:
                    for j in range(RING):
                        act.wait_ge(acc_ready, i * RING + (ph.at.acc + j + 1))
                        act.wait_ge(glu_done, i * RING + (ph.at.glu + j - 1))
                        act.activation(sa[:, j % 2, 0:ph.tokens], PS[:, j % 4, 0:ph.tokens], ACT.Relu)\
                            .then_inc(relu_read, 1)
                        if ph.ada and j == 3:
                            ada_copy(ph, 0, i)

            def mix_in(ph):
                for j in range(MIX_FM + ph.tiles):
                    if j in (4, 8):
                        ada_copy(ph, j // 4 - 1)
                    act.wait_ge(acc_ready, ph.at.acc + j + 1)
                    bank = PS[:, j % 4, :]
                    if j < QC + KC:
                        n = ph.tokens if j < QC else TOK
                        ins = act.activation(arena[:, j, 0:n], bank[:, 0:n], ACT.Copy)
                    elif j == QC + KC:
                        ins = act.activation(qkraw[64:128, 1, :], bank[64:128, :], ACT.Copy)
                    elif j < MIX_FM - 2:
                        ins = act.activation(arena[:, j - 1, 0:ph.tokens], bank[:, 0:ph.tokens], ACT.Copy)
                    elif j < MIX_FM:
                        ins = act.activation(arena[:, j - 1, 0:ph.tokens], bank[:, 0:ph.tokens],
                                             ACT.Gelu_apprx_tanh)
                    else:
                        ins = act.activation(sgv[:, j - MIX_FM, :], bank[:, 0:SG], ACT.Gelu_apprx_tanh)
                    ins.then_inc(acc_evacuated, 1)

            def gating(ph):
                act.wait_ge(sg_var, ph.at.sg + 1)
                act.activation(sgt[:, 1, 0:4 * ph.tiles], sgt[:, 1, 32:32 + 4 * ph.tiles], ACT.Sqrt, bias=eps[:, :],
                               scale=1.0 / 64).then_inc(sg_std, 1)

            def heads(ph):
                tiles, H0, T0 = ph.tiles, ph.at.head, ph.at.headtile
                with act.Fori(0, HEADS) as i:
                    act.wait_ge(head_qk, i * 2 + (2 * H0 + 1))
                    act.activation(qkraw[:, 0, 0:ph.tokens], PS[:, 0, 0:ph.tokens], ACT.Copy).then_inc(head_raw, 1)
                    act.wait_ge(head_qk, i * 2 + (2 * H0 + 2))
                    act.activation(qkraw[0:64, 1, :], PS[0:64, 1, :], ACT.Copy).then_inc(head_raw, 1)
                    act.wait_ge(head_raw, i * 2 + (2 * H0 + 1))
                    act.activation(qkt[:, 0, 0:ph.tokens], qkraw[:, 0, 0:ph.tokens], ACT.Square).then_inc(head_sq, 1)
                    act.wait_ge(head_raw, i * 2 + (2 * H0 + 2))
                    act.activation(qkt[:, 1, :], qkraw[:, 1, :], ACT.Square).then_inc(head_sq, 1)
                    act.wait_ge(head_v, i + (H0 + 1 + CREDIT))
                    act.activation(vtok[:, :, :].rearrange("p t d -> p (t d)"), PS[:, 2, 0:4 * VD], ACT.Copy)\
                        .then_inc(head_vtok, 1)
                    act.wait_ge(head_ss, i + (H0 + 1))
                    act.activation(probsT[:, 0, 0:ph.tokens], PS[:, 3, 0:ph.tokens], ACT.Sqrt, bias=eps[:, :],
                                   scale=1.0 / QK).then_inc(head_std, 1)
                    act.activation(probsT[:, 1, :], PS[:, 4, :], ACT.Sqrt, bias=eps[:, :],
                                   scale=1.0 / QK).then_inc(head_std, 1)

                    def exps(t):
                        k = 0 if t < 2 else LAT
                        act.wait_ge(max_ready, i * tiles + (T0 + t + 1))
                        if t >= 2:
                            act.wait_ge(probs_turned, i * tiles + (T0 + t - 1))
                        act.activation(probs[:, t % 2, k:TOK], PS[:, 5 + t % 2, k:TOK], ACT.Exp,
                                       bias=nmax[:, t:t + 1], accum_out=rsum[:, t:t + 1]).then_inc(exp_done, 1)

                    def turned(t):
                        k = 0 if t < 2 else LAT
                        act.wait_ge(probs_turned, i * tiles + (T0 + t + 1))
                        if t >= 2:
                            act.wait_ge(pv_ready, i * tiles + (T0 + t - 1))
                        act.activation(probsT[:, t % 2, k:TOK], PS[:, 7 if t % 2 == 0 else 3, k:TOK], ACT.Copy)\
                            .then_inc(probsT_ready, 1)
                    exps(0)
                    for t in range(1, tiles + 1):
                        if t < tiles:
                            exps(t)
                        turned(t - 1)

            def turn(ph):
                for c in range(4):
                    act.wait_ge(attn_turned, ph.at.merge + c + 1)
                    act.activation(merged[:, c, 0:ph.tokens], PS[:, c, 0:ph.tokens], ACT.Copy)\
                        .then_inc(merge_ready, 1)
                act.wait_ge(merge_ready, ph.at.merge + 4)

            def gates(ph):
                G = ph.at.gates
                act.wait_ge(gate_mm, 2 * G + 2)
                o, _ = COLS[("b_gate", ph.layer)]
                link(act.activation(g_soft, PS[0:64, 1, :], ACT.Abs, bias=par[0:64, o + 1:o + 2]))
                link(act.activation(g_soft, g_soft, ACT.Exp, scale=-1.0))
                act.activation(g_soft, g_soft, ACT.Ln, bias=1.0).then_inc(gate_softplus, 1)
                for mixer in range(2):
                    for t in range(4):
                        act.wait_ge(v_acc, 8 * G + 4 * mixer + t + 1)
                        act.activation(vall[:, mixer, t, :], PS[:, 4 + t, :], ACT.Copy).then_inc(v_copied, 1)

            def pairs(ph):
                tiles, Q0, N0, per, T = ph.tiles, ph.at.pair, ph.at.pairtile, 2 * ph.tiles, ph.tokens
                G = ph.at.gates

                def mlstm_copy(p, j):
                    act.wait_ge(pm_acc, p * 3 + (3 * Q0 + j + 1 + CREDIT))
                    if j == 0:
                        ins = act.activation(qkraw[:, 0, 0:T], PS[:, 2, 0:T], ACT.Copy, scale=float(HD) ** -0.5)
                    elif j == 1:
                        ins = act.activation(qkraw[:, 1, :], PS[:, 3, :], ACT.Copy)
                    else:
                        if not isinstance(p, int) or p:
                            act.wait_ge(pm_final, p + Q0)
                        ins = act.activation(osig[:, 0:T], PS[:, 2, 0:T], ACT.Sigmoid)
                    ins.then_inc(pm_copied, 1)

                def neighbour_copy(p, j):
                    act.wait_ge(na_acc, p * 2 + (2 * Q0 + j + 1 + CREDIT))
                    n = TOK if j else T
                    act.activation(qkna[:, j, 0:n], PS[:, 2 + j, 0:n], ACT.Copy, scale=1.0 if j else float(HD) ** -0.5)\
                        .then_inc(na_copied, 1)

                for j in range(3):
                    mlstm_copy(0, j)
                act.wait_ge(gate_rows, G)
                act.activation(g_guard, g_guard, ACT.Exp, scale=-1.0).then_inc(gate_guard, 1)
                act.wait_ge(gate_turned, G)
                turned = PS[:, 0, :].rearrange("p (t e n) -> p t e n", t=4, e=2)
                cols = arena[:, 9, :].rearrange("p (t e n) -> p t e n", t=4, e=2)
                act.activation(cols[:, :, 0, :], turned[:, :, 0, :], ACT.Copy, scale=-1.0).then_inc(gate_cols, 1)
                act.activation(cols[:, :, 1, :], turned[:, :, 1, :], ACT.Copy).then_inc(gate_cols, 1)

                def transposed(i, n, turned_, pv, sem_):
                    k = 0 if n % tiles < 2 else LAT
                    act.wait_ge(turned_, i * per + (N0 + n + 1))
                    if n >= 2:
                        act.wait_ge(pv, i * per + (N0 + n - 1))
                    act.activation(probsT[:, n % 2, k:TOK], PS[:, 0, k:TOK], ACT.Copy).then_inc(sem_, 1)

                def weigh(i, n):
                    k = 0 if n % tiles < 2 else LAT
                    w = (wt0, qkn)[n % 2]
                    act.wait_ge(pm_logw, i * per + (N0 + n + 1))
                    act.activation(w[:, :, k:TOK], w[:, :, k:TOK], ACT.Exp).then_inc(pm_w, 1)

                def exps(i, n):
                    k = 0 if n % tiles < 2 else LAT
                    act.wait_ge(na_max, i * per + (N0 + n + 1))
                    if n >= 2:
                        act.wait_ge(na_turned, i * per + (N0 + n - 1))
                    act.activation(probs[:, n % 2, k:TOK], PS[:, 6 + n % 2, k:TOK], ACT.Exp,
                                   bias=small[:, 32 + n:33 + n], accum_out=small[:, 40 + n:41 + n])\
                        .then_inc(na_exp, 1)

                def iteration(i, last):
                    step = 2 * DC // per
                    weigh(i, 0)
                    for n in range(per):
                        if n + 1 < per:
                            weigh(i, n + 1)
                        transposed(i, n, pm_turned, pm_pv, pm_pT)
                        for j in range(2):
                            if n == (DC * (j + 1) - 1) // step:
                                neighbour_copy(i, j)
                        act.wait_ge(pm_pv, i * per + (N0 + n + 1))
                        e, t = n // tiles, n % tiles
                        act.activation(tok[:, t, e * HD:(e + 1) * HD], PS[:, 1, 0:HD], ACT.Copy).then_inc(pm_o, 1)
                    step = 3 * DC // per
                    exps(i, 0)
                    act.wait_ge(pm_var, i + (Q0 + 1))
                    act.activation(small[:, 16:16 + per], small[:, 8:8 + per], ACT.Sqrt, bias=eps[:, :],
                                   scale=1.0 / HD).then_inc(pm_std, 1)
                    for n in range(per):
                        if n + 1 < per:
                            exps(i, n + 1)
                        transposed(i, n, na_turned, na_pv, na_pT)
                        for j in range(3):
                            if not last and n == (DC * (j + 1) - 1) // step:
                                mlstm_copy(i + 1, j)

                with act.Fori(0, HP - 1) as i:
                    iteration(i, False)
                iteration(HP - 1, True)

            run = dict(ada=ada, norm=norm, swiglu=swiglu, down=lambda ph: None, mix_in=mix_in, gating=gating,
                       heads=heads, turn=turn, gates=gates, pairs=pairs, mlp=mlp)
            for ph in PLAN:
                if ph.kind == "norm" and ph.what in ("q_lat", "kv_lat"):
                    act.wait_ge(acc_evacuated, ph.at.evac)
                run[ph.kind](ph)

        @block.vector
        def _(dve):
            chain = [0, None, 0]

            def link(ins):
                chain[0] += 1
                ins.then_inc(dve_chain, 1)
                if chain[1] is None:
                    dve.wait_ge(dve_chain, chain[0])
                else:
                    dve.wait_ge(dve_chain, chain[1] * chain[2] + chain[0])

            def loop(i, per):
                chain[1], chain[2] = i, per
                return chain[0]

            def loop_end(start, times):
                assert chain[0] - start == chain[2], (chain[0] - start, chain[2])
                chain[0] = start + chain[2] * times
                chain[1] = None

            tt = dve.tensor_tensor
            stt = dve.scalar_tensor_tensor
            link(dve.memset(vpad[:, :, :, :], 0.0))
            link(dve.memset(zc[:, :, :, :], 0.0))
            link(dve.memset(cond[:, :, :], 0.0))
            dve.memset(eps[:, :], EPS).then_inc(setup_done, 1)
            dve.sem_inc(glu_done, 2)
            dve.sem_inc(acc_evacuated, 4)
            dve.sem_inc(ada_row, 1)
            dve.sem_inc(ada_done, 1)
            for s in (head_v, attn_done, pm_acc, na_acc, pair_done):
                dve.sem_inc(s, CREDIT)
            dve.wait_ge(params_in, 32)

            def ada_add(ph, block, i=0):
                ob, _ = COLS["b_ada"]
                first = ph.at.ada - 1 + block
                out = mod[:, bass.ds(i * 32 + 32 * first, 32)]
                bias = par[:, bass.ds(i * DC + (ob + DC * first), DC)]
                dve.wait_ge(ada_turned, i + (first + 1))
                tt(out.rearrange("p (h c j) -> p h c j", h=2, c=4),
                   PS[:, 6, 0:32].rearrange("p (c h j) -> p h c j", c=4, h=2),
                   bias.rearrange("p (h c j) -> p h c j", h=2, j=1).broadcast_to([P, 2, 4, 4]),
                   ALU.add).then_inc(ada_done, 1)

            def ada(ph):
                with dve.Fori(0, ph.blocks) as i:
                    ada_add(ph, 0, i)

            def norm(ph):
                s = norm_spec(ph)
                if ph.shifted:
                    dve.wait_ge(ada_done, s.blocks + 1)
                    if ph.at.scaled:
                        dve.wait_ge(norm_scaled, ph.at.scaled)
                    link(stt(gain.rearrange("p (c j) -> p c j", j=2), s.scale, 1.0,
                             s.g.rearrange("p (c o) -> p c o", o=1).broadcast_to([P, DC, 2]), ALU.add, ALU.mult))
                dve.wait_ge(norm_std, ph.at.std + 1)
                if ph.at.scaled:
                    dve.wait_ge(norm_scaled, ph.at.scaled)
                dve.reciprocal(rstd[:, 0:ph.tokens], std[:, 0:ph.tokens]).then_inc(norm_rstd, 1)
                dve.wait_ge(norm_rstd, ph.at.rstd + 1)
                for c in range(ph.chunks):
                    for a, b, cnd in s.pieces:
                        stt(s.dst[:, c, a:b], s.src[:, c, a:b], s.gain(c, cnd), rstd[:, a:b], ALU.mult, ALU.mult)\
                            .then_inc(norm_scaled, 1)

            def swiglu(ph):
                head = U_SWIGLU % RING // 2

                def pair(i, j):
                    dst = hidden[:, j, 0:ph.tokens] if isinstance(i, int) else \
                        hidden[:, bass.ds(i * (RING // 2) + j, 1), 0:ph.tokens].rearrange("p o n -> p (o n)")
                    dve.wait_ge(silu_done, i * (RING // 2) + (ph.at.silu + j + 1))
                    dve.wait_ge(acc_ready, i * RING + (ph.at.acc + 2 * j + 2))
                    tt(dst, PS[:, 2 * (j % 2) + 1, 0:ph.tokens], sa[:, j % 2, 0:ph.tokens], ALU.mult)\
                        .then_inc(glu_done, 1)
                for j in range(head):
                    pair(0, j)
                with dve.Fori(0, U_SWIGLU // RING) as i:
                    for j in range(RING // 2):
                        if j == 3:
                            ada_add(ph, 0, i)
                        pair(i, head + j)

            def down(ph):
                v, weight = {"ffn1": (2, 0.5), "mix": (5, 1.0), "ffn2": (8, 0.5), "mix2": (2, 1.0),
                             "mlp": (5, 1.0)}[ph.which]
                dve.wait_ge(ada_done, ADA_AT[ph.layer] + v + 2)
                if ph.at.h:
                    dve.wait_ge(h_ready, ph.at.h)
                link(dve.tensor_scalar(gate.rearrange("p (c j) -> p c j", j=2), mod_of(ph.layer, v), weight, None,
                                       ALU.mult))
                for m in range(DC):
                    dve.wait_ge(out_ready, ph.at.out + 4 * (ph.n - 1) + m // 2 + 1)
                    for a, b, cnd in HALVES[:ph.tokens // LAT]:
                        g = 2 * m + cnd
                        stt(h[:, m, a:b], PS[:, out_bank(m), a:b], gate[:, g:g + 1], h[:, m, a:b],
                            ALU.mult, ALU.add).then_inc(h_ready, 1)

            def mix_in(ph):
                for block in range(ph.ada):
                    ada_add(ph, block)

            def gating(ph):
                l, n = ph.layer, ph.tiles
                dve.wait_ge(acc_evacuated, ph.at.evac)
                v = sgv[:, 0:n, :].rearrange("p t c -> p (t c)")
                t0 = sgt[:, 0:1, :].rearrange("p o n -> p (o n)")
                for q in range(n // 2):
                    part = v[:, q * 512:(q + 1) * 512]
                    link(tt(t0, part, part, ALU.mult))
                    red = dve.tensor_reduce(sgt[:, 1, 32 + 8 * q:40 + 8 * q], t0.rearrange("p (g c) -> p g c", c=64),
                                            AXX, ALU.add)
                    if q == n // 2 - 1:
                        red.then_inc(sg_var, 1)
                    else:
                        link(red)
                dve.wait_ge(sg_std, ph.at.sg + 1)
                link(dve.reciprocal(sgt[:, 1, 64:64 + 4 * n], sgt[:, 1, 0:4 * n]))
                if ph.at.sg:
                    dve.wait_ge(sg_mixed, ph.at.sg)
                for e in range(2):
                    src = sgv[:, 0:n, :].rearrange("p t (g e c) -> p t g e c", e=2, c=64)[:, :, :, e, :]
                    r = sgt[:, 1, 64:64 + 4 * n].rearrange("p (t g e) -> p t g e", e=2, g=2)[:, :, :, e:e + 1]\
                        .broadcast_to([P, n, 2, 64])
                    dst = vpad[:, 0:n, :, :].rearrange("p t (g e) c -> p t g e c", e=2)[:, :, :, e,
                                                                                       64 * e:64 * e + 64]
                    ins = tt(dst, src, r, ALU.mult)
                    if e == 0:
                        link(ins)
                ins.then_inc(sg_v, 1)
                hs = ph.tokens // LAT
                for cb in range(2):
                    part = lambda j: cv[:, 2 * j + cb, 0:ph.tokens].rearrange("p (s t) -> p s t", s=hs)
                    z = zc[:, cb, 0:hs, :]
                    y = merged[:, 6 + cb, 0:ph.tokens].rearrange("p (s t) -> p s t", s=hs)
                    link(tt(z[:, :, 1:LAT + 1], part(1), part(2), ALU.mult))
                    w = lambda k: col("w_conv", l, 3 * cb + k)
                    link(dve.tensor_scalar(y, z[:, :, 0:LAT], w(0), None, ALU.mult))
                    link(stt(y, z[:, :, 1:LAT + 1], w(1), y, ALU.mult, ALU.add))
                    link(stt(y, z[:, :, 2:LAT + 2], w(2), y, ALU.mult, ALU.add))
                    link(tt(y, y, part(0), ALU.mult))
                dve.wait_ge(sg_mixed, ph.at.sg + 1)
                for cb in range(2):
                    b = sgw[:, (4 + cb) * P:(5 + cb) * P].rearrange("p (o n) -> p o n", o=1).broadcast_to([P, n, P])
                    y = merged[:, 4 + cb, 0:ph.tokens]
                    link(stt(y.rearrange("p (t n) -> p t n", n=P),
                             PS[:, 5 + cb, 0:ph.tokens].rearrange("p (t n) -> p t n", n=P),
                             col("g_sgu", l, cb), b, ALU.mult, ALU.add))
                    link(tt(y, y, sgu[:, cb, 0:ph.tokens], ALU.mult))
                dve.tensor_scalar(gqs[:, :], col("g_q_head", l), float(QK) ** -0.5, None, ALU.mult)\
                    .then_inc(sg_done, 1)

            def heads(ph):
                l, tiles, H0, T0 = ph.layer, ph.tiles, ph.at.head, ph.at.headtile
                dve.wait_ge(sg_done, ph.at.sg)
                with dve.Fori(0, HEADS) as i:
                    start = loop(i, 4 + tiles)
                    dve.wait_ge(head_std, i * 2 + (2 * H0 + 1))
                    link(dve.reciprocal(probs[:, 0, 0:ph.tokens], probsT[:, 0, 0:ph.tokens]))
                    stt(qkn[:, 0, 0:ph.tokens], qkraw[:, 0, 0:ph.tokens], gqs[:, :], probs[:, 0, 0:ph.tokens],
                        ALU.mult, ALU.mult).then_inc(head_qn, 1)
                    dve.wait_ge(head_std, i * 2 + (2 * H0 + 2))
                    link(dve.reciprocal(probs[:, 1, :], probsT[:, 1, :]))
                    stt(qkn[:, 1, :], qkraw[:, 1, :], col("g_k_head", l), probs[:, 1, :], ALU.mult, ALU.mult)\
                        .then_inc(head_qn, 1)
                    trig = lambda name: const(name).rearrange("p (o n) -> p o n", o=1).broadcast_to([P, 2, LAT])
                    dve.wait_ge(head_rot, i + (H0 + 1))
                    link(tt(qkt[:, :, 0:LAT], PS[:, 0:2, 0:LAT], trig("sin1"), ALU.mult))
                    link(tt(qkn[:, :, 0:LAT], qkn[:, :, 0:LAT], trig("cos1"), ALU.mult))
                    tt(qkn[:, :, 0:LAT], qkn[:, :, 0:LAT], qkt[:, :, 0:LAT], ALU.add).then_inc(head_rope, 1)

                    def maxes(t):
                        k = 0 if t < 2 else LAT
                        dve.wait_ge(score_ready, i * tiles + (T0 + t + 1))
                        dve.tensor_reduce(nmax[:, t:t + 1], PS[:, 5 + t % 2, k:TOK], AXX, ALU.max, negate=True)\
                            .then_inc(max_ready, 1)

                    def outs(t):
                        dve.wait_ge(exp_done, i * tiles + (T0 + t + 1))
                        link(dve.reciprocal(rinv[:, t:t + 1], rsum[:, t:t + 1]))
                        dve.wait_ge(pv_ready, i * tiles + (T0 + t + 1))
                        dve.tensor_scalar(attn_tok[:, t, bass.ds(i * VD, VD)], PS[:, 4 - 2 * (t % 2), 0:VD],
                                          rinv[:, t:t + 1], None, ALU.mult).then_inc(attn_done, 1)
                    maxes(0)
                    for t in range(1, tiles + 1):
                        if t < tiles:
                            maxes(t)
                        outs(t - 1)
                    loop_end(start, HEADS)

            def gates(ph):
                G = ph.at.gates
                o, _ = COLS[("b_gate", ph.layer)]
                dve.wait_ge(gate_mm, 2 * G + 2)
                dve.wait_ge(gate_softplus, G + 1)
                link(dve.tensor_scalar(g_f, PS[0:64, 1, :], par[0:64, o + 1:o + 2], 0.0, ALU.add, ALU.min))
                link(tt(g_f, g_f, g_soft, ALU.subtract))

                def scan(out, src, initial, op0, op1):
                    for rows, back, edge in ((slice(0, 32), False, TOK - 1), (slice(32, 64), True, LAT)):
                        for part, first in ((slice(LAT, TOK), True), (slice(0, LAT), False)):
                            o_, s_ = out[rows, part], src[rows, part]
                            if back:
                                o_, s_ = o_[:, ::-1], s_[:, ::-1]
                            link(dve.tensor_tensor_scan(o_, s_, s_, initial if first else out[rows, edge:edge + 1],
                                                        op0, op1))
                scan(g_b, g_f, 0.0, ALU.add, ALU.bypass)
                link(stt(g_a, PS[0:64, 0, :], par[0:64, o:o + 1], g_b, ALU.add, ALU.subtract))
                scan(g_m, g_a, 0.0, ALU.max, ALU.max)
                tt(g_guard, g_b, g_m, ALU.add).then_inc(gate_rows, 1)
                dve.wait_ge(masks_in, 16)

            def pairs(ph):
                tiles, Q0, N0, per, T = ph.tiles, ph.at.pair, ph.at.pairtile, 2 * ph.tiles, ph.tokens
                og, _ = COLS[("norm_g", ph.layer)]
                mtok = tok[:, 0:tiles, :].rearrange("p t (e d) -> p (t e) d", e=2)
                tmp = qkt[:, 0, 0:T].rearrange("p (g d) -> p g d", d=HD)

                def selectors(p):
                    for d in range(2):
                        for e in range(2):
                            ins = dve.tensor_scalar(sel[:, 2 * d + e, :], ones[0:64, :],
                                                    ident[0:64, bass.ds(p * 2 + (32 * d + e), 1)], None, ALU.mult)
                    ins.then_inc(pm_sel, 1)

                def rope(p):
                    trig = lambda name: const(name).rearrange("p (o n) -> p o n", o=1).broadcast_to([P, 2, LAT])
                    rot = PS[:, 3, :].rearrange("p (e n) -> p e n", e=2)
                    dve.wait_ge(pm_rot, p + (Q0 + 1))
                    link(tt(qkt[:, :, 0:LAT], rot, trig("sin2"), ALU.mult))
                    link(tt(qkraw[:, :, 0:LAT], qkraw[:, :, 0:LAT], trig("cos2"), ALU.mult))
                    tt(qkraw[:, :, 0:LAT], qkraw[:, :, 0:LAT], qkt[:, :, 0:LAT], ALU.add).then_inc(pm_rope, 1)

                def log_weights(i, n):
                    e, t = n // tiles, n % tiles
                    k = 0 if t < 2 else LAT
                    w = (wt0, qkn)[n % 2]
                    dve.wait_ge(pm_arow, i * 2 + (2 * Q0 + e + 1))
                    for d in range(2):
                        ins = stt(w[:, d, k:TOK], PS[:, 4 + d, k:TOK],
                                  gcol[:, t, 0, d, bass.ds(i * 2 + e, 1)], maskt[:, d, t, k:TOK],
                                  ALU.add, ALU.add)
                    ins.then_inc(pm_logw, 1)

                def weighted(i, n):
                    e, t = n // tiles, n % tiles
                    k = 0 if t < 2 else LAT
                    w = (wt0, qkn)[n % 2]
                    dve.wait_ge(pm_w, i * per + (N0 + n + 1))
                    dve.wait_ge(pm_score, i * per + (N0 + n + 1))
                    for d in range(2):
                        ins = dve.tensor_tensor_reduce(w[:, d, k:TOK], PS[:, 6 + n % 2, k:TOK], w[:, d, k:TOK],
                                                       1.0, 0.0, ALU.mult, ALU.add, small[:, d:d + 1])
                    link(ins)
                    link(stt(small[:, 2:4], small[:, 0:2], -1.0, small[:, 0:2], ALU.mult, ALU.max))
                    link(tt(small[:, 2:4], small[:, 2:4],
                            gcol[:, t, 1, :, bass.ds(i * 2 + e, 1)].rearrange("p d o -> p (d o)"), ALU.max))
                    link(dve.reciprocal(small[:, 4:6], small[:, 2:4]))
                    link(dve.tensor_scalar(w[:, 1, k:TOK], w[:, 1, k:TOK], small[:, 5:6], None, ALU.mult))
                    if n >= 2:
                        dve.wait_ge(pm_turned, i * per + (N0 + n - 1))
                    stt(probs[:, n % 2, k:TOK], w[:, 0, k:TOK], small[:, 4:5], w[:, 1, k:TOK], ALU.mult, ALU.add)\
                        .then_inc(pm_p, 1)
                    dve.wait_ge(pm_p, i * per + (N0 + n + 1))

                def maxes(i, n):
                    e, t = n // tiles, n % tiles
                    k = 0 if t < 2 else LAT
                    dve.wait_ge(na_score, i * per + (N0 + n + 1))
                    if t < 2:
                        s = PS[:, 6 + n % 2, 0:LAT]
                        link(tt(s, s, nabias[:, e, t, :], ALU.add))
                    dve.tensor_reduce(small[:, 32 + n:33 + n], PS[:, 6 + n % 2, k:TOK], AXX, ALU.max, negate=True)\
                        .then_inc(na_max, 1)

                def outs(i, n):
                    e, t = n // tiles, n % tiles
                    dve.wait_ge(na_exp, i * per + (N0 + n + 1))
                    link(dve.reciprocal(small[:, 48 + n:49 + n], small[:, 40 + n:41 + n]))
                    dve.wait_ge(na_pv, i * per + (N0 + n + 1))
                    dve.tensor_scalar(tokn[:, t, e * HD:(e + 1) * HD], PS[:, 1, 0:HD],
                                      small[:, 48 + n:49 + n], None, ALU.mult).then_inc(na_o, 1)

                def out_chunk(i, first):
                    return merged2[:, first + i, 0:T] if isinstance(i, int) else \
                        merged2[:, bass.ds(i + first, 1), 0:T].rearrange("p o n -> p (o n)")

                wide = lambda a: a.rearrange("p (g o) -> p g o", o=1).broadcast_to([P, per, HD])

                def iteration(i, last):
                    log_weights(i, 0)
                    for n in range(per):
                        if n + 1 < per:
                            log_weights(i, n + 1)
                        weighted(i, n)
                    dve.wait_ge(bias_in, i * 16 + 16 * (Q0 + 1))
                    maxes(i, 0)
                    dve.wait_ge(pm_o, i * per + (N0 + per))
                    mu = small[:, 0:per]
                    link(dve.tensor_reduce(mu, mtok, AXX, ALU.add))
                    link(dve.tensor_scalar(mu, mu, 1.0 / HD, None, ALU.mult))
                    link(tt(mtok, mtok, wide(mu), ALU.subtract))
                    link(tt(tmp, mtok, mtok, ALU.mult))
                    dve.tensor_reduce(small[:, 8:8 + per], tmp, AXX, ALU.add).then_inc(pm_var, 1)
                    maxes(i, 1)
                    dve.wait_ge(pm_std, i + (Q0 + 1))
                    link(dve.reciprocal(small[:, 24:24 + per], small[:, 16:16 + per]))
                    tt(mtok, mtok, wide(small[:, 24:24 + per]), ALU.mult).then_inc(pm_normed, 1)
                    for n in range(per):
                        if n >= 1 and n + 1 < per:
                            maxes(i, n + 1)
                        outs(i, n)
                        if n == 1:
                            if not last:
                                selectors(i + 1)
                            dve.wait_ge(pm_fm, i + (Q0 + 1))
                            stt(out_chunk(i, 0), PS[:, 4, 0:T], par[:, bass.ds(i + og, 1)], osig[:, 0:T],
                                ALU.mult, ALU.mult).then_inc(pm_final, 1)
                    if not last:
                        rope(i + 1)
                    dve.wait_ge(na_fm, i + (Q0 + 1))
                    dve.tensor_scalar(out_chunk(i, HP), PS[:, 0, 0:T], 1.0, None, ALU.mult).then_inc(pair_done, 1)

                selectors(0)
                rope(0)
                dve.wait_ge(gate_cols, 2 * ph.at.gates)
                with dve.Fori(0, HP - 1) as i:
                    start = loop(i, 11 + 6 * per)
                    iteration(i, False)
                    loop_end(start, HP - 1)
                iteration(HP - 1, True)

            def mlp(ph):
                with dve.Fori(0, MC // RING) as i:
                    for j in range(RING):
                        dve.wait_ge(relu_read, i * RING + (ph.at.silu + j + 1))
                        r = sa[:, j % 2, 0:ph.tokens]
                        tt(hidden[:, bass.ds(i * RING + j, 1), 0:ph.tokens].rearrange("p o n -> p (o n)"), r, r,
                           ALU.mult).then_inc(glu_done, 1)
                        if ph.ada and j == 5:
                            ada_add(ph, 0, i)

            run = dict(ada=ada, norm=norm, swiglu=swiglu, down=down, mix_in=mix_in, gating=gating,
                       heads=heads, turn=lambda ph: None, gates=gates, pairs=pairs, mlp=mlp)
            for ph in PLAN:
                if ph.kind == "norm" and ph.what in ("q_lat", "kv_lat"):
                    dve.wait_ge(acc_evacuated, ph.at.evac)
                if ph.kind == "norm" and ph.what == "attn":
                    dve.wait_ge(merge_ready, ph.at.merge)
                run[ph.kind](ph)


def unit_fm(w):
    m = w.shape[1] // P
    return w.reshape(DC, P, m, P).transpose(2, 1, 0, 3).reshape(m, P, UNIT)


def unit_tm(w):
    n = w.shape[1]
    return w.reshape(DC * n // UNIT, UNIT // n, P, n).transpose(0, 2, 1, 3).reshape(-1, P, UNIT)


def unit_rows(w):
    return w.reshape(-1, P, UNIT)


def unit_ada(w):
    return w.reshape(DC, P, -1, UNIT).transpose(2, 0, 1, 3)


def padded(w, left, width):
    out = np.zeros((w.shape[0], width), np.float32)
    out[:, left:left + w.shape[1]] = w
    return out


def interleaved(w):
    return w.reshape(D, 2, PAIRS, P).transpose(0, 2, 1, 3).reshape(D, 2 * D_FF)


def columns(v):
    return v.reshape(-1, P).T


def rope_tables():
    t = np.arange(LAT)
    row, colm = (t // GRID_W).astype(np.float32), (t % GRID_W).astype(np.float32)
    axis = ROPE // 2
    inv = (1.0 / (10000.0 ** (np.arange(0, axis, 2, dtype=np.float32) / axis))).astype(np.float32)
    ar, ac = row[:, None] * inv, colm[:, None] * inv
    ang = np.concatenate([ar, ar, ac, ac], axis=-1)
    cos1, sin1 = np.ones((P, LAT), np.float32), np.zeros((P, LAT), np.float32)
    cos1[NOPE:QK], sin1[NOPE:QK] = np.cos(ang).T, np.sin(ang).T
    rot1 = np.zeros((P, P), np.float32)
    for a in range(NOPE, QK, axis):
        for j in range(axis // 2):
            rot1[a + axis // 2 + j, a + j] = -1.0
            rot1[a + j, a + axis // 2 + j] = 1.0
    n = HD // 4
    inv2 = (10000.0 ** (-np.arange(n, dtype=np.float32) / n)).astype(np.float32)
    ang2 = np.concatenate([row[:, None] * inv2, colm[:, None] * inv2], axis=-1)
    cos2, sin2 = np.tile(np.cos(ang2).T, (4, 1)), np.tile(np.sin(ang2).T, (4, 1))
    rot2 = np.zeros((P, P), np.float32)
    for a in range(0, P, HD):
        for j in range(HD // 2):
            rot2[a + HD // 2 + j, a + j] = -1.0
            rot2[a + j, a + HD // 2 + j] = 1.0
    return rot1, cos1, sin1, rot2, cos2.astype(np.float32), sin2.astype(np.float32)


def ada_selector():
    m = np.zeros((P, 8), np.float32)
    for q in range(4):
        for j in range(4):
            m[32 * q + j, 4 * (q % 2) + j] = 1.0
    return m


def neighbour_bias(rpb):
    t = np.arange(LAT)
    row, colm = t // GRID_W, t % GRID_W
    start = np.clip(colm - 8, 0, GRID_W - 16)
    inside = (colm[None, :] >= start[:, None]) & (colm[None, :] < start[:, None] + 16)
    dr = row[None, :] - row[:, None] + 7
    dc = np.clip(colm[None, :] - colm[:, None] + 15, 0, 30)
    bias = np.where(inside, rpb[:, dr, dc], np.float32(NEG))
    return bias.reshape(HP, 2, 2, P, LAT).transpose(0, 3, 1, 2, 4).reshape(HP, P, 4 * LAT)


def scan_masks():
    m = np.full((P, 2, 4, TOK), np.float32(NEG))
    key = np.arange(LAT)[None, :]
    for t in range(4):
        query = (t % 2) * P + np.arange(P)[:, None]
        own = slice(0, LAT) if t < 2 else slice(LAT, TOK)
        if t < 2:
            m[:, :, t, LAT:TOK] = 0.0
        m[:, 0, t, own] = np.where(key <= query, np.float32(0), np.float32(NEG))
        m[:, 1, t, own] = np.where(key >= query, np.float32(0), np.float32(NEG))
    return m


def layout(x, c, ctx, c_ctx, w_ada, b_ada, g_ffn1, w_ffn1_in, w_ffn1_out, g_mix, w_mix_in, g_q_lat, w_q_up, g_kv_lat,
           w_kv_up, g_q_head, g_k_head, g_sgu, w_spatial, b_spatial, w_conv, g_out, w_mix_out, g_ffn2, w_ffn2_in,
           w_ffn2_out, c_2, ctx_2, c_ctx_2, w_ada_2, b_ada_2, norm1_g_2, w_in_2, b_gate_2, mlstm_norm_g_2, rpb_2,
           w_out_2, norm2_g_2, w_mlp1_2, w_mlp2_2, final_g_2):
    cut = np.cumsum([Q_LORA, KV_LORA, ROPE, 2 * SG])
    ada = np.concatenate([unit_ada(w_ada[0]), unit_ada(w_ada[1]), unit_ada(w_ada_2[0]), unit_ada(w_ada_2[1])])
    pair_m, pair_n, na_bias, gate_units = [], [], [], []
    q_, k_, v_, o_, nq, nk, nv, gm = range(8)
    for l in range(2):
        w = np.split(w_in_2[l], np.cumsum([512] * 7), axis=1)
        gate = np.zeros((D, P), np.float32)
        for e in range(2):
            for d in range(2):
                gate[:, 64 * e + 32 * d:64 * e + 32 * d + 8] = w[gm][:, 16 * e + 8 * d:16 * e + 8 * d + 8]
        gate_units.append(unit_fm(gate))
        fm = [unit_fm(a) for a in w[:7]]
        pair_m.append(np.concatenate([fm[j] for j in (q_, k_, o_)], axis=2))
        pair_n.append(np.concatenate([fm[j] for j in (nq, nk)], axis=2))
        gate_units += [unit_tm(np.ascontiguousarray(w[v_])), unit_tm(np.ascontiguousarray(w[nv]))]
        na_bias.append(neighbour_bias(rpb_2[l]))

    parts = []
    for ph in PLAN:
        l, b = ph.layer, ph.at.ada - 1
        if ph.kind == "ada":
            parts += list(ada[b:b + ph.blocks])
        if ph.kind == "swiglu":
            w = unit_fm(interleaved((w_ffn1_in if ph.which == "ffn1" else w_ffn2_in)[l]))
            head = U_SWIGLU % RING
            parts.append(w[:head])
            for i in range(ph.ada):
                w8 = w[head + RING * i:head + RING * (i + 1)]
                parts += [w8[0:2], ada[b + i, 0:2], w8[2:4], ada[b + i, 2:4], w8[4:6], ada[b + i, 4:8], w8[6:8]]
        if ph.kind == "down":
            parts.append(unit_rows({"ffn1": w_ffn1_out, "mix": w_mix_out, "ffn2": w_ffn2_out}[ph.which][l] if l < 2
                                   else {"mix2": w_out_2, "mlp": w_mlp2_2}[ph.which][l - 2]))
        if ph.kind == "mix_in":
            q, kv, kpe, sgm, cvm = np.split(w_mix_in[l], cut, axis=1)
            w = np.concatenate([unit_fm(q), unit_fm(kv), unit_fm(padded(kpe, NOPE, P)), unit_fm(cvm),
                                unit_fm(sgm[:, :SG])])
            for j in range(MIX_FM):
                parts.append(w[j:j + 1])
                if j < DC:
                    parts.append(ada[b + j // 4, 2 * (j % 4):2 * (j % 4) + 2])
            parts.append(unit_tm(np.ascontiguousarray(sgm[:, SG:])))
        if ph.kind == "gates":
            parts += gate_units[3 * (l - 2):3 * (l - 2) + 3]
        if ph.kind == "mlp":
            w = unit_fm(w_mlp1_2[l - 2])
            if not ph.ada:
                parts.append(w)
            for i in range(ph.ada):
                for j in range(RING):
                    parts.append(w[RING * i + j:RING * i + j + 1])
                    if j < 4:
                        parts.append(ada[b + i, 2 * j:2 * j + 2])
    stream = np.concatenate(parts)

    head_w = np.zeros((2, HEADS, P, HW), np.float32)
    for l in range(2):
        for hd in range(HEADS):
            q = padded(w_q_up[l][:, hd * QK:(hd + 1) * QK], 0, P).reshape(QC, P, P).transpose(1, 0, 2)
            kv = w_kv_up[l][:, hd * P:(hd + 1) * P]
            k = padded(kv[:, :NOPE], 0, P).reshape(KC, P, P).transpose(1, 0, 2)
            v = kv[:, NOPE:].reshape(KC, P, VD).transpose(1, 0, 2)
            head_w[l, hd] = np.concatenate([q.reshape(P, -1), k.reshape(P, -1), v.reshape(P, -1)], axis=1)

    sg_w = np.stack([np.concatenate([
        w_spatial[l].transpose(2, 0, 1).reshape(P, 4 * P),
        np.repeat(b_spatial[l], 64, axis=0).reshape(2, P, P).transpose(1, 0, 2).reshape(P, 2 * P)], axis=1)
        for l in range(2)])

    rot1, cos1, sin1, rot2, cos2, sin2 = rope_tables()
    consts = np.concatenate([np.eye(P, dtype=np.float32), np.ones((P, P), np.float32), rot1, cos1, sin1,
                             rot2, cos2, sin2, ada_selector()], axis=1)
    cols = []
    for l in range(2):
        cols += [columns(g_ffn1[l]), columns(g_mix[l]), columns(g_ffn2[l]), columns(g_q_lat[l]),
                 columns(g_kv_lat[l]), padded(g_q_head[l][None], 0, P).T, padded(g_k_head[l][None], 0, P).T,
                 columns(g_sgu[l]), columns(g_out[l]),
                 w_conv[l].reshape(3, 2, P).transpose(2, 1, 0).reshape(P, 6)]
    for l in range(2):
        bg = np.zeros((P, 2), np.float32)
        for e in range(2):
            for d in range(2):
                bg[32 * d:32 * d + 8, e] = b_gate_2[l, 16 * e + 8 * d:16 * e + 8 * d + 8]
        cols += [columns(norm1_g_2[l]), columns(norm2_g_2[l]), columns(mlstm_norm_g_2[l]), bg]
    cols += [columns(final_g_2), columns(b_ada), columns(b_ada_2),
             np.stack([columns(v) for v in (c[0], c_ctx, c_2[0], c_ctx_2)], axis=2).reshape(P, 4 * DC)]
    params = np.concatenate(cols, axis=1)
    return dict(pair_m=np.concatenate(pair_m), pair_n=np.concatenate(pair_n), na_bias=np.concatenate(na_bias),
                masks=scan_masks(), stream=stream, head_w=head_w.reshape(2 * HEADS, P, HW), sg_w=sg_w, consts=consts, params=params,
                xT=np.ascontiguousarray(x[0].T), ctxT=np.ascontiguousarray(ctx[0].T),
                ctx2T=np.ascontiguousarray(ctx_2[0].T))


def kernel(**inputs):
    import concourse.bacc as bacc
    from concourse.bass_utils import run_bass_kernel_spmd

    arrays = layout(**{k: np.asarray(v) for k, v in inputs.items()})
    nc = bacc.Bacc("TRN2", target_bir_lowering=False, num_devices=1)
    args = {k: nc.dram_tensor(k, a.shape, F32, kind="ExternalInput").ap() for k, a in arrays.items()}
    out = nc.dram_tensor("outT", (D, LAT), F32, kind="ExternalOutput").ap()
    build(nc, outT=out, **args)
    r = run_bass_kernel_spmd(nc, [arrays], core_ids=[0])
    return np.ascontiguousarray(r.results[0]["outT"].T)[None]
```

```python
from collections import namedtuple
from contextlib import ExitStack

import numpy as np

import concourse.bass as bass
from concourse import mybir

P = 128
D = 1024
DC = D // P
LAT, CTX = 256, 256
TOK = LAT + CTX
HALVES = ((0, LAT, 0), (LAT, TOK, 1))
EPS = 1e-6
GRID_W = 64

D_FF = 2816
PAIRS = D_FF // P
Q_LORA, KV_LORA, ROPE = 384, 256, 32
NOPE, QK, VD = 64, 96, 64
HEADS = 8
SG = 256
CONV = 256
QC, KC = Q_LORA // P, KV_LORA // P
ADA = (9, 9, 6, 6)
ADA_AT = tuple(sum(ADA[:l]) for l in range(4))

D_MLP = 4 * D
MC = D_MLP // P
HD = 64
HP = 4

CREDIT = 1
RING = 8
UNIT = 1024
HW = (QC + KC) * P
NEG = -1.0e30
ROTATE_AT = 2 * DC + 2
MERGED_BANKS = (1, 2, 3)
VALUE_BANKS = (2, 3, 4, 7)

U_SWIGLU, U_DOWN = 2 * PAIRS, PAIRS
MIX_FM = QC + KC + 1 + 6 + 2
U_MIX = MIX_FM + 2
U_OUT = DC

F32 = mybir.dt.float32
ACT = mybir.ActivationFunctionType
ALU = mybir.AluOpType
AXX = mybir.AxisListType.X

def param_columns():
    at, off = {}, 0
    def put(key, width):
        nonlocal off
        at[key] = (off, width)
        off += width
    for l in range(2):
        for name, width in (("g_ffn1", DC), ("g_mix", DC), ("g_ffn2", DC), ("g_q_lat", QC), ("g_kv_lat", KC),
                            ("g_q_head", 1), ("g_k_head", 1), ("g_sgu", 2), ("g_out", DC), ("w_conv", 6)):
            put((name, l), width)
    for l in range(2, 4):
        for name, width in (("norm1_g", DC), ("norm2_g", DC), ("norm_g", HP), ("b_gate", 2)):
            put((name, l), width)
    put("final_g", DC)
    put("b_ada", sum(ADA) * DC)
    put("cond", DC * 4)
    return at, off


COLS, N_COLS = param_columns()
CONSTS = {}
_off = 0
for _name, _w in (("ident", P), ("ones", P), ("rot1", P), ("cos1", LAT), ("sin1", LAT),
                  ("rot2", P), ("cos2", LAT), ("sin2", LAT), ("ada_sel", 8)):
    CONSTS[_name] = (_off, _w)
    _off += _w
N_CONSTS = _off


COUNTED = ("unit", "acc", "evac", "silu", "glu", "out", "h", "sq", "sum", "std", "rstd", "scaled", "nout", "ada",
           "sg", "head", "headtile", "merge", "gates", "pair", "pairtile", "values")
Counts = namedtuple("Counts", COUNTED)
Phase = namedtuple("Phase", ("kind", "at", "layer", "what", "tokens", "tiles", "blocks", "chunks", "pieces",
                             "shifted", "which", "n", "src", "glu_end", "ada"), defaults=(None,) * 12 + (0,))


class NormSpec:
    pass


def make_plan():
    count = dict.fromkeys(COUNTED, 0)
    count["glu"] = 2
    count["evac"] = 4
    count["ada"] = 1
    plan = []

    def phase(kind, **more):
        adds = more.pop("adds")
        ph = Phase(kind=kind, at=Counts(**count), **more)
        for key, n in adds.items():
            count[key] += n
        plan.append(ph)
        return ph

    def norm(what, chunks, tokens, pieces, shifted, layer):
        n = chunks * pieces
        ada = 1 if shifted and (what, layer) != ("ffn1", 0) else 0
        return phase("norm", what=what, chunks=chunks, tokens=tokens, pieces=pieces, shifted=shifted, layer=layer,
                     ada=ada, adds=dict(unit=ada * DC, ada=ada, sq=chunks, sum=1,
                                        std=1, rstd=1, scaled=n, nout=n if shifted else 0))

    def swiglu(layer, which, tokens, ada):
        halves = tokens // LAT
        norm(which, DC, tokens, halves, True, layer)
        phase("swiglu", layer=layer, which=which, tokens=tokens, ada=ada,
              adds=dict(unit=U_SWIGLU + ada * DC, acc=U_SWIGLU, silu=PAIRS, glu=PAIRS, ada=ada))
        phase("down", layer=layer, which=which, tokens=tokens, n=U_DOWN, src="hidden", glu_end=count["glu"],
              adds=dict(unit=U_DOWN, out=4 * U_DOWN, h=DC * halves))

    phase("ada", blocks=2, adds=dict(unit=2 * DC, ada=2))
    for l in range(2):
        tokens = TOK if l == 0 else LAT
        halves = tokens // LAT
        tiles = tokens // P
        swiglu(l, "ffn1", TOK, 0 if l else 5)
        norm("mix", DC, TOK, 2, True, l)
        phase("mix_in", layer=l, tokens=tokens, tiles=tiles,
              adds=dict(unit=U_MIX, acc=MIX_FM + tiles, evac=MIX_FM + tiles))
        norm("q_lat", QC, tokens, 1, False, l)
        norm("kv_lat", KC, TOK, 1, False, l)
        phase("values", layer=l, tokens=tokens, adds=dict(unit=1, values=4))
        phase("gating", layer=l, tokens=tokens, tiles=tiles, adds=dict(sg=1))
        phase("heads", layer=l, tokens=tokens, tiles=tiles, ada=HEADS - 1,
              adds=dict(unit=(HEADS - 1) * DC, ada=HEADS - 1, head=HEADS, headtile=HEADS * tiles))
        phase("turn", layer=l, tokens=tokens, tiles=tiles, adds=dict(merge=4))
        norm("attn", 4, tokens, 1, False, l)
        norm("sg", 2, tokens, 1, False, l)
        norm("cv", 2, tokens, 1, False, l)
        phase("down", layer=l, which="mix", tokens=tokens, n=U_OUT, src="merged", glu_end=0,
              adds=dict(unit=U_OUT, out=4 * U_OUT, h=DC * halves))
        swiglu(l, "ffn2", tokens, 0)
    for l in range(2, 4):
        tokens = TOK if l == 2 else LAT
        halves, tiles = tokens // LAT, tokens // P
        norm("norm1", DC, TOK, 2, True, l)
        phase("gates", layer=l, adds=dict(unit=1 + 2 * 4, gates=1))
        phase("pairs", layer=l, tokens=tokens, tiles=tiles, adds=dict(pair=HP, pairtile=2 * HP * tiles))
        phase("down", layer=l, which="mix2", tokens=tokens, n=U_OUT, src="merged", glu_end=0,
              adds=dict(unit=U_OUT, out=4 * U_OUT, h=DC * halves))
        norm("norm2", DC, tokens, halves, True, l)
        phase("mlp", layer=l, tokens=tokens, adds=dict(unit=MC, acc=MC, silu=MC, glu=MC))
        phase("down", layer=l, which="mlp", tokens=tokens, n=MC, src="hidden", glu_end=count["glu"],
              adds=dict(unit=MC, out=4 * MC, h=DC * halves))
    norm("final", DC, LAT, 1, False, 4)
    return plan, count


PLAN, TOTAL = make_plan()


def build(nc, stream, head_w, pair_m, pair_n, na_bias, sg_w, masks, consts, params, xT, ctxT, ctx2T, outT):
    units = TOTAL["unit"]
    with ExitStack() as ctx:
        def sb(name, shape):
            return ctx.enter_context(nc.sbuf_tensor(name, shape, F32))

        def sem(name):
            return ctx.enter_context(nc.semaphore(name))

        h = sb("h", [P, DC, TOK])
        xn = sb("xn", [P, DC, TOK])
        ring = sb("ring", [P, RING, UNIT])
        arena = sb("arena", [P, 32, TOK])
        cst = sb("cst", [P, N_CONSTS])
        par = sb("par", [P, N_COLS])
        cond = sb("cond", [P, DC, 32])
        mod = sb("mod", [P, sum(ADA) * DC * 4])
        gain = sb("gain", [P, 16])
        gate = sb("gate", [P, 16])
        eps = sb("eps", [P, 1])
        root_table = sb("root_table", [1, 1])
        sa = sb("sa", [P, 2, TOK])
        std = sb("std", [P, P])
        rstd = sb("rstd", [P, 3, P])
        adarow = sb("adarow", [P, 512])
        mix = sb("mix", [P, 6720])
        mix_at = [0]

        def carve(*shape):
            n = int(np.prod(shape))
            part = mix[:, mix_at[0]:mix_at[0] + n]
            mix_at[0] += n
            if len(shape) == 1:
                return part
            names = "abcd"[:len(shape)]
            return part.rearrange(f"p ({' '.join(names)}) -> p {' '.join(names)}",
                                  **{k: v for k, v in zip(names[1:], shape[1:])})
        qkraw = sb("qkraw", [P, 2, TOK])
        qkn = sb("qkn", [P, 2, TOK])
        qkt = sb("qkt", [P, 2, TOK])
        probs = sb("probs", [P, 2, TOK])
        probsT = sb("probsT", [P, 2, TOK])
        nmax = sb("nmax", [P, 4])
        rsum = sb("rsum", [P, 4])
        rinv = sb("rinv", [P, 4])
        gqs = sb("gqs", [P, 1])
        small = sb("small", [P, 64])
        headw = carve(HW)
        attn_tok = carve(4, HEADS * VD)
        vpad = carve(4, 4, P)
        sgw = carve(6 * P)
        zc = carve(2, 2, LAT + 2)
        mix_at[0] = 0
        maskt = carve(2, 4, TOK)
        nabias = carve(2, 2, LAT)
        osig = carve(TOK)
        sel = carve(4, P)[0:64]
        tokn = carve(4, P)
        tok = sb("tok", [P, 4, P])
        qkna = sa
        wt0 = sb("wt0", [P, 2, TOK])
        PS = ctx.enter_context(nc.psum_tensor("PS", [P, 8, 512], F32))

        qlat, kvlat = arena[:, 0:3, :], arena[:, 3:5, :]
        cv = arena[:, 5:11, :]
        sgu = arena[:, 11:13, :]
        merged = arena[:, 13:21, :]
        sgv = arena[:, 21:23, :].rearrange("p a (b n) -> p (a b) n", n=SG)
        sgt = arena[:, 23:25, :]
        sq = arena[:, 24:32, :]
        hval = arena[:, 25:29, :]
        hqk = arena[:, 29:31, :]
        hroots = arena[:, 31, :].rearrange("p (r j n) -> p r j n", r=2, j=2)
        hstd, hrstd = hroots[:, 0], hroots[:, 1]
        hidden = arena
        merged2 = arena[:, 0:8, :]
        g_a = arena[0:64, 8, :]
        gcol = arena[:, 9, :].rearrange("p (t e d h) -> p t e d h", t=4, e=2, d=2)
        pairw = arena[:, 10:20, :].rearrange("p (j a) n -> p j (a n)", a=2)
        vall = arena[:, 20:28, :].rearrange("p (m t) n -> p m t n", m=2)
        g_soft, g_f, g_b, g_m = (arena[0:64, 28 + j, :] for j in range(4))
        g_guard = g_f

        def const(name):
            o, w = CONSTS[name]
            return cst[:, o:o + w]

        def col(name, l, j=0, w=1):
            o, _ = COLS[(name, l) if l is not None else name]
            return par[:, o + j:o + j + w]

        ident, ones = const("ident"), const("ones")

        weights_in = [sem(f"weights_in{s}") for s in range(RING)]
        weights_used = sem("weights_used")
        params_in = sem("params_in")
        x_in = sem("x_in")
        ctx2_in = sem("ctx2_in")
        sgw_in = sem("sgw_in")
        headw_in = sem("headw_in")
        setup_done = sem("setup_done")
        cond_ready = sem("cond_ready")
        ada_mm = sem("ada_mm")
        ada_row = sem("ada_row")
        ada_turned = sem("ada_turned")
        ada_done = sem("ada_done")
        acc_ready = sem("acc_ready")
        acc_evacuated = sem("acc_evacuated")
        silu_done = sem("silu_done")
        glu_done = sem("glu_done")
        out_ready = sem("out_ready")
        h_ready = sem("h_ready")
        norm_sq = sem("norm_sq")
        norm_sum = sem("norm_sum")
        norm_std = sem("norm_std")
        norm_rstd = sem("norm_rstd")
        norm_spread = sem("norm_spread")
        norm_scaled = sem("norm_scaled")
        norm_out = sem("norm_out")
        dve_chain = sem("dve_chain")
        act_chain = sem("act_chain")
        sg_var = sem("sg_var")
        sg_std = sem("sg_std")
        sg_v = sem("sg_v")
        sg_mixed = sem("sg_mixed")
        sg_done = sem("sg_done")
        head_qk = sem("head_qk")
        query_gain = sem("query_gain")
        value_ready = sem("value_ready")
        head_raw = sem("head_raw")
        value_copied = sem("value_copied")
        head_sq = sem("head_sq")
        head_ss = sem("head_ss")
        head_std = sem("head_std")
        head_rstd = sem("head_rstd")
        head_rot = sem("head_rot")
        head_rotated = sem("head_rotated")
        head_spread = sem("head_spread")
        kpe_rot = sem("kpe_rot")
        kpe_rotated = sem("kpe_rotated")
        head_rope = sem("head_rope")
        score_ready = sem("score_ready")
        max_ready = sem("max_ready")
        exp_done = sem("exp_done")
        probs_turned = sem("probs_turned")
        probsT_ready = sem("probsT_ready")
        pv_ready = sem("pv_ready")
        attn_done = sem("attn_done")
        attn_turned = sem("attn_turned")
        merge_ready = sem("merge_ready")
        out_done = sem("out_done")
        relu_read = silu_done
        masks_in = sem("masks_in")
        pairm_in = sem("pairm_in")
        pairn_in = sem("pairn_in")
        bias_in = sem("bias_in")
        gate_mm = sem("gate_mm")
        gate_softplus = sem("gate_softplus")
        gate_rows = sem("gate_rows")
        gate_guard = sem("gate_guard")
        gate_turned = sem("gate_turned")
        gate_cols = sem("gate_cols")
        v_acc = sem("v_acc")
        v_copied = sem("v_copied")
        pm_acc = sem("pm_acc")
        pm_copied = sem("pm_copied")
        pm_rot = sem("pm_rot")
        pm_rope = sem("pm_rope")
        pm_sel = sem("pm_sel")
        pm_arow = sem("pm_arow")
        pm_score = sem("pm_score")
        pm_logw = sem("pm_logw")
        pm_w = sem("pm_w")
        pm_p = sem("pm_p")
        pm_turned = sem("pm_turned")
        pm_pT = sem("pm_pT")
        pm_pv = sem("pm_pv")
        pm_o = sem("pm_o")
        pm_var = sem("pm_var")
        pm_std = sem("pm_std")
        pm_normed = sem("pm_normed")
        pm_final = sem("pm_final")
        pm_fm = sem("pm_fm")
        na_acc = sem("na_acc")
        na_copied = sem("na_copied")
        na_score = sem("na_score")
        na_max = sem("na_max")
        na_exp = sem("na_exp")
        na_turned = sem("na_turned")
        na_pT = sem("na_pT")
        na_pv = sem("na_pv")
        na_o = sem("na_o")
        na_fm = sem("na_fm")
        pair_done = sem("pair_done")

        def mod_of(l, v):
            at = (ADA_AT[l] + v) * DC * 4
            pair = slice(0, 2) if l < 2 else slice(2, 4)
            return mod[:, at:at + DC * 4].rearrange("p (c j) -> p c j", j=4)[:, :, pair]

        def norm_spec(ph):
            l = ph.layer
            s = NormSpec()
            s.dim = ph.chunks * P
            pieces = HALVES[:ph.pieces] if ph.pieces == ph.tokens // LAT and ph.shifted else ((0, ph.tokens, 0),)
            s.pieces = pieces
            if ph.shifted:
                s.src = h
                s.dst = xn
                s.bank = out_bank(0)
                k = {"ffn1": 0, "mix": 1, "ffn2": 2, "norm1": 0, "norm2": 1}[ph.what]
                s.scale = mod_of(l, 3 * k + 1)
                s.blocks = ADA_AT[l] + 3 * k + 2
                s.g = col({"ffn1": "g_ffn1", "mix": "g_mix", "ffn2": "g_ffn2", "norm1": "norm1_g",
                           "norm2": "norm2_g"}[ph.what], l, 0, DC)
                s.gain = lambda c, cnd: gain[:, 2 * c + cnd:2 * c + cnd + 1]
                s.shift = lambda c, cnd: mod_of(l, 3 * k)[:, c, cnd:cnd + 1]
            elif ph.what == "final":
                s.src, s.dst, s.bank = h, xn, out_bank(0)
                s.gain = lambda c, cnd: col("final_g", None, c)
            else:
                src, name, j, s.bank = {"q_lat": (qlat, "g_q_lat", 0, 0), "kv_lat": (kvlat, "g_kv_lat", 0, 1),
                                        "attn": (merged[:, 0:4, :], "g_out", 0, MERGED_BANKS[0]),
                                        "sg": (merged[:, 4:6, :], "g_out", 4, MERGED_BANKS[1]),
                                        "cv": (merged[:, 6:8, :], "g_out", 6, MERGED_BANKS[2])}[ph.what]
                s.src = s.dst = src
                s.gain = lambda c, cnd: col(name, l, j + c)
            return s

        def in_a_row(ph):
            i = PLAN.index(ph)
            if i + 1 < len(PLAN) and PLAN[i + 1].kind == "norm":
                return []
            first = i
            while PLAN[first - 1].kind == "norm":
                first -= 1
            return PLAN[first:i + 1]

        def out_bank(m):
            return (m + 4) % 8

        def h_wait(eng, ph, c):
            if ph.at.h == 0:
                eng.wait_ge(x_in, 32)
            else:
                last = last_down(ph)
                eng.wait_ge(h_ready, last.at.h + (c + 1) * (last.tokens // LAT))
                if ph.layer == 2:
                    eng.wait_ge(ctx2_in, 16)

        def last_down(ph):
            return [q for q in PLAN[:PLAN.index(ph)] if q.kind == "down"][-1]

        block = ctx.enter_context(nc.Block())

        @block.sync
        def _(sp):
            for u in range(RING):
                sp.dma_start(ring[:, u, :], stream[u]).then_inc(weights_in[u], 16)
            whole = units // RING
            with sp.Fori(1, whole) as i:
                for s in range(RING):
                    sp.wait_ge(weights_used, i * RING + (s - RING + 2))
                    sp.dma_start(ring[:, s, :], stream[bass.ds(i * RING + s, 1)].rearrange("o p n -> p (o n)"))\
                        .then_inc(weights_in[s], 16)
            for u in range(whole * RING, units):
                sp.wait_ge(weights_used, u - RING + 2)
                sp.dma_start(ring[:, u % RING, :], stream[u]).then_inc(weights_in[u % RING], 16)
            for c in range(DC):
                sp.wait_ge(norm_scaled, TOTAL["scaled"] - DC + c + 1)
                sp.dma_start(outT[c * P:(c + 1) * P, :], xn[:, c, 0:LAT]).then_inc(out_done, 16)
            sp.wait_ge(out_done, 16 * DC)

        @block.gpsimd
        def _(pool):
            pool.dma_start(sgw[:, :], sg_w[0]).then_inc(sgw_in, 16)
            for ph in PLAN:
                if ph.kind == "gating" and ph.layer == 1:
                    pool.wait_ge(sg_done, ph.at.sg)
                    pool.dma_start(sgw[:, :], sg_w[1]).then_inc(sgw_in, 16)
                if ph.kind == "heads":
                    with pool.Fori(0, HEADS) as i:
                        pool.wait_ge(head_qk, i * 2 + (2 * ph.at.head + CREDIT))
                        pool.dma_start(headw[:, :], head_w[bass.ds(i + ph.at.head, 1)]
                                       .rearrange("o p n -> p (o n)")).then_inc(headw_in, 16)
                if ph.kind == "norm" and ph.what == "q_lat" and ph.layer == 1:
                    pool.wait_ge(norm_scaled, ph.at.scaled)
                    pool.dma_start(h[:, :, LAT:TOK], ctx2T.rearrange("(c p) t -> p c t", p=P)).then_inc(ctx2_in, 16)
                if ph.kind == "gates" and ph.layer == 2:
                    pool.wait_ge(gate_mm, 1)
                    pool.dma_start(maskt[:, :, :, :], masks).then_inc(masks_in, 16)
                if ph.kind == "pairs":
                    Q0 = ph.at.pair
                    pool.wait_ge(gate_mm, 2 * ph.at.gates)
                    with pool.Fori(0, HP) as i:
                        pool.wait_ge(pm_acc, i * 3 + (3 * Q0 + CREDIT))
                        pool.dma_start(pairw[:, 0:3, :].rearrange("p j n -> p (j n)"),
                                       pair_m[bass.ds(i + Q0, 1)].rearrange("o p n -> p (o n)")).then_inc(pairm_in, 16)
                        pool.wait_ge(na_acc, i * 2 + (2 * Q0 + CREDIT))
                        pool.dma_start(pairw[:, 3:5, :].rearrange("p j n -> p (j n)"),
                                       pair_n[bass.ds(i + Q0, 1)].rearrange("o p n -> p (o n)")).then_inc(pairn_in, 16)
                        pool.wait_ge(pair_done, i + (Q0 + CREDIT))
                        pool.dma_start(nabias.rearrange("p a b n -> p (a b n)"),
                                       na_bias[bass.ds(i + Q0, 1)].rearrange("o p n -> p (o n)")).then_inc(bias_in, 16)

        @block.tensor
        def _(pe):
            def unit_in(u0, j, i=0, rounds=1):
                u = u0 + j
                pe.wait_ge(weights_in[u % RING], i * (16 * rounds) + 16 * (u // RING + 1))
                return u % RING

            def ada_units(ph, block, j, k, i=0, rounds=1):
                if k == 0:
                    pe.wait_ge(ada_row, i + (ph.at.ada + block))
                for kk in range(2):
                    s = unit_in(ph.at.unit, j + kk, i, rounds)
                    for half in range(2):
                        q = 32 * (2 * kk + half)
                        m = pe.matmul(PS[q:q + 32, 5, :], cond[:, k + kk, :], ring[:, s, half * 512:half * 512 + 512],
                                      start=k == 0, stop=k == DC - 2)
                        if half == 0:
                            m.then_inc(weights_used, 1)
                if k == DC - 2:
                    m.then_inc(ada_mm, 1)

            def ada_turn(ph, block, i=0):
                pe.wait_ge(ada_done, i + (ph.at.ada + block))
                pe.wait_ge(ada_row, i + (ph.at.ada + block + 1))
                for c in range(4):
                    m = pe.matmul(PS[:, 6, 8 * c:8 * c + 8], adarow[:, c * P:(c + 1) * P], const("ada_sel"),
                                  start=True, stop=True)
                m.then_inc(ada_turned, 1)

            def ada(ph):
                with pe.Fori(0, ph.blocks) as i:
                    for k in range(0, DC, 2):
                        ada_units(ph, 0, k, k, i)
                    ada_turn(ph, 0, i)

            def norm(ph):
                s = norm_spec(ph)
                if ph.at.std:
                    pe.wait_ge(norm_std, ph.at.std)
                for c in range(ph.chunks):
                    pe.wait_ge(norm_sq, ph.at.sq + c + 1)
                    for t in range(ph.tokens // P):
                        m = pe.matmul(PS[32 * t:32 * t + 32, s.bank, 0:P], ones[:, 0:32], sq[:, c, t * P:(t + 1) * P],
                                      start=c == 0, stop=c == ph.chunks - 1)
                m.then_inc(norm_sum, 1)
                if ph.ada:
                    pe.wait_ge(h_ready, ph.at.h)
                    ada_units(ph, 0, 0, 0)
                    ada_units(ph, 0, 2, 2)
                for n, q in enumerate(in_a_row(ph)):
                    pe.wait_ge(norm_rstd, q.at.rstd + 1)
                    spread(rstd[:, n, :], norm_spec(q).bank, q.tokens).then_inc(norm_spread, 1)
                if ph.ada:
                    ada_units(ph, 0, 4, 4)
                    ada_units(ph, 0, 6, 6)

            def spread(src, bank, tokens):
                rows = tokens // 4
                for t in range(tokens // P):
                    m = pe.matmul(PS[:, bank, t * P:(t + 1) * P],
                                  ident[0:rows, 32 * t:32 * t + 1].broadcast_to([rows, P]), src[0:rows, :],
                                  start=True, stop=True)
                return m

            def xn_in(ph, k):
                last = PLAN[PLAN.index(ph) - 1]
                if k == DC - 2 and last.ada:
                    ada_turn(last, 0)
                pe.wait_ge(norm_out, last.at.nout + (k + 1) * last.pieces)

            def fm_unit(s, bank, tokens, first=None):
                for k in range(DC):
                    if first:
                        xn_in(first, k)
                    m = pe.matmul(PS[:, bank, 0:tokens], ring[:, s, k * P:(k + 1) * P], xn[:, k, 0:tokens],
                                  start=k == 0, stop=k == DC - 1)
                    if k == 0:
                        m.then_inc(weights_used, 1)
                m.then_inc(acc_ready, 1)

            def swiglu(ph):
                head = U_SWIGLU % RING

                def pair(i, j, at, rounds=1, between=None):
                    pe.wait_ge(glu_done, i * (RING // 2) + (ph.at.glu + j - 1))
                    for e in range(2):
                        s = unit_in(ph.at.unit, at + e, i, rounds)
                        fm_unit(s, 2 * (j % 2) + e, ph.tokens, ph if at + e == 0 else None)
                        if e == 0 and between:
                            between()
                for j in range(head // 2):
                    pair(0, j, 2 * j)
                if not ph.ada:
                    with pe.Fori(0, U_SWIGLU // RING) as i:
                        for j in range(RING // 2):
                            pair(i, head // 2 + j, head + 2 * j)
                    return
                with pe.Fori(0, ph.ada) as i:
                    pair(i, head // 2, head, 2)
                    ada_units(ph, 0, head + 2, 0, i, 2)
                    pair(i, head // 2 + 1, head + 4, 2)
                    ada_units(ph, 0, head + 6, 2, i, 2)
                    pair(i, head // 2 + 2, head + 8, 2)
                    ada_units(ph, 0, head + 10, 4, i, 2)
                    ada_units(ph, 0, head + 12, 6, i, 2)
                    pair(i, head // 2 + 3, head + 14, 2, between=lambda: ada_turn(ph, 0, i))

            def down(ph):
                src = hidden if ph.src == "hidden" else merged if ph.layer < 2 else merged2
                head = ph.n % RING or RING

                def rows(i, k):
                    s = unit_in(ph.at.unit, k, i)
                    if ph.src == "hidden":
                        pe.wait_ge(glu_done, i * RING + (ph.glu_end - ph.n + k + 1))
                    if ph.src == "merged" and ph.layer < 2:
                        pe.wait_ge(norm_scaled, ph.at.scaled - DC + k + 1)
                    for m_ in range(DC):
                        if ph.src == "merged" and ph.layer < 2 and k == 0 and out_bank(m_) in MERGED_BANKS:
                            group = MERGED_BANKS.index(out_bank(m_))
                            pe.wait_ge(norm_scaled, ph.at.scaled - DC + (4, 6, 8)[group])
                        if ph.src == "hidden" and isinstance(i, int) and k == 0 and m_ == 1:
                            pe.wait_ge(ada_done, ph.at.ada)
                        if ph.src == "hidden" and isinstance(i, int) and k == 0 and m_ == 4:
                            pe.wait_ge(glu_done, ph.glu_end)
                        rhs = src[:, k, 0:ph.tokens] if isinstance(i, int) else \
                            src[:, bass.ds(i * RING + k, 1), 0:ph.tokens].rearrange("p o n -> p (o n)")
                        m = pe.matmul(PS[:, out_bank(m_), 0:ph.tokens], ring[:, s, m_ * P:(m_ + 1) * P], rhs,
                                      start=isinstance(i, int) and k == 0, stop=True, skip_group_check=True)
                        if m_ == 0:
                            m.then_inc(weights_used, 1)
                        if m_ % 2:
                            m.then_inc(out_ready, 1)
                if ph.src == "merged" and ph.layer >= 2:
                    pe.wait_ge(pair_done, ph.at.pair + CREDIT)
                for k in range(head):
                    rows(0, k)
                if ph.n > head:
                    with pe.Fori(0, (ph.n - head) // RING) as i:
                        for k in range(RING):
                            rows(i, head + k)

            def mix_in(ph):
                for j in range(MIX_FM):
                    pe.wait_ge(acc_evacuated, ph.at.evac + j - 3)
                    tokens = TOK if QC <= j <= QC + KC else ph.tokens
                    fm_unit(unit_in(ph.at.unit, j), j % 4, tokens, ph if j == 0 else None)
                s = [unit_in(ph.at.unit, MIX_FM + e) for e in range(2)]
                for t in range(ph.tiles):
                    j = MIX_FM + t
                    pe.wait_ge(acc_evacuated, ph.at.evac + j - 3)
                    for k in range(DC):
                        m = pe.matmul(PS[:, j % 4, 0:SG], xn[:, k, t * P:(t + 1) * P],
                                      ring[:, s[k // 4], (k % 4) * SG:(k % 4 + 1) * SG],
                                      start=k == 0, stop=k == DC - 1)
                        if (t, k) in ((0, 0), (ph.tiles - 1, 4)):
                            m.then_inc(weights_used, 1)
                    m.then_inc(acc_ready, 1)

            def project(ph, p, j):
                if j == 0:
                    pe.wait_ge(headw_in, p * 16 + 16 * (ph.at.head + 1))
                src, n, o, cols = ((qlat, QC, 0, ph.tokens), (kvlat, KC, QC, TOK))[j]
                for k in range(n):
                    m = pe.matmul(PS[:, j, 0:cols], headw[:, (o + k) * P:(o + k + 1) * P], src[:, k, 0:cols],
                                  start=k == 0, stop=k == n - 1)
                m.then_inc(head_qk, 1)

            def value_tile(s, t):
                for k in range(KC):
                    m = pe.matmul(PS[:, VALUE_BANKS[t], :], kvlat[:, k, t * P:(t + 1) * P],
                                  ring[:, s, k * 512:(k + 1) * 512], start=k == 0, stop=k == KC - 1)
                    if (t, k) == (0, 0):
                        m.then_inc(weights_used, 1)
                m.then_inc(value_ready, 1)

            def values(ph):
                pe.wait_ge(norm_scaled, ph.at.scaled)
                project(ph, 0, 0)
                project(ph, 0, 1)
                s = unit_in(ph.at.unit, 0)
                for t in range(2):
                    value_tile(s, t)

            def gating(ph):
                pe.wait_ge(sgw_in, 16 * (ph.at.sg + 1))
                pe.wait_ge(ada_done, ph.at.ada)
                pe.wait_ge(sg_v, ph.at.sg + 1)
                for t in range(ph.tiles):
                    for cb in range(2):
                        for e in range(2):
                            g = 2 * cb + e
                            m = pe.matmul(PS[:, 5 + cb, t * P:(t + 1) * P], vpad[:, t, g, :],
                                          sgw[:, g * P:(g + 1) * P], start=e == 0, stop=e == 1)
                m.then_inc(sg_mixed, 1)

            def heads(ph):
                tiles, H0, T0 = ph.tiles, ph.at.head, ph.at.headtile

                def rotate(j, sem_):
                    pe.matmul(PS[:, 7 - j, 0:LAT], const("rot1"), qkraw[:, j, 0:LAT], start=True, stop=True)\
                        .then_inc(sem_, 1)

                def sums(p):
                    pe.wait_ge(head_raw, p * 2 + (2 * H0 + 1))
                    if not isinstance(p, int):
                        pe.wait_ge(attn_done, p * tiles + (T0 - tiles + CREDIT))
                    rotate(0, head_rot)
                    for j in range(2):
                        pe.wait_ge(head_sq, p * 2 + (2 * H0 + j + 1))
                        for t in range(4 if j else tiles):
                            m = pe.matmul(PS[32 * t:32 * t + 32, j, 0:P], ones[:, 0:32],
                                          qkt[:, j, t * P:(t + 1) * P], start=True, stop=True)
                        m.then_inc(head_ss, 1)

                def spread_roots(p):
                    pe.wait_ge(head_rstd, p * 2 + (2 * H0 + 2))
                    for j in range(2):
                        m = spread(hrstd[:, j, :], j, TOK if j else ph.tokens)
                    m.then_inc(head_spread, 1)

                def scores(i, t):
                    keys = 0 if t < 2 else LAT
                    if t >= 2:
                        pe.wait_ge(exp_done, i * tiles + (T0 + t - 1))
                    pe.matmul(PS[:, 2 + t % 2, keys:TOK], hqk[:, 0, t * P:(t + 1) * P], hqk[:, 1, keys:TOK],
                              start=True, stop=True).then_inc(score_ready, 1)

                def turned(i, t):
                    pe.wait_ge(exp_done, i * tiles + (T0 + t + 1))
                    for k in range(0 if t < 2 else 2, 4):
                        m = pe.transpose(PS[:, 4, k * P:(k + 1) * P], probs[:, t % 2, k * P:(k + 1) * P],
                                         ident)
                    m.then_inc(probs_turned, 1)

                def values(i, t, last):
                    k0 = 0 if t < 2 else 2
                    pe.wait_ge(probsT_ready, i * tiles + (T0 + t + 1))
                    pe.wait_ge(attn_done, i * tiles + (T0 + t + CREDIT))
                    if t == 0 and not last:
                        pe.wait_ge(head_rotated, i + (H0 + 2))
                    for k in range(k0, 4):
                        m = pe.matmul(PS[:, 7, 0:VD], probsT[:, t % 2, k * P:(k + 1) * P],
                                      hval[:, k, bass.ds(i * VD, VD)], start=k == k0, stop=k == 3)
                    m.then_inc(pv_ready, 1)

                def iteration(i, last):
                    fill = (lambda k: None) if last else (lambda k: ada_units(ph, 0, k, k, i))
                    pe.wait_ge(head_rope, i + (H0 + 1))
                    scores(i, 0)
                    scores(i, 1)
                    if not last:
                        project(ph, i + 1, 0)
                        project(ph, i + 1, 1)
                    if tiles == 2:
                        fill(0)
                    turned(i, 0)
                    if not last:
                        sums(i + 1)
                    fill(0 if tiles > 2 else 2)
                    values(i, 0, last)
                    if tiles > 2:
                        scores(i, 2)
                        turned(i, 1)
                        scores(i, 3)
                        fill(2)
                        values(i, 1, last)
                        fill(4)
                        turned(i, 2)
                    else:
                        fill(4)
                        turned(i, 1)
                    fill(6)
                    if not last:
                        spread_roots(i + 1)
                    if tiles > 2:
                        values(i, 2, last)
                        turned(i, 3)
                        if not last:
                            ada_turn(ph, 0, i)
                    values(i, tiles - 1, last)
                    if tiles == 2 and not last:
                        ada_turn(ph, 0, i)

                for t in range(2, 4):
                    value_tile((ph.at.unit - 1) % RING, t)
                pe.wait_ge(sg_done, ph.at.sg)
                pe.wait_ge(head_raw, 2 * H0 + 2)
                rotate(1, kpe_rot)
                pe.wait_ge(value_copied, ph.at.values)
                sums(0)
                spread_roots(0)
                with pe.Fori(0, HEADS - 1) as i:
                    iteration(i, False)
                iteration(HEADS - 1, True)

            def turn(ph):
                pe.wait_ge(attn_done, ph.at.headtile + CREDIT)
                for c in range(4):
                    for t in range(ph.tiles):
                        m = pe.transpose(PS[:, c, t * P:(t + 1) * P], attn_tok[:, t, c * P:(c + 1) * P], ident)
                    m.then_inc(attn_turned, 1)

            def gates(ph):
                s = unit_in(ph.at.unit, 0)
                for e in range(2):
                    for k in range(DC):
                        if e == 0:
                            xn_in(ph, k)
                        m = pe.matmul(PS[0:64, e, :], ring[:, s, k * P + 64 * e:k * P + 64 * e + 64], xn[:, k, :],
                                      start=k == 0, stop=k == DC - 1)
                        if e == 0 and k == 0:
                            m.then_inc(weights_used, 1)
                    m.then_inc(gate_mm, 1)
                pe.wait_ge(ada_done, ph.at.ada)
                for mixer in range(2):
                    for u in range(4):
                        s = unit_in(ph.at.unit, 1 + 4 * mixer + u)
                        for t in range(4):
                            if mixer and u == 0:
                                pe.wait_ge(v_copied, 8 * ph.at.gates + t + 1)
                            for k in range(2):
                                m = pe.matmul(PS[:, 4 + t, :], xn[:, 2 * u + k, t * P:(t + 1) * P],
                                              ring[:, s, k * 512:(k + 1) * 512], start=u == 0 and k == 0,
                                              stop=u == 3 and k == 1)
                                if t == 0 and k == 0:
                                    m.then_inc(weights_used, 1)
                            if u == 3:
                                m.then_inc(v_acc, 1)

            def pair_product(ph, j, k, bank, tokens, weights):
                return pe.matmul(PS[:, bank, 0:tokens], pairw[:, weights, k * P:(k + 1) * P], xn[:, k, 0:tokens],
                                 start=k == 0, stop=k == DC - 1)

            def mlstm_products(ph, p, a, b):
                Q = ph.at.pair
                for x in range(a, b):
                    j, k = x // DC, x % DC
                    if x == 0:
                        pe.wait_ge(pairm_in, p * 16 + 16 * (Q + 1))
                    if x == 2 * DC:
                        pe.wait_ge(pm_copied, p * 3 + (3 * Q + 1))
                    if x == ROTATE_AT:
                        pe.wait_ge(pm_copied, p * 3 + (3 * Q + 2))
                        for e in range(2):
                            m = pe.matmul(PS[:, 3, e * LAT:(e + 1) * LAT], const("rot2"), qkraw[:, e, 0:LAT],
                                          start=True, stop=True)
                        m.then_inc(pm_rot, 1)
                    m = pair_product(ph, j, k, 2 + j % 2, TOK if j == 1 else ph.tokens, j)
                    if k == DC - 1:
                        m.then_inc(pm_acc, 1)

            def neighbour_products(ph, p, a, b):
                Q = ph.at.pair
                for x in range(a, b):
                    j, k = x // DC, x % DC
                    if x == 0:
                        pe.wait_ge(pairn_in, p * 16 + 16 * (Q + 1))
                        pe.wait_ge(pm_copied, p * 3 + (3 * Q + 3))
                    m = pair_product(ph, j, k, 2 + j, TOK if j else ph.tokens, 3 + j)
                    if k == DC - 1:
                        m.then_inc(na_acc, 1)

            def pairs(ph):
                tiles, Q0, N0, per = ph.tiles, ph.at.pair, ph.at.pairtile, 2 * ph.tiles
                pe.wait_ge(v_copied, 8 * ph.at.gates)
                mlstm_products(ph, 0, 0, 3 * DC)
                pe.wait_ge(gate_guard, ph.at.gates)
                for t in range(4):
                    for e, g in enumerate((g_m, g_guard)):
                        m = pe.transpose(PS[:, 0, (2 * t + e) * 64:(2 * t + e + 1) * 64], g[:, t * P:(t + 1) * P],
                                         ident[0:64, 0:64])
                m.then_inc(gate_turned, 1)

                def arow(p, e):
                    for d in range(2):
                        m = pe.matmul(PS[:, 4 + d, :], sel[:, 2 * d + e, :], g_a, start=True, stop=True)
                    m.then_inc(pm_arow, 1)

                def score(i, n, qk, free, ready):
                    e, t = n // tiles, n % tiles
                    keys = 0 if t < 2 else LAT
                    if n >= 2:
                        pe.wait_ge(free, i * per + (N0 + n - 1))
                    r = slice(64 * e, 64 * e + 64)
                    pe.matmul(PS[:, 6 + n % 2, keys:TOK], qk[r, 0, t * P:(t + 1) * P], qk[r, 1, keys:TOK],
                              start=True, stop=True).then_inc(ready, 1)

                def turned(i, n, made, copied, turned_):
                    k0 = 0 if n % tiles < 2 else 2
                    pe.wait_ge(made, i * per + (N0 + n + 1))
                    if n >= 1:
                        pe.wait_ge(copied, i * per + (N0 + n))
                    for k in range(k0, 4):
                        m = pe.transpose(PS[:, 0, k * P:(k + 1) * P], probs[:, n % 2, k * P:(k + 1) * P], ident)
                    m.then_inc(turned_, 1)

                def value(i, n, mixer, copied, left, pv):
                    e, k0 = n // tiles, 0 if n % tiles < 2 else 2
                    if n >= 1:
                        pe.wait_ge(left, i * per + (N0 + n))
                    pe.wait_ge(copied, i * per + (N0 + n + 1))
                    for k in range(k0, 4):
                        m = pe.matmul(PS[:, 1, 0:HD], probsT[:, n % 2, k * P:(k + 1) * P],
                                      vall[:, mixer, k, bass.ds(i * P + e * HD, HD)], start=k == k0, stop=k == 3)
                    m.then_inc(pv, 1)

                def turn_tok(src, bank, sem_):
                    for t in range(tiles):
                        m = pe.transpose(PS[:, bank, t * P:(t + 1) * P], src[:, t, :], ident)
                    m.then_inc(sem_, 1)

                def iteration(i, last):
                    pe.wait_ge(pm_rope, i + (Q0 + 1))
                    step = 2 * DC // per
                    score(i, 0, qkraw, pm_p, pm_score)
                    for n in range(per):
                        if n + 1 < per:
                            score(i, n + 1, qkraw, pm_p, pm_score)
                        neighbour_products(ph, i, n * step, n * step + step // 2)
                        if n == 0:
                            pe.wait_ge(pair_done, i + (Q0 + CREDIT))
                        turned(i, n, pm_p, pm_pT, pm_turned)
                        if n + 2 == tiles:
                            pe.wait_ge(pm_logw, i * per + (N0 + tiles))
                            arow(i, 1)
                        neighbour_products(ph, i, n * step + step // 2, (n + 1) * step)
                        value(i, n, 0, pm_pT, pm_o, pm_pv)
                    step = 3 * DC // per
                    pe.wait_ge(na_copied, i * 2 + (2 * Q0 + 2))
                    score(i, 0, qkna, na_exp, na_score)
                    for n in range(per):
                        if n + 1 < per:
                            score(i, n + 1, qkna, na_exp, na_score)
                        if not last:
                            mlstm_products(ph, i + 1, n * step, n * step + step // 2)
                        turned(i, n, na_exp, na_pT, na_turned)
                        if not last:
                            mlstm_products(ph, i + 1, n * step + step // 2, (n + 1) * step)
                        if n == 0:
                            pe.wait_ge(pm_o, i * per + (N0 + per))
                        value(i, n, 1, na_pT, na_o, na_pv)
                        if n == 1:
                            pe.wait_ge(pm_normed, i + (Q0 + 1))
                            turn_tok(tok, 4, pm_fm)
                        if n == 2 and not last:
                            pe.wait_ge(pm_sel, i + (Q0 + 2))
                            pe.wait_ge(pm_final, i + (Q0 + 1))
                            arow(i + 1, 0)
                    pe.wait_ge(na_o, i * per + (N0 + per))
                    turn_tok(tokn, 0, na_fm)

                pe.wait_ge(pm_sel, Q0 + 1)
                arow(0, 0)
                pe.wait_ge(gate_cols, 2 * ph.at.gates)
                with pe.Fori(0, HP - 1) as i:
                    iteration(i, False)
                iteration(HP - 1, True)

            def mlp(ph):
                def eight(i, first):
                    for j in range(RING):
                        pe.wait_ge(relu_read, i * RING + (ph.at.silu + j - 3))
                        fm_unit(unit_in(ph.at.unit, j, i), j % 4, ph.tokens, ph if first and j == 0 else None)
                eight(0, True)
                with pe.Fori(1, MC // RING) as i:
                    eight(i, False)

            pe.wait_ge(setup_done, 1)
            pe.wait_ge(params_in, 32)
            pe.wait_ge(cond_ready, 1)
            run = dict(ada=ada, norm=norm, swiglu=swiglu, down=down, mix_in=mix_in, values=values, gating=gating,
                       heads=heads, turn=turn, gates=gates, pairs=pairs, mlp=mlp)
            for ph in PLAN:
                run[ph.kind](ph)

        @block.scalar
        def _(act):
            chain = [0]

            def link(ins):
                chain[0] += 1
                ins.then_inc(act_chain, 1)
                act.wait_ge(act_chain, chain[0])

            act.dma_start(cst[:, :], consts).then_inc(params_in, 16)
            act.dma_start(par[:, :], params).then_inc(params_in, 16)
            act.dma_start(h[:, :, 0:LAT], xT.rearrange("(c p) t -> p c t", p=P)).then_inc(x_in, 16)
            act.dma_start(h[:, :, LAT:TOK], ctxT.rearrange("(c p) t -> p c t", p=P)).then_inc(x_in, 16)
            act.wait_ge(params_in, 32)
            act.wait_ge(setup_done, 1)
            act.activation(cond[:, :, 0:4], col("cond", None, 0, 4 * DC).rearrange("p (c j) -> p c j", j=4),
                           ACT.Silu).then_inc(cond_ready, 1)

            def ada_copy(ph, block, i=0):
                act.wait_ge(ada_mm, i + (ph.at.ada + block))
                act.activation(adarow[:, :], PS[:, 5, :], ACT.Copy).then_inc(ada_row, 1)

            def ada(ph):
                with act.Fori(0, ph.blocks) as i:
                    ada_copy(ph, 0, i)

            def norm(ph):
                s = norm_spec(ph)
                if ph.at.sum:
                    act.wait_ge(norm_sum, ph.at.sum)
                link(act.activation(root_table[:, :], eps[0:1, :], ACT.Sqrt))
                for c in range(ph.chunks):
                    if s.src is h:
                        h_wait(act, ph, c)
                    elif ph.what == "sg" or ph.what == "cv":
                        act.wait_ge(sg_done, ph.at.sg)
                    act.activation(sq[:, c, 0:ph.tokens], s.src[:, c, 0:ph.tokens], ACT.Square).then_inc(norm_sq, 1)
                act.wait_ge(norm_sum, ph.at.sum + 1)
                if ph.at.rstd:
                    act.wait_ge(norm_rstd, ph.at.rstd)
                rows = ph.tokens // 4
                act.activation(std[0:rows, :], PS[0:rows, s.bank, 0:P], ACT.Sqrt, bias=eps[0:rows, :],
                               scale=1.0 / s.dim).then_inc(norm_std, 1)
                if ph.shifted:
                    n = 0
                    for c in range(ph.chunks):
                        if c == 2 and ph.ada:
                            ada_copy(ph, 0)
                        for a, b, cnd in s.pieces:
                            n += 1
                            act.wait_ge(norm_scaled, ph.at.scaled + n)
                            act.activation(s.dst[:, c, a:b], s.dst[:, c, a:b], ACT.Identity, bias=s.shift(c, cnd))\
                                .then_inc(norm_out, 1)

            def swiglu(ph):
                head = U_SWIGLU % RING // 2

                def pair(i, j):
                    act.wait_ge(acc_ready, i * RING + (ph.at.acc + 2 * j + 1))
                    act.wait_ge(glu_done, i * (RING // 2) + (ph.at.glu + j - 1))
                    act.activation(sa[:, j % 2, 0:ph.tokens], PS[:, 2 * (j % 2), 0:ph.tokens], ACT.Silu)\
                        .then_inc(silu_done, 1)
                for j in range(head):
                    pair(0, j)
                with act.Fori(0, U_SWIGLU // RING) as i:
                    for j in range(RING // 2):
                        if j == 3 and ph.ada:
                            ada_copy(ph, 0, i)
                        pair(i, head + j)

            def mlp(ph):
                with act.Fori(0, MC // RING) as i:
                    for j in range(RING):
                        act.wait_ge(acc_ready, i * RING + (ph.at.acc + j + 1))
                        act.wait_ge(glu_done, i * RING + (ph.at.glu + j - 1))
                        act.activation(sa[:, j % 2, 0:ph.tokens], PS[:, j % 4, 0:ph.tokens], ACT.Relu)\
                            .then_inc(relu_read, 1)

            def mix_in(ph):
                for j in range(MIX_FM + ph.tiles):
                    act.wait_ge(acc_ready, ph.at.acc + j + 1)
                    bank = PS[:, j % 4, :]
                    if j < QC + KC:
                        n = ph.tokens if j < QC else TOK
                        ins = act.activation(arena[:, j, 0:n], bank[:, 0:n], ACT.Copy)
                    elif j == QC + KC:
                        act.activation(qkraw[64:128, 1, :], bank[64:128, :], ACT.Copy,
                                       scale=col("g_k_head", ph.layer)[64:128, :])
                        ins = act.activation(qkt[64:128, 1, :], bank[64:128, :], ACT.Square)
                    elif j < MIX_FM - 2:
                        ins = act.activation(arena[:, j - 1, 0:ph.tokens], bank[:, 0:ph.tokens], ACT.Copy)
                    elif j < MIX_FM:
                        ins = act.activation(arena[:, j - 1, 0:ph.tokens], bank[:, 0:ph.tokens],
                                             ACT.Gelu_apprx_tanh)
                    else:
                        ins = act.activation(sgv[:, j - MIX_FM, :], bank[:, 0:SG], ACT.Gelu_apprx_tanh)
                    ins.then_inc(acc_evacuated, 1)

            def gating(ph):
                act.wait_ge(sg_var, ph.at.sg + 1)
                act.activation(sgt[:, 1, 0:4 * ph.tiles], sgt[:, 1, 32:32 + 4 * ph.tiles], ACT.Sqrt, bias=eps[:, :],
                               scale=1.0 / 64).then_inc(sg_std, 1)

            def heads(ph):
                tiles, H0, T0 = ph.tiles, ph.at.head, ph.at.headtile
                widths = (ph.tokens, TOK)

                def raw(p):
                    for j, (rows, n, gain_) in enumerate(zip((P, NOPE), widths, (gqs, col("g_k_head", ph.layer)))):
                        act.wait_ge(head_qk, p * 2 + (2 * H0 + j + 1 + CREDIT))
                        act.activation(qkraw[0:rows, j, 0:n], PS[0:rows, j, 0:n], ACT.Copy, scale=gain_[0:rows, :])\
                            .then_inc(head_raw, 1)
                        act.activation(qkt[0:rows, j, 0:n], PS[0:rows, j, 0:n], ACT.Square).then_inc(head_sq, 1)

                def roots(p):
                    for j, n in enumerate(widths):
                        rows = n // 4
                        act.wait_ge(head_ss, p * 2 + (2 * H0 + j + 1))
                        act.activation(hstd[0:rows, j, :], PS[0:rows, j, 0:P], ACT.Sqrt, bias=eps[0:rows, :],
                                       scale=1.0 / QK).then_inc(head_std, 1)

                def exps(i, t):
                    k = 0 if t < 2 else LAT
                    act.wait_ge(max_ready, i * tiles + (T0 + t + 1))
                    act.activation(probs[:, t % 2, k:TOK], PS[:, 2 + t % 2, k:TOK], ACT.Exp,
                                   bias=nmax[:, t:t + 1], accum_out=rsum[:, t:t + 1]).then_inc(exp_done, 1)

                def turned(i, t):
                    k = 0 if t < 2 else LAT
                    act.wait_ge(probs_turned, i * tiles + (T0 + t + 1))
                    act.activation(probsT[:, t % 2, k:TOK], PS[:, 4, k:TOK], ACT.Copy)\
                        .then_inc(probsT_ready, 1)

                def iteration(i, last):
                    exps(i, 0)
                    exps(i, 1)
                    if not last:
                        raw(i + 1)
                    turned(i, 0)
                    if not last:
                        roots(i + 1)
                    if tiles > 2:
                        exps(i, 2)
                        turned(i, 1)
                        exps(i, 3)
                        turned(i, 2)
                        if not last:
                            ada_copy(ph, 0, i)
                    turned(i, tiles - 1)
                    if tiles == 2 and not last:
                        ada_copy(ph, 0, i)

                act.wait_ge(query_gain, ph.layer + 1)
                raw(0)
                for t in range(4):
                    act.wait_ge(value_ready, ph.at.values - 3 + t)
                    act.activation(hval[:, t, :], PS[:, VALUE_BANKS[t], :], ACT.Copy).then_inc(value_copied, 1)
                roots(0)
                with act.Fori(0, HEADS - 1) as i:
                    iteration(i, False)
                iteration(HEADS - 1, True)

            def turn(ph):
                for c in range(4):
                    act.wait_ge(attn_turned, ph.at.merge + c + 1)
                    act.activation(merged[:, c, 0:ph.tokens], PS[:, c, 0:ph.tokens], ACT.Copy)\
                        .then_inc(merge_ready, 1)
                act.wait_ge(merge_ready, ph.at.merge + 4)

            def gates(ph):
                G = ph.at.gates
                act.wait_ge(gate_mm, 2 * G + 2)
                o, _ = COLS[("b_gate", ph.layer)]
                link(act.activation(g_soft, PS[0:64, 1, :], ACT.Abs, bias=par[0:64, o + 1:o + 2]))
                link(act.activation(g_soft, g_soft, ACT.Exp, scale=-1.0))
                act.activation(g_soft, g_soft, ACT.Ln, bias=1.0).then_inc(gate_softplus, 1)
                for mixer in range(2):
                    for t in range(4):
                        act.wait_ge(v_acc, 8 * G + 4 * mixer + t + 1)
                        act.activation(vall[:, mixer, t, :], PS[:, 4 + t, :], ACT.Copy).then_inc(v_copied, 1)

            def pairs(ph):
                tiles, Q0, N0, per, T = ph.tiles, ph.at.pair, ph.at.pairtile, 2 * ph.tiles, ph.tokens
                G = ph.at.gates

                def mlstm_copy(p, j):
                    act.wait_ge(pm_acc, p * 3 + (3 * Q0 + j + 1 + CREDIT))
                    if j == 0:
                        ins = act.activation(qkraw[:, 0, 0:T], PS[:, 2, 0:T], ACT.Copy, scale=float(HD) ** -0.5)
                    elif j == 1:
                        ins = act.activation(qkraw[:, 1, :], PS[:, 3, :], ACT.Copy)
                    else:
                        if not isinstance(p, int) or p:
                            act.wait_ge(pm_final, p + Q0)
                        ins = act.activation(osig[:, 0:T], PS[:, 2, 0:T], ACT.Sigmoid)
                    ins.then_inc(pm_copied, 1)

                def neighbour_copy(p, j):
                    act.wait_ge(na_acc, p * 2 + (2 * Q0 + j + 1 + CREDIT))
                    n = TOK if j else T
                    act.activation(qkna[:, j, 0:n], PS[:, 2 + j, 0:n], ACT.Copy, scale=1.0 if j else float(HD) ** -0.5)\
                        .then_inc(na_copied, 1)

                for j in range(3):
                    mlstm_copy(0, j)
                act.wait_ge(gate_rows, G)
                act.activation(g_guard, g_guard, ACT.Exp, scale=-1.0).then_inc(gate_guard, 1)
                act.wait_ge(gate_turned, G)
                turned = PS[:, 0, :].rearrange("p (t e n) -> p t e n", t=4, e=2)
                cols = arena[:, 9, :].rearrange("p (t e n) -> p t e n", t=4, e=2)
                act.activation(cols[:, :, 0, :], turned[:, :, 0, :], ACT.Copy, scale=-1.0).then_inc(gate_cols, 1)
                act.activation(cols[:, :, 1, :], turned[:, :, 1, :], ACT.Copy).then_inc(gate_cols, 1)

                def transposed(i, n, turned_, pv, sem_):
                    k = 0 if n % tiles < 2 else LAT
                    act.wait_ge(turned_, i * per + (N0 + n + 1))
                    if n >= 2:
                        act.wait_ge(pv, i * per + (N0 + n - 1))
                    act.activation(probsT[:, n % 2, k:TOK], PS[:, 0, k:TOK], ACT.Copy).then_inc(sem_, 1)

                def weigh(i, n):
                    k = 0 if n % tiles < 2 else LAT
                    w = (wt0, qkn)[n % 2]
                    act.wait_ge(pm_logw, i * per + (N0 + n + 1))
                    act.activation(w[:, :, k:TOK], w[:, :, k:TOK], ACT.Exp).then_inc(pm_w, 1)

                def exps(i, n):
                    k = 0 if n % tiles < 2 else LAT
                    act.wait_ge(na_max, i * per + (N0 + n + 1))
                    if n >= 2:
                        act.wait_ge(na_turned, i * per + (N0 + n - 1))
                    act.activation(probs[:, n % 2, k:TOK], PS[:, 6 + n % 2, k:TOK], ACT.Exp,
                                   bias=small[:, 32 + n:33 + n], accum_out=small[:, 40 + n:41 + n])\
                        .then_inc(na_exp, 1)

                def iteration(i, last):
                    step = 2 * DC // per
                    for n in range(per):
                        if n >= 1 and n + 1 < per:
                            weigh(i, n + 1)
                        transposed(i, n, pm_turned, pm_pv, pm_pT)
                        for j in range(2):
                            if n == (DC * (j + 1) - 1) // step:
                                neighbour_copy(i, j)
                        act.wait_ge(pm_pv, i * per + (N0 + n + 1))
                        e, t = n // tiles, n % tiles
                        act.activation(tok[:, t, e * HD:(e + 1) * HD], PS[:, 1, 0:HD], ACT.Copy).then_inc(pm_o, 1)
                    step = 3 * DC // per
                    exps(i, 0)
                    exps(i, 1)
                    for n in range(per):
                        if n >= 1 and n + 1 < per:
                            exps(i, n + 1)
                        transposed(i, n, na_turned, na_pv, na_pT)
                        if n == 0:
                            act.wait_ge(pm_var, i + (Q0 + 1))
                            act.activation(small[:, 16:16 + per], small[:, 8:8 + per], ACT.Sqrt, bias=eps[:, :],
                                           scale=1.0 / HD).then_inc(pm_std, 1)
                        if not last and n == ROTATE_AT // step:
                            weigh(i + 1, 0)
                        if not last and n == per - 1:
                            weigh(i + 1, 1)
                        for j in range(3):
                            if not last and n == (DC * (j + 1) - 1) // step:
                                mlstm_copy(i + 1, j)

                weigh(0, 0)
                weigh(0, 1)
                with act.Fori(0, HP - 1) as i:
                    iteration(i, False)
                iteration(HP - 1, True)

            run = dict(ada=ada, norm=norm, swiglu=swiglu, down=lambda ph: None, mix_in=mix_in,
                       values=lambda ph: None, gating=gating, heads=heads, turn=turn, gates=gates, pairs=pairs, mlp=mlp)
            for ph in PLAN:
                if ph.kind == "norm" and ph.what in ("q_lat", "kv_lat"):
                    act.wait_ge(acc_evacuated, ph.at.evac)
                run[ph.kind](ph)

        @block.vector
        def _(dve):
            chain = [0, None, 0]

            def link(ins):
                chain[0] += 1
                ins.then_inc(dve_chain, 1)
                if chain[1] is None:
                    dve.wait_ge(dve_chain, chain[0])
                else:
                    dve.wait_ge(dve_chain, chain[1] * chain[2] + chain[0])

            def loop(i, per):
                chain[1], chain[2] = i, per
                return chain[0]

            def loop_end(start, times):
                assert chain[0] - start == chain[2], (chain[0] - start, chain[2])
                chain[0] = start + chain[2] * times
                chain[1] = None

            tt = dve.tensor_tensor
            stt = dve.scalar_tensor_tensor
            link(dve.memset(vpad[:, :, :, :], 0.0))
            link(dve.memset(zc[:, :, :, :], 0.0))
            link(dve.memset(cond[:, :, :], 0.0))
            dve.memset(eps[:, :], EPS).then_inc(setup_done, 1)
            dve.sem_inc(glu_done, 2)
            dve.sem_inc(acc_evacuated, 4)
            dve.sem_inc(ada_row, 1)
            dve.sem_inc(ada_done, 1)
            for s in (head_qk, attn_done, pm_acc, na_acc, pair_done):
                dve.sem_inc(s, CREDIT)
            dve.wait_ge(params_in, 32)

            def ada_add(ph, block, i=0):
                ob, _ = COLS["b_ada"]
                first = ph.at.ada - 1 + block
                out = mod[:, bass.ds(i * 32 + 32 * first, 32)]
                bias = par[:, bass.ds(i * DC + (ob + DC * first), DC)]
                dve.wait_ge(ada_turned, i + (first + 1))
                tt(out.rearrange("p (h c j) -> p h c j", h=2, c=4),
                   PS[:, 6, 0:32].rearrange("p (c h j) -> p h c j", c=4, h=2),
                   bias.rearrange("p (h c j) -> p h c j", h=2, j=1).broadcast_to([P, 2, 4, 4]),
                   ALU.add).then_inc(ada_done, 1)

            def ada(ph):
                with dve.Fori(0, ph.blocks) as i:
                    ada_add(ph, 0, i)

            def norm(ph):
                s = norm_spec(ph)
                if ph.shifted:
                    dve.wait_ge(ada_done, s.blocks + 1)
                    if ph.at.scaled:
                        dve.wait_ge(norm_scaled, ph.at.scaled)
                    link(stt(gain.rearrange("p (c j) -> p c j", j=2), s.scale, 1.0,
                             s.g.rearrange("p (c o) -> p c o", o=1).broadcast_to([P, DC, 2]), ALU.add, ALU.mult))
                dve.wait_ge(norm_std, ph.at.std + 1)
                rows = ph.tokens // 4
                place = 0
                while PLAN[PLAN.index(ph) - 1 - place].kind == "norm":
                    place += 1
                dve.reciprocal(rstd[0:rows, place, :], std[0:rows, :]).then_inc(norm_rstd, 1)
                for q in in_a_row(ph):
                    s = norm_spec(q)
                    dve.wait_ge(norm_spread, q.at.rstd + 1)
                    for c in range(q.chunks):
                        for a, b, cnd in s.pieces:
                            stt(s.dst[:, c, a:b], s.src[:, c, a:b], s.gain(c, cnd), PS[:, s.bank, a:b],
                                ALU.mult, ALU.mult).then_inc(norm_scaled, 1)
                if ph.ada:
                    ada_add(ph, 0)

            def swiglu(ph):
                head = U_SWIGLU % RING // 2

                def pair(i, j):
                    dst = hidden[:, j, 0:ph.tokens] if isinstance(i, int) else \
                        hidden[:, bass.ds(i * (RING // 2) + j, 1), 0:ph.tokens].rearrange("p o n -> p (o n)")
                    dve.wait_ge(silu_done, i * (RING // 2) + (ph.at.silu + j + 1))
                    dve.wait_ge(acc_ready, i * RING + (ph.at.acc + 2 * j + 2))
                    tt(dst, PS[:, 2 * (j % 2) + 1, 0:ph.tokens], sa[:, j % 2, 0:ph.tokens], ALU.mult)\
                        .then_inc(glu_done, 1)
                for j in range(head):
                    pair(0, j)
                with dve.Fori(0, U_SWIGLU // RING) as i:
                    for j in range(RING // 2):
                        if j == 3 and ph.ada:
                            ada_add(ph, 0, i)
                        pair(i, head + j)

            def down(ph):
                v, weight = {"ffn1": (2, 0.5), "mix": (5, 1.0), "ffn2": (8, 0.5), "mix2": (2, 1.0),
                             "mlp": (5, 1.0)}[ph.which]
                dve.wait_ge(ada_done, ADA_AT[ph.layer] + v + 2)
                if ph.at.h:
                    dve.wait_ge(h_ready, ph.at.h)
                link(dve.tensor_scalar(gate.rearrange("p (c j) -> p c j", j=2), mod_of(ph.layer, v), weight, None,
                                       ALU.mult))
                for m in range(DC):
                    dve.wait_ge(out_ready, ph.at.out + 4 * (ph.n - 1) + m // 2 + 1)
                    for a, b, cnd in HALVES[:ph.tokens // LAT]:
                        g = 2 * m + cnd
                        stt(h[:, m, a:b], PS[:, out_bank(m), a:b], gate[:, g:g + 1], h[:, m, a:b],
                            ALU.mult, ALU.add).then_inc(h_ready, 1)

            def gating(ph):
                l, n = ph.layer, ph.tiles
                dve.tensor_scalar(gqs[:, :], col("g_q_head", l), float(QK) ** -0.5, None, ALU.mult)\
                    .then_inc(query_gain, 1)
                dve.wait_ge(acc_evacuated, ph.at.evac)
                v = sgv[:, 0:n, :].rearrange("p t c -> p (t c)")
                t0 = sgt[:, 0:1, :].rearrange("p o n -> p (o n)")
                for q in range(n // 2):
                    part = v[:, q * 512:(q + 1) * 512]
                    link(tt(t0, part, part, ALU.mult))
                    red = dve.tensor_reduce(sgt[:, 1, 32 + 8 * q:40 + 8 * q], t0.rearrange("p (g c) -> p g c", c=64),
                                            AXX, ALU.add)
                    if q == n // 2 - 1:
                        red.then_inc(sg_var, 1)
                    else:
                        link(red)
                dve.wait_ge(sg_std, ph.at.sg + 1)
                link(dve.reciprocal(sgt[:, 1, 64:64 + 4 * n], sgt[:, 1, 0:4 * n]))
                if ph.at.sg:
                    dve.wait_ge(sg_mixed, ph.at.sg)
                for e in range(2):
                    src = sgv[:, 0:n, :].rearrange("p t (g e c) -> p t g e c", e=2, c=64)[:, :, :, e, :]
                    r = sgt[:, 1, 64:64 + 4 * n].rearrange("p (t g e) -> p t g e", e=2, g=2)[:, :, :, e:e + 1]\
                        .broadcast_to([P, n, 2, 64])
                    dst = vpad[:, 0:n, :, :].rearrange("p t (g e) c -> p t g e c", e=2)[:, :, :, e,
                                                                                       64 * e:64 * e + 64]
                    ins = tt(dst, src, r, ALU.mult)
                    if e == 0:
                        link(ins)
                ins.then_inc(sg_v, 1)
                hs = ph.tokens // LAT
                for cb in range(2):
                    part = lambda j: cv[:, 2 * j + cb, 0:ph.tokens].rearrange("p (s t) -> p s t", s=hs)
                    z = zc[:, cb, 0:hs, :]
                    y = merged[:, 6 + cb, 0:ph.tokens].rearrange("p (s t) -> p s t", s=hs)
                    link(tt(z[:, :, 1:LAT + 1], part(1), part(2), ALU.mult))
                    w = lambda k: col("w_conv", l, 3 * cb + k)
                    link(dve.tensor_scalar(y, z[:, :, 0:LAT], w(0), None, ALU.mult))
                    link(stt(y, z[:, :, 1:LAT + 1], w(1), y, ALU.mult, ALU.add))
                    link(stt(y, z[:, :, 2:LAT + 2], w(2), y, ALU.mult, ALU.add))
                    link(tt(y, y, part(0), ALU.mult))
                dve.wait_ge(sg_mixed, ph.at.sg + 1)
                for cb in range(2):
                    b = sgw[:, (4 + cb) * P:(5 + cb) * P].rearrange("p (o n) -> p o n", o=1).broadcast_to([P, n, P])
                    y = merged[:, 4 + cb, 0:ph.tokens]
                    link(stt(y.rearrange("p (t n) -> p t n", n=P),
                             PS[:, 5 + cb, 0:ph.tokens].rearrange("p (t n) -> p t n", n=P),
                             col("g_sgu", l, cb), b, ALU.mult, ALU.add))
                    ins = tt(y, y, sgu[:, cb, 0:ph.tokens], ALU.mult)
                    if cb == 0:
                        link(ins)
                ins.then_inc(sg_done, 1)

            def heads(ph):
                l, tiles, H0, T0 = ph.layer, ph.tiles, ph.at.head, ph.at.headtile
                def rope(j, sem_):
                    x = qkraw[:, j, 0:LAT]
                    term = qkt[:, 0, 0:LAT] if j == 0 else hqk[:, 1, 0:LAT]
                    tt(term, PS[:, 7 - j, 0:LAT], const("sin1"), ALU.mult).then_inc(sem_, 1)
                    link(tt(x, x, const("cos1"), ALU.mult))
                    link(tt(x, x, term, ALU.add))

                def roots(p):
                    dve.wait_ge(head_rot, p + (H0 + 1))
                    dve.wait_ge(head_ss, p * 2 + (2 * H0 + 1))
                    rope(0, head_rotated)
                    for j, n in enumerate((ph.tokens, TOK)):
                        dve.wait_ge(head_std, p * 2 + (2 * H0 + j + 1))
                        dve.reciprocal(hrstd[0:n // 4, j, :], hstd[0:n // 4, j, :]).then_inc(head_rstd, 1)

                def normed(p):
                    dve.wait_ge(head_spread, p + (H0 + 1))
                    if tiles > 2:
                        ins = tt(hqk[:, :, :], qkraw[:, :, :], PS[:, 0:2, :], ALU.mult)
                    else:
                        tt(hqk[:, 0, 0:LAT], qkraw[:, 0, 0:LAT], PS[:, 0, 0:LAT], ALU.mult)
                        ins = tt(hqk[:, 1, :], qkraw[:, 1, :], PS[:, 1, :], ALU.mult)
                    ins.then_inc(head_rope, 1)

                def maxes(i, t):
                    k = 0 if t < 2 else LAT
                    dve.wait_ge(score_ready, i * tiles + (T0 + t + 1))
                    dve.tensor_reduce(nmax[:, t:t + 1], PS[:, 2 + t % 2, k:TOK], AXX, ALU.max, negate=True)\
                        .then_inc(max_ready, 1)

                def outs(i, t):
                    dve.wait_ge(exp_done, i * tiles + (T0 + t + 1))
                    link(dve.reciprocal(rinv[:, t:t + 1], rsum[:, t:t + 1]))
                    dve.wait_ge(pv_ready, i * tiles + (T0 + t + 1))
                    dve.tensor_scalar(attn_tok[:, t, bass.ds(i * VD, VD)], PS[:, 7, 0:VD],
                                      rinv[:, t:t + 1], None, ALU.mult).then_inc(attn_done, 1)

                def iteration(i, last):
                    maxes(i, 0)
                    maxes(i, 1)
                    if not last:
                        roots(i + 1)
                    outs(i, 0)
                    if tiles > 2:
                        maxes(i, 2)
                        maxes(i, 3)
                        outs(i, 1)
                    if not last:
                        normed(i + 1)
                    if tiles > 2:
                        outs(i, 2)
                    outs(i, tiles - 1)
                    if not last:
                        ada_add(ph, 0, i)

                dve.wait_ge(sg_done, ph.at.sg)
                dve.wait_ge(kpe_rot, ph.layer + 1)
                rope(1, kpe_rotated)
                roots(0)
                normed(0)
                with dve.Fori(0, HEADS - 1) as i:
                    start = loop(i, 2 + tiles)
                    iteration(i, False)
                    loop_end(start, HEADS - 1)
                iteration(HEADS - 1, True)

            def gates(ph):
                G = ph.at.gates
                o, _ = COLS[("b_gate", ph.layer)]
                dve.wait_ge(gate_mm, 2 * G + 2)
                dve.wait_ge(gate_softplus, G + 1)
                link(dve.tensor_scalar(g_f, PS[0:64, 1, :], par[0:64, o + 1:o + 2], 0.0, ALU.add, ALU.min))
                link(tt(g_f, g_f, g_soft, ALU.subtract))

                def scan(out, src, initial, op0, op1):
                    for rows, back, edge in ((slice(0, 32), False, TOK - 1), (slice(32, 64), True, LAT)):
                        for part, first in ((slice(LAT, TOK), True), (slice(0, LAT), False)):
                            o_, s_ = out[rows, part], src[rows, part]
                            if back:
                                o_, s_ = o_[:, ::-1], s_[:, ::-1]
                            link(dve.tensor_tensor_scan(o_, s_, s_, initial if first else out[rows, edge:edge + 1],
                                                        op0, op1))
                scan(g_b, g_f, 0.0, ALU.add, ALU.bypass)
                link(stt(g_a, PS[0:64, 0, :], par[0:64, o:o + 1], g_b, ALU.add, ALU.subtract))
                scan(g_m, g_a, 0.0, ALU.max, ALU.max)
                tt(g_guard, g_b, g_m, ALU.add).then_inc(gate_rows, 1)
                dve.wait_ge(masks_in, 16)

            def pairs(ph):
                tiles, Q0, N0, per, T = ph.tiles, ph.at.pair, ph.at.pairtile, 2 * ph.tiles, ph.tokens
                og, _ = COLS[("norm_g", ph.layer)]
                mtok = tok[:, 0:tiles, :].rearrange("p t (e d) -> p (t e) d", e=2)
                tmp = qkt[:, 0, 0:T].rearrange("p (g d) -> p g d", d=HD)

                def selectors(p):
                    for d in range(2):
                        for e in range(2):
                            ins = dve.tensor_scalar(sel[:, 2 * d + e, :], ones[0:64, :],
                                                    ident[0:64, bass.ds(p * 2 + (32 * d + e), 1)], None, ALU.mult)
                    ins.then_inc(pm_sel, 1)

                def rope(p):
                    trig = lambda name: const(name).rearrange("p (o n) -> p o n", o=1).broadcast_to([P, 2, LAT])
                    rot = PS[:, 3, :].rearrange("p (e n) -> p e n", e=2)
                    dve.wait_ge(pm_rot, p + (Q0 + 1))
                    link(tt(qkt[:, :, 0:LAT], rot, trig("sin2"), ALU.mult))
                    link(tt(qkraw[:, :, 0:LAT], qkraw[:, :, 0:LAT], trig("cos2"), ALU.mult))
                    tt(qkraw[:, :, 0:LAT], qkraw[:, :, 0:LAT], qkt[:, :, 0:LAT], ALU.add).then_inc(pm_rope, 1)

                def log_weights(i, n):
                    e, t = n // tiles, n % tiles
                    k = 0 if t < 2 else LAT
                    w = (wt0, qkn)[n % 2]
                    dve.wait_ge(pm_arow, i * 2 + (2 * Q0 + e + 1))
                    for d in range(2):
                        ins = stt(w[:, d, k:TOK], PS[:, 4 + d, k:TOK],
                                  gcol[:, t, 0, d, bass.ds(i * 2 + e, 1)], maskt[:, d, t, k:TOK],
                                  ALU.add, ALU.add)
                    ins.then_inc(pm_logw, 1)

                def weighted(i, n):
                    e, t = n // tiles, n % tiles
                    k = 0 if t < 2 else LAT
                    w = (wt0, qkn)[n % 2]
                    dve.wait_ge(pm_w, i * per + (N0 + n + 1))
                    dve.wait_ge(pm_score, i * per + (N0 + n + 1))
                    for d in range(2):
                        ins = dve.tensor_tensor_reduce(w[:, d, k:TOK], PS[:, 6 + n % 2, k:TOK], w[:, d, k:TOK],
                                                       1.0, 0.0, ALU.mult, ALU.add, small[:, d:d + 1])
                    link(ins)
                    link(stt(small[:, 2:4], small[:, 0:2], -1.0, small[:, 0:2], ALU.mult, ALU.max))
                    link(tt(small[:, 2:4], small[:, 2:4],
                            gcol[:, t, 1, :, bass.ds(i * 2 + e, 1)].rearrange("p d o -> p (d o)"), ALU.max))
                    link(dve.reciprocal(small[:, 4:6], small[:, 2:4]))
                    link(dve.tensor_scalar(w[:, 1, k:TOK], w[:, 1, k:TOK], small[:, 5:6], None, ALU.mult))
                    if n >= 2:
                        dve.wait_ge(pm_turned, i * per + (N0 + n - 1))
                    stt(probs[:, n % 2, k:TOK], w[:, 0, k:TOK], small[:, 4:5], w[:, 1, k:TOK], ALU.mult, ALU.add)\
                        .then_inc(pm_p, 1)
                    dve.wait_ge(pm_p, i * per + (N0 + n + 1))

                def maxes(i, n):
                    e, t = n // tiles, n % tiles
                    k = 0 if t < 2 else LAT
                    dve.wait_ge(na_score, i * per + (N0 + n + 1))
                    if t < 2:
                        s = PS[:, 6 + n % 2, 0:LAT]
                        link(tt(s, s, nabias[:, e, t, :], ALU.add))
                    dve.tensor_reduce(small[:, 32 + n:33 + n], PS[:, 6 + n % 2, k:TOK], AXX, ALU.max, negate=True)\
                        .then_inc(na_max, 1)

                def outs(i, n):
                    e, t = n // tiles, n % tiles
                    dve.wait_ge(na_exp, i * per + (N0 + n + 1))
                    link(dve.reciprocal(small[:, 48 + n:49 + n], small[:, 40 + n:41 + n]))
                    dve.wait_ge(na_pv, i * per + (N0 + n + 1))
                    dve.tensor_scalar(tokn[:, t, e * HD:(e + 1) * HD], PS[:, 1, 0:HD],
                                      small[:, 48 + n:49 + n], None, ALU.mult).then_inc(na_o, 1)

                def out_chunk(i, first):
                    return merged2[:, first + i, 0:T] if isinstance(i, int) else \
                        merged2[:, bass.ds(i + first, 1), 0:T].rearrange("p o n -> p (o n)")

                wide = lambda a: a.rearrange("p (g o) -> p g o", o=1).broadcast_to([P, per, HD])

                def iteration(i, last):
                    for n in range(per):
                        if n >= 1 and n + 1 < per:
                            log_weights(i, n + 1)
                        weighted(i, n)
                    dve.wait_ge(bias_in, i * 16 + 16 * (Q0 + 1))
                    maxes(i, 0)
                    maxes(i, 1)
                    dve.wait_ge(pm_o, i * per + (N0 + per))
                    mu = small[:, 0:per]
                    link(dve.tensor_reduce(mu, mtok, AXX, ALU.add))
                    link(dve.tensor_scalar(mu, mu, 1.0 / HD, None, ALU.mult))
                    link(tt(mtok, mtok, wide(mu), ALU.subtract))
                    link(tt(tmp, mtok, mtok, ALU.mult))
                    dve.tensor_reduce(small[:, 8:8 + per], tmp, AXX, ALU.add).then_inc(pm_var, 1)
                    for n in range(per):
                        if n >= 1 and n + 1 < per:
                            maxes(i, n + 1)
                        if not last and n == ROTATE_AT // (3 * DC // per):
                            rope(i + 1)
                            log_weights(i + 1, 0)
                        outs(i, n)
                        if not last and n == ROTATE_AT // (3 * DC // per):
                            log_weights(i + 1, 1)
                        if n == 0:
                            dve.wait_ge(pm_std, i + (Q0 + 1))
                            link(dve.reciprocal(small[:, 24:24 + per], small[:, 16:16 + per]))
                            tt(mtok, mtok, wide(small[:, 24:24 + per]), ALU.mult).then_inc(pm_normed, 1)
                        if n == 1:
                            if not last:
                                selectors(i + 1)
                            dve.wait_ge(pm_fm, i + (Q0 + 1))
                            stt(out_chunk(i, 0), PS[:, 4, 0:T], par[:, bass.ds(i + og, 1)], osig[:, 0:T],
                                ALU.mult, ALU.mult).then_inc(pm_final, 1)
                    dve.wait_ge(na_fm, i + (Q0 + 1))
                    dve.tensor_scalar(out_chunk(i, HP), PS[:, 0, 0:T], 1.0, None, ALU.mult).then_inc(pair_done, 1)

                selectors(0)
                rope(0)
                dve.wait_ge(gate_cols, 2 * ph.at.gates)
                log_weights(0, 0)
                log_weights(0, 1)
                with dve.Fori(0, HP - 1) as i:
                    start = loop(i, 11 + 6 * per)
                    iteration(i, False)
                    loop_end(start, HP - 1)
                iteration(HP - 1, True)

            def mlp(ph):
                with dve.Fori(0, MC // RING) as i:
                    for j in range(RING):
                        dve.wait_ge(relu_read, i * RING + (ph.at.silu + j + 1))
                        r = sa[:, j % 2, 0:ph.tokens]
                        tt(hidden[:, bass.ds(i * RING + j, 1), 0:ph.tokens].rearrange("p o n -> p (o n)"), r, r,
                           ALU.mult).then_inc(glu_done, 1)

            run = dict(ada=ada, norm=norm, swiglu=swiglu, down=down, mix_in=lambda ph: None,
                       values=lambda ph: None, gating=gating, heads=heads, turn=lambda ph: None,
                       gates=gates, pairs=pairs, mlp=mlp)
            for ph in PLAN:
                if ph.kind == "norm" and ph.what in ("q_lat", "kv_lat"):
                    dve.wait_ge(acc_evacuated, ph.at.evac)
                if ph.kind == "norm" and ph.what == "attn":
                    dve.wait_ge(merge_ready, ph.at.merge)
                run[ph.kind](ph)


def unit_fm(w):
    m = w.shape[1] // P
    return w.reshape(DC, P, m, P).transpose(2, 1, 0, 3).reshape(m, P, UNIT)


def unit_tm(w):
    n = w.shape[1]
    return w.reshape(DC * n // UNIT, UNIT // n, P, n).transpose(0, 2, 1, 3).reshape(-1, P, UNIT)


def unit_rows(w):
    return w.reshape(-1, P, UNIT)


def unit_ada(w):
    return w.reshape(DC, P, -1, UNIT).transpose(2, 0, 1, 3)


def padded(w, left, width):
    out = np.zeros((w.shape[0], width), np.float32)
    out[:, left:left + w.shape[1]] = w
    return out


def interleaved(w):
    return w.reshape(D, 2, PAIRS, P).transpose(0, 2, 1, 3).reshape(D, 2 * D_FF)


def columns(v):
    return v.reshape(-1, P).T


def rope_tables():
    t = np.arange(LAT)
    row, colm = (t // GRID_W).astype(np.float32), (t % GRID_W).astype(np.float32)
    axis = ROPE // 2
    inv = (1.0 / (10000.0 ** (np.arange(0, axis, 2, dtype=np.float32) / axis))).astype(np.float32)
    ar, ac = row[:, None] * inv, colm[:, None] * inv
    ang = np.concatenate([ar, ar, ac, ac], axis=-1)
    cos1, sin1 = np.ones((P, LAT), np.float32), np.zeros((P, LAT), np.float32)
    cos1[NOPE:QK], sin1[NOPE:QK] = np.cos(ang).T, np.sin(ang).T
    rot1 = np.zeros((P, P), np.float32)
    for a in range(NOPE, QK, axis):
        for j in range(axis // 2):
            rot1[a + axis // 2 + j, a + j] = -1.0
            rot1[a + j, a + axis // 2 + j] = 1.0
    n = HD // 4
    inv2 = (10000.0 ** (-np.arange(n, dtype=np.float32) / n)).astype(np.float32)
    ang2 = np.concatenate([row[:, None] * inv2, colm[:, None] * inv2], axis=-1)
    cos2, sin2 = np.tile(np.cos(ang2).T, (4, 1)), np.tile(np.sin(ang2).T, (4, 1))
    rot2 = np.zeros((P, P), np.float32)
    for a in range(0, P, HD):
        for j in range(HD // 2):
            rot2[a + HD // 2 + j, a + j] = -1.0
            rot2[a + j, a + HD // 2 + j] = 1.0
    return rot1, cos1, sin1, rot2, cos2.astype(np.float32), sin2.astype(np.float32)


def ada_selector():
    m = np.zeros((P, 8), np.float32)
    for q in range(4):
        for j in range(4):
            m[32 * q + j, 4 * (q % 2) + j] = 1.0
    return m


def neighbour_bias(rpb):
    t = np.arange(LAT)
    row, colm = t // GRID_W, t % GRID_W
    start = np.clip(colm - 8, 0, GRID_W - 16)
    inside = (colm[None, :] >= start[:, None]) & (colm[None, :] < start[:, None] + 16)
    dr = row[None, :] - row[:, None] + 7
    dc = np.clip(colm[None, :] - colm[:, None] + 15, 0, 30)
    bias = np.where(inside, rpb[:, dr, dc], np.float32(NEG))
    return bias.reshape(HP, 2, 2, P, LAT).transpose(0, 3, 1, 2, 4).reshape(HP, P, 4 * LAT)


def scan_masks():
    m = np.full((P, 2, 4, TOK), np.float32(NEG))
    key = np.arange(LAT)[None, :]
    for t in range(4):
        query = (t % 2) * P + np.arange(P)[:, None]
        own = slice(0, LAT) if t < 2 else slice(LAT, TOK)
        if t < 2:
            m[:, :, t, LAT:TOK] = 0.0
        m[:, 0, t, own] = np.where(key <= query, np.float32(0), np.float32(NEG))
        m[:, 1, t, own] = np.where(key >= query, np.float32(0), np.float32(NEG))
    return m


def layout(x, c, ctx, c_ctx, w_ada, b_ada, g_ffn1, w_ffn1_in, w_ffn1_out, g_mix, w_mix_in, g_q_lat, w_q_up, g_kv_lat,
           w_kv_up, g_q_head, g_k_head, g_sgu, w_spatial, b_spatial, w_conv, g_out, w_mix_out, g_ffn2, w_ffn2_in,
           w_ffn2_out, c_2, ctx_2, c_ctx_2, w_ada_2, b_ada_2, norm1_g_2, w_in_2, b_gate_2, mlstm_norm_g_2, rpb_2,
           w_out_2, norm2_g_2, w_mlp1_2, w_mlp2_2, final_g_2):
    cut = np.cumsum([Q_LORA, KV_LORA, ROPE, 2 * SG])
    ada = np.concatenate([unit_ada(w_ada[0]), unit_ada(w_ada[1]), unit_ada(w_ada_2[0]), unit_ada(w_ada_2[1])])
    pair_m, pair_n, na_bias, gate_units = [], [], [], []
    q_, k_, v_, o_, nq, nk, nv, gm = range(8)
    for l in range(2):
        w = np.split(w_in_2[l], np.cumsum([512] * 7), axis=1)
        gate = np.zeros((D, P), np.float32)
        for e in range(2):
            for d in range(2):
                gate[:, 64 * e + 32 * d:64 * e + 32 * d + 8] = w[gm][:, 16 * e + 8 * d:16 * e + 8 * d + 8]
        gate_units.append(unit_fm(gate))
        fm = [unit_fm(a) for a in w[:7]]
        pair_m.append(np.concatenate([fm[j] for j in (q_, k_, o_)], axis=2))
        pair_n.append(np.concatenate([fm[j] for j in (nq, nk)], axis=2))
        gate_units += [unit_tm(np.ascontiguousarray(w[v_])), unit_tm(np.ascontiguousarray(w[nv]))]
        na_bias.append(neighbour_bias(rpb_2[l]))

    parts = []
    for ph in PLAN:
        l, b = ph.layer, ph.at.ada - 1
        if ph.kind == "ada":
            parts += list(ada[b:b + ph.blocks])
        if ph.kind == "norm":
            parts += list(ada[b:b + ph.ada])
        if ph.kind == "swiglu":
            w = unit_fm(interleaved((w_ffn1_in if ph.which == "ffn1" else w_ffn2_in)[l]))
            head = U_SWIGLU % RING
            parts.append(w[:head] if ph.ada else w)
            for i in range(ph.ada):
                w8 = w[head + RING * i:head + RING * (i + 1)]
                parts += [w8[0:2], ada[b + i, 0:2], w8[2:4], ada[b + i, 2:4], w8[4:6], ada[b + i, 4:8], w8[6:8]]
        if ph.kind == "down":
            parts.append(unit_rows({"ffn1": w_ffn1_out, "mix": w_mix_out, "ffn2": w_ffn2_out}[ph.which][l] if l < 2
                                   else {"mix2": w_out_2, "mlp": w_mlp2_2}[ph.which][l - 2]))
        if ph.kind == "mix_in":
            q, kv, kpe, sgm, cvm = np.split(w_mix_in[l], cut, axis=1)
            w = np.concatenate([unit_fm(q), unit_fm(kv), unit_fm(padded(kpe, NOPE, P)), unit_fm(cvm),
                                unit_fm(sgm[:, :SG])])
            parts.append(w)
            parts.append(unit_tm(np.ascontiguousarray(sgm[:, SG:])))
        if ph.kind == "values":
            v = w_kv_up[l].reshape(KV_LORA, HEADS, NOPE + VD)[:, :, NOPE:]
            parts.append(v.reshape(KC, P, HEADS * VD).transpose(1, 0, 2).reshape(1, P, UNIT))
        if ph.kind == "heads":
            parts += list(ada[b:b + ph.ada])
        if ph.kind == "gates":
            parts += gate_units[3 * (l - 2):3 * (l - 2) + 3]
        if ph.kind == "mlp":
            parts.append(unit_fm(w_mlp1_2[l - 2]))
    stream = np.concatenate(parts)

    head_w = np.zeros((2, HEADS, P, HW), np.float32)
    for l in range(2):
        for hd in range(HEADS):
            q = padded(w_q_up[l][:, hd * QK:(hd + 1) * QK], 0, P).reshape(QC, P, P).transpose(1, 0, 2)
            kv = w_kv_up[l][:, hd * P:(hd + 1) * P]
            k = padded(kv[:, :NOPE], 0, P).reshape(KC, P, P).transpose(1, 0, 2)
            head_w[l, hd] = np.concatenate([q.reshape(P, -1), k.reshape(P, -1)], axis=1)

    sg_w = np.stack([np.concatenate([
        w_spatial[l].transpose(2, 0, 1).reshape(P, 4 * P),
        np.repeat(b_spatial[l], 64, axis=0).reshape(2, P, P).transpose(1, 0, 2).reshape(P, 2 * P)], axis=1)
        for l in range(2)])

    rot1, cos1, sin1, rot2, cos2, sin2 = rope_tables()
    consts = np.concatenate([np.eye(P, dtype=np.float32), np.ones((P, P), np.float32), rot1, cos1, sin1,
                             rot2, cos2, sin2, ada_selector()], axis=1)
    cols = []
    for l in range(2):
        cols += [columns(g_ffn1[l]), columns(g_mix[l]), columns(g_ffn2[l]), columns(g_q_lat[l]),
                 columns(g_kv_lat[l]), padded(g_q_head[l][None], 0, P).T, padded(g_k_head[l][None], 0, P).T,
                 columns(g_sgu[l]), columns(g_out[l]),
                 w_conv[l].reshape(3, 2, P).transpose(2, 1, 0).reshape(P, 6)]
    for l in range(2):
        bg = np.zeros((P, 2), np.float32)
        for e in range(2):
            for d in range(2):
                bg[32 * d:32 * d + 8, e] = b_gate_2[l, 16 * e + 8 * d:16 * e + 8 * d + 8]
        cols += [columns(norm1_g_2[l]), columns(norm2_g_2[l]), columns(mlstm_norm_g_2[l]), bg]
    cols += [columns(final_g_2), columns(b_ada), columns(b_ada_2),
             np.stack([columns(v) for v in (c[0], c_ctx, c_2[0], c_ctx_2)], axis=2).reshape(P, 4 * DC)]
    params = np.concatenate(cols, axis=1)
    return dict(pair_m=np.concatenate(pair_m), pair_n=np.concatenate(pair_n), na_bias=np.concatenate(na_bias),
                masks=scan_masks(), stream=stream, head_w=head_w.reshape(2 * HEADS, P, HW), sg_w=sg_w, consts=consts,
                params=params,
                xT=np.ascontiguousarray(x[0].T), ctxT=np.ascontiguousarray(ctx[0].T),
                ctx2T=np.ascontiguousarray(ctx_2[0].T))


def kernel(**inputs):
    import concourse.bacc as bacc
    from concourse.bass_utils import run_bass_kernel_spmd

    arrays = layout(**{k: np.asarray(v) for k, v in inputs.items()})
    nc = bacc.Bacc("TRN2", target_bir_lowering=False, num_devices=1)
    args = {k: nc.dram_tensor(k, a.shape, F32, kind="ExternalInput").ap() for k, a in arrays.items()}
    out = nc.dram_tensor("outT", (D, LAT), F32, kind="ExternalOutput").ap()
    build(nc, outT=out, **args)
    r = run_bass_kernel_spmd(nc, [arrays], core_ids=[0])
    return np.ascontiguousarray(r.results[0]["outT"].T)[None]
```
